# Optimizing a Trainium2 kernel written in Bass

```python
import math
import jax, jax.numpy as jnp
from jax import lax
import numpy as np

D_MODEL = 1024
BATCH = 1
SEQ = 512
DEPTH = 2
DEC_BATCH = 8
DEC_SEQ = 4
PAST_LEN = 4096
PAGE_SIZE = 128

N_MIXERS = 2
N_MLA_LAYERS = (DEPTH + 1) // 2
N_SWA_LAYERS = DEPTH // 2
RMS_EPS = 1e-6
ROPE_THETA = 10000.0
Q_BLOCK = 128
MLA_HEADS = 8
Q_LORA = 384
KV_LORA = 256
QK_NOPE = 128
QK_ROPE = 64
V_HEAD = 128
MLA_ROW = KV_LORA + QK_ROPE
MLA_SCALE = 1.0 / math.sqrt(QK_NOPE + QK_ROPE)
SWA_HEADS = 16
SWA_KV_HEADS = 4
SWA_GROUP = SWA_HEADS // SWA_KV_HEADS
SWA_HEAD_DIM = 64
WINDOW = 128
SWA_SCALE = 1.0 / math.sqrt(SWA_HEAD_DIM)
N_GROUPS = 4
EXPERTS_PER_GROUP = 8
N_EXPERTS = N_GROUPS * EXPERTS_PER_GROUP
TOP_K_IN_GROUP = 2
D_FF_EXPERT = 512
MOE_BLOCK = 128

kernel_name = 'hybrid_mla_swa_hmoe_step'

def rms_norm(x, g):
    xf = x.astype(jnp.float32)
    y = xf * lax.rsqrt(jnp.mean(xf * xf, axis=-1, keepdims=True) + RMS_EPS)
    return (y * g.astype(jnp.float32)).astype(x.dtype)

def rope(x, pos):
    half = x.shape[-1] // 2
    inv_freq = ROPE_THETA ** (-jnp.arange(half, dtype=jnp.float32) / half)
    ang = pos.astype(jnp.float32)[:, None] * inv_freq[None, :]
    cos = jnp.cos(ang)[:, None, :]
    sin = jnp.sin(ang)[:, None, :]
    xf = x.astype(jnp.float32)
    x1, x2 = xf[..., :half], xf[..., half:]
    return jnp.concatenate([x1 * cos - x2 * sin, x2 * cos + x1 * sin], axis=-1).astype(x.dtype)

def mla_project(h, pos, w_a, q_norm, wq_b, kv_norm):
    b, s, _ = h.shape
    a = h @ w_a
    cq = rms_norm(a[..., :Q_LORA], q_norm)
    c = rms_norm(a[..., Q_LORA:Q_LORA + KV_LORA], kv_norm)
    k_rope = rope(a[..., None, Q_LORA + KV_LORA:], pos)[:, :, 0]
    q = (cq @ wq_b).reshape(b, s, MLA_HEADS, QK_NOPE + QK_ROPE)
    return q[..., :QK_NOPE], rope(q[..., QK_NOPE:], pos), c, k_rope

def split_wkv_b(wkv_b):
    w = wkv_b.reshape(KV_LORA, MLA_HEADS, QK_NOPE + V_HEAD)
    return w[..., :QK_NOPE], w[..., QK_NOPE:]

def mla_prompt(h, w_a, q_norm, wq_b, kv_norm, wkv_b, wo):
    b, s, _ = h.shape
    pos = jnp.arange(s, dtype=jnp.int32)
    q_nope, q_rope, c, k_rope = mla_project(h, pos, w_a, q_norm, wq_b, kv_norm)
    w_uk, w_uv = split_wkv_b(wkv_b)
    k_nope = jnp.einsum('bsc,chd->bshd', c, w_uk)
    v = jnp.einsum('bsc,chd->bshd', c, w_uv)
    nb = s // Q_BLOCK
    qn_blocks = q_nope.reshape(b, nb, Q_BLOCK, MLA_HEADS, QK_NOPE).swapaxes(0, 1)
    qr_blocks = q_rope.reshape(b, nb, Q_BLOCK, MLA_HEADS, QK_ROPE).swapaxes(0, 1)
    key_pos = jnp.arange(s)

    def attend_block(args):
        qn, qr, blk = args
        sc = (jnp.einsum('bqhd,bkhd->bhqk', qn, k_nope).astype(jnp.float32)
              + jnp.einsum('bqhr,bkr->bhqk', qr, k_rope).astype(jnp.float32)) * MLA_SCALE
        q_pos = blk * Q_BLOCK + jnp.arange(Q_BLOCK)
        sc = jnp.where(key_pos[None, :] <= q_pos[:, None], sc, -jnp.inf)
        p = jax.nn.softmax(sc, axis=-1).astype(v.dtype)
        return jnp.einsum('bhqk,bkhd->bqhd', p, v)

    o = lax.map(attend_block, (qn_blocks, qr_blocks, jnp.arange(nb)))
    o = o.swapaxes(0, 1).reshape(b, s, MLA_HEADS * V_HEAD)
    rows = jnp.concatenate([c, k_rope], axis=-1)
    return o @ wo, rows

def mla_sample(h, cache_pool, page_table, w_a, q_norm, wq_b, kv_norm, wkv_b, wo):
    b, t, _ = h.shape
    past_len = page_table.shape[1] * PAGE_SIZE
    pos = past_len + jnp.arange(t, dtype=jnp.int32)
    q_nope, q_rope, c, k_rope = mla_project(h, pos, w_a, q_norm, wq_b, kv_norm)
    w_uk, w_uv = split_wkv_b(wkv_b)
    past = cache_pool[page_table].reshape(b, past_len, MLA_ROW)
    c_past, kr_past = past[..., :KV_LORA], past[..., KV_LORA:]
    q_lat = jnp.einsum('bthd,chd->bthc', q_nope, w_uk)
    s_past = (jnp.einsum('bthc,bkc->bhtk', q_lat, c_past).astype(jnp.float32)
              + jnp.einsum('bthr,bkr->bhtk', q_rope, kr_past).astype(jnp.float32)) * MLA_SCALE
    s_new = (jnp.einsum('bthc,bkc->bhtk', q_lat, c).astype(jnp.float32)
             + jnp.einsum('bthr,bkr->bhtk', q_rope, k_rope).astype(jnp.float32)) * MLA_SCALE
    causal = jnp.tril(jnp.ones((t, t), dtype=bool))
    s_new = jnp.where(causal, s_new, -jnp.inf)
    p = jax.nn.softmax(jnp.concatenate([s_past, s_new], axis=-1), axis=-1).astype(c.dtype)
    o_lat = (jnp.einsum('bhtk,bkc->bthc', p[..., :past_len], c_past)
             + jnp.einsum('bhtk,bkc->bthc', p[..., past_len:], c))
    o = jnp.einsum('bthc,chd->bthd', o_lat, w_uv).reshape(b, t, MLA_HEADS * V_HEAD)
    rows = jnp.concatenate([c, k_rope], axis=-1)
    return o @ wo, rows

def swa_project(h, pos, wqkv, bqkv):
    b, s, _ = h.shape
    nq = SWA_HEADS * SWA_HEAD_DIM
    nk = SWA_KV_HEADS * SWA_HEAD_DIM
    qkv = h @ wqkv + bqkv
    q = qkv[..., :nq].reshape(b, s, SWA_HEADS, SWA_HEAD_DIM)
    k = qkv[..., nq:nq + nk].reshape(b, s, SWA_KV_HEADS, SWA_HEAD_DIM)
    v = qkv[..., nq + nk:].reshape(b, s, SWA_KV_HEADS, SWA_HEAD_DIM)
    return rope(q, pos), rope(k, pos), v

def sink_softmax(sc, sink):
    m = jnp.maximum(jnp.max(sc, axis=-1, keepdims=True), sink)
    e = jnp.exp(sc - m)
    return e / (jnp.sum(e, axis=-1, keepdims=True) + jnp.exp(sink - m))

def swa_prompt(h, wqkv, bqkv, sinks, wo, bo):
    b, s, _ = h.shape
    pos = jnp.arange(s, dtype=jnp.int32)
    q, k, v = swa_project(h, pos, wqkv, bqkv)
    nb = s // WINDOW
    qb = q.reshape(b, nb, WINDOW, SWA_KV_HEADS, SWA_GROUP, SWA_HEAD_DIM)

    def band(z):
        cur = z.reshape(b, nb, WINDOW, SWA_KV_HEADS, SWA_HEAD_DIM)
        prev = jnp.concatenate([jnp.zeros_like(cur[:, :1]), cur[:, :-1]], axis=1)
        return jnp.concatenate([prev, cur], axis=2)

    kb, vb = band(k), band(v)
    sc = jnp.einsum('bnqhgd,bnshd->bnhgqs', qb, kb).astype(jnp.float32) * SWA_SCALE
    blk = jnp.arange(nb)[:, None, None] * WINDOW
    q_pos = blk + jnp.arange(WINDOW)[None, :, None]
    k_pos = blk - WINDOW + jnp.arange(2 * WINDOW)[None, None, :]
    dist = q_pos - k_pos
    valid = (dist >= 0) & (dist < WINDOW) & (k_pos >= 0)
    sc = jnp.where(valid[None, :, None, None], sc, -jnp.inf)
    sink = sinks.astype(jnp.float32).reshape(SWA_KV_HEADS, SWA_GROUP)[None, None, :, :, None, None]
    p = sink_softmax(sc, sink).astype(v.dtype)
    o = jnp.einsum('bnhgqs,bnshd->bnqhgd', p, vb).reshape(b, s, SWA_HEADS * SWA_HEAD_DIM)
    state = jnp.stack([k[:, -WINDOW:], v[:, -WINDOW:]], axis=2)
    return o @ wo + bo, state

def swa_sample(h, buf, wqkv, bqkv, sinks, wo, bo):
    b, t, _ = h.shape
    pos = PAST_LEN + jnp.arange(t, dtype=jnp.int32)
    q, k, v = swa_project(h, pos, wqkv, bqkv)
    kc = jnp.concatenate([buf[:, :, 0], k], axis=1)
    vc = jnp.concatenate([buf[:, :, 1], v], axis=1)
    qg = q.reshape(b, t, SWA_KV_HEADS, SWA_GROUP, SWA_HEAD_DIM)
    sc = jnp.einsum('bthgd,bshd->bhgts', qg, kc).astype(jnp.float32) * SWA_SCALE
    k_rel = jnp.arange(WINDOW + t) - WINDOW
    dist = jnp.arange(t)[:, None] - k_rel[None, :]
    valid = (dist >= 0) & (dist < WINDOW)
    sc = jnp.where(valid, sc, -jnp.inf)
    sink = sinks.astype(jnp.float32).reshape(SWA_KV_HEADS, SWA_GROUP)[None, :, :, None, None]
    p = sink_softmax(sc, sink).astype(vc.dtype)
    o = jnp.einsum('bhgts,bshd->bthgd', p, vc).reshape(b, t, SWA_HEADS * SWA_HEAD_DIM)
    state = jnp.stack([kc[:, -WINDOW:], vc[:, -WINDOW:]], axis=2)
    return o @ wo + bo, state

def hier_moe(x, w_group, b_group, w_expert, b_expert, w_gate, w_up, w_down):
    shape = x.shape
    xt = x.reshape(-1, shape[-1])
    n_tok = xt.shape[0]
    g_logits = (xt @ w_group).astype(jnp.float32) + b_group.astype(jnp.float32)
    g_prob = jax.nn.softmax(g_logits, axis=-1)
    g_p, g_idx = lax.top_k(g_prob, 1)
    e_logits = ((xt @ w_expert).astype(jnp.float32) + b_expert.astype(jnp.float32)).reshape(
        n_tok, N_GROUPS, EXPERTS_PER_GROUP)
    e_sel = e_logits[jnp.arange(n_tok), g_idx[:, 0]]
    e_top, e_idx = lax.top_k(e_sel, TOP_K_IN_GROUP)
    gate = g_p * jax.nn.softmax(e_top, axis=-1)
    expert_id = g_idx * EXPERTS_PER_GROUP + e_idx

    n_slots = n_tok * TOP_K_IN_GROUP
    eid = expert_id.reshape(n_slots).astype(jnp.int32)
    tok = jnp.repeat(jnp.arange(n_tok, dtype=jnp.int32), TOP_K_IN_GROUP)
    wt = gate.reshape(n_slots)
    order = jnp.argsort(eid)
    sorted_e = eid[order]
    counts = jnp.bincount(eid, length=N_EXPERTS)
    padded = (counts + MOE_BLOCK - 1) // MOE_BLOCK * MOE_BLOCK
    seg_start = jnp.cumsum(counts) - counts
    pad_end = jnp.cumsum(padded)
    pad_start = pad_end - padded
    dest = pad_start[sorted_e] + jnp.arange(n_slots) - seg_start[sorted_e]
    n_rows = -(-n_slots // MOE_BLOCK) * MOE_BLOCK + N_EXPERTS * MOE_BLOCK
    row_tok = jnp.zeros((n_rows,), jnp.int32).at[dest].set(tok[order])
    row_w = jnp.zeros((n_rows,), jnp.float32).at[dest].set(wt[order])
    n_blk = n_rows // MOE_BLOCK
    blk_e = jnp.minimum(jnp.searchsorted(pad_end, jnp.arange(n_blk) * MOE_BLOCK, side='right'),
                        N_EXPERTS - 1)
    xr = xt[row_tok].reshape(n_blk, MOE_BLOCK, shape[-1])

    def run_block(args):
        xb, e = args
        hid = jax.nn.silu(xb @ w_gate[e]) * (xb @ w_up[e])
        return hid @ w_down[e]

    yr = lax.map(run_block, (xr, blk_e)).reshape(n_rows, shape[-1])
    yr = yr.astype(jnp.float32) * row_w[:, None]
    y = jnp.zeros((n_tok, shape[-1]), jnp.float32).at[row_tok].add(yr)
    return y.astype(x.dtype).reshape(shape)

def setup_inputs(seed: int = 0) -> dict:
    key = jax.random.key(seed)
    ks = iter(jax.random.split(key, 32))
    f32 = jnp.float32

    def dense(shape, fan_in):
        return jax.random.normal(next(ks), shape, f32) * fan_in ** -0.5

    def gain(shape):
        return 1.0 + 0.02 * jax.random.normal(next(ks), shape, f32)

    def small(shape, scale):
        return scale * jax.random.normal(next(ks), shape, f32)

    n_pages = PAST_LEN // PAGE_SIZE
    n_used = DEC_BATCH * n_pages
    n_phys = (5 * n_used + 3) // 4
    x_prompt = jax.random.normal(next(ks), (BATCH, SEQ, D_MODEL), f32)
    x_sample = jax.random.normal(next(ks), (DEC_BATCH, DEC_SEQ, D_MODEL), f32)
    cache_mla = jax.random.normal(next(ks), (N_MLA_LAYERS, n_phys, PAGE_SIZE, MLA_ROW), f32)
    cache_swa_kv = jax.random.normal(
        next(ks), (N_SWA_LAYERS, DEC_BATCH, WINDOW, 2, SWA_KV_HEADS, SWA_HEAD_DIM), f32)
    page_table = jax.random.permutation(next(ks), n_phys)[:n_used].reshape(
        DEC_BATCH, n_pages).astype(jnp.int32)
    qkv_w = (SWA_HEADS + 2 * SWA_KV_HEADS) * SWA_HEAD_DIM
    return {
        'x_prompt': x_prompt,
        'x_sample': x_sample,
        'cache_mla': cache_mla,
        'cache_swa_kv': cache_swa_kv,
        'page_table': page_table,
        'norm_mix': gain((DEPTH, D_MODEL)),
        'norm_ffn': gain((DEPTH, D_MODEL)),
        'norm_final': gain((D_MODEL,)),
        'mla_w_a': dense((N_MLA_LAYERS, D_MODEL, Q_LORA + KV_LORA + QK_ROPE), D_MODEL),
        'mla_q_norm': gain((N_MLA_LAYERS, Q_LORA)),
        'mla_wq_b': dense((N_MLA_LAYERS, Q_LORA, MLA_HEADS * (QK_NOPE + QK_ROPE)), Q_LORA),
        'mla_kv_norm': gain((N_MLA_LAYERS, KV_LORA)),
        'mla_wkv_b': dense((N_MLA_LAYERS, KV_LORA, MLA_HEADS * (QK_NOPE + V_HEAD)), KV_LORA),
        'mla_wo': dense((N_MLA_LAYERS, MLA_HEADS * V_HEAD, D_MODEL), MLA_HEADS * V_HEAD),
        'swa_wqkv': dense((N_SWA_LAYERS, D_MODEL, qkv_w), D_MODEL),
        'swa_bqkv': small((N_SWA_LAYERS, qkv_w), 0.02),
        'swa_sinks': small((N_SWA_LAYERS, SWA_HEADS), 0.5),
        'swa_wo': dense((N_SWA_LAYERS, SWA_HEADS * SWA_HEAD_DIM, D_MODEL), SWA_HEADS * SWA_HEAD_DIM),
        'swa_bo': small((N_SWA_LAYERS, D_MODEL), 0.02),
        'moe_w_group': dense((DEPTH, D_MODEL, N_GROUPS), D_MODEL),
        'moe_b_group': small((DEPTH, N_GROUPS), 0.01),
        'moe_w_expert': dense((DEPTH, D_MODEL, N_EXPERTS), D_MODEL),
        'moe_b_expert': small((DEPTH, N_EXPERTS), 0.01),
        'moe_w_gate': dense((DEPTH, N_EXPERTS, D_MODEL, D_FF_EXPERT), D_MODEL),
        'moe_w_up': dense((DEPTH, N_EXPERTS, D_MODEL, D_FF_EXPERT), D_MODEL),
        'moe_w_down': dense((DEPTH, N_EXPERTS, D_FF_EXPERT, D_MODEL), D_FF_EXPERT),
    }

def reference(x_prompt, x_sample, cache_mla, cache_swa_kv, page_table, norm_mix, norm_ffn,
              norm_final, mla_w_a, mla_q_norm, mla_wq_b, mla_kv_norm, mla_wkv_b, mla_wo,
              swa_wqkv, swa_bqkv, swa_sinks, swa_wo, swa_bo, moe_w_group, moe_b_group,
              moe_w_expert, moe_b_expert, moe_w_gate, moe_w_up, moe_w_down):
    xp, xs = x_prompt, x_sample
    mla_p, mla_s, swa_p, swa_s = [], [], [], []
    for layer in range(DEPTH):
        j = layer // N_MIXERS
        hp = rms_norm(xp, norm_mix[layer])
        hs = rms_norm(xs, norm_mix[layer])
        if layer % N_MIXERS == 0:
            w = (mla_w_a[j], mla_q_norm[j], mla_wq_b[j], mla_kv_norm[j], mla_wkv_b[j], mla_wo[j])
            dp, rp = mla_prompt(hp, *w)
            ds, rs = mla_sample(hs, cache_mla[j], page_table, *w)
            mla_p.append(rp)
            mla_s.append(rs)
        else:
            w = (swa_wqkv[j], swa_bqkv[j], swa_sinks[j], swa_wo[j], swa_bo[j])
            dp, rp = swa_prompt(hp, *w)
            ds, rs = swa_sample(hs, cache_swa_kv[j], *w)
            swa_p.append(rp)
            swa_s.append(rs)
        xp = xp + dp
        xs = xs + ds
        moe_w = (moe_w_group[layer], moe_b_group[layer], moe_w_expert[layer], moe_b_expert[layer],
                 moe_w_gate[layer], moe_w_up[layer], moe_w_down[layer])
        xp = xp + hier_moe(rms_norm(xp, norm_ffn[layer]), *moe_w)
        xs = xs + hier_moe(rms_norm(xs, norm_ffn[layer]), *moe_w)
    y_prompt = rms_norm(xp, norm_final)
    y_sample = rms_norm(xs, norm_final)
    mla_rows_prompt = jnp.stack(mla_p)
    mla_rows_sample = jnp.stack(mla_s)
    swa_kv_prompt = jnp.stack(swa_p)
    swa_kv_sample = jnp.stack(swa_s)
    return (y_prompt, y_sample, mla_rows_prompt, mla_rows_sample, swa_kv_prompt, swa_kv_sample)


_drawn_inputs = setup_inputs


def setup_inputs(seed=0):
    import zlib

    import numpy as np

    out = dict(_drawn_inputs(seed))
    spreads = {}
    factors = {'norm_final': 2.865, 'swa_sinks': 4.831, 'moe_b_group': 2.773}
    for name, (base, spread) in spreads.items():
        noise = np.random.default_rng([zlib.crc32(name.encode()), seed]).standard_normal(out[name].shape)
        drawn = base * np.exp(spread * noise) if base else spread * noise
        out[name] = __import__('jax').numpy.asarray(drawn.astype(out[name].dtype))
    for name, factor in factors.items():
        out[name] = (out[name] * factor).astype(out[name].dtype)
    return out
```

```python
from contextlib import ExitStack

import concourse.bass as bass
from concourse import mybir

F32 = mybir.dt.float32
I32 = mybir.dt.int32
U32 = mybir.dt.uint32
ALU = mybir.AluOpType
ACT = mybir.ActivationFunctionType
X = mybir.AxisListType.X

P = 128
D = 1024
KD = D // P
SEQ, NB, NT = 512, 8, 4
NS = NB * NT
PT = SEQ // P
TILES = PT + 1
TOK = SEQ + NS
QL, CL, DR = 384, 256, 64
ROW = CL + DR
H, DN = 8, 128
PAIRS = H // 2
PAGES = 32
PHYS = 320
MLA_SCALE = 1.0 / (DN + DR) ** 0.5
UNITS = H * PT
SH, SKV, SD = 16, 4, 64
SG = SH // SKV
SUNITS = SH // 2
WIN = 128
SWA_SCALE = 1.0 / SD ** 0.5
QKV = (SH + 2 * SKV) * SD
NE, NG, EG = 32, 4, 8
FF = 512
KF = FF // P
BLK = 64
MORE = (TOK + BLK - 1) // BLK - 1
LIST = 2 * TOK // BLK + 1
FAR = 4096.0
EPS = 1e-6
NEG = -1e30
AHEAD = 2
LOOK = 3
FETCHES = NE + LOOK
INTO = ((FETCHES + 1) // 2, FETCHES // 2)
STORES = NE // 2 + 1
DMA = 16

EVENTS = {
    "pool": "moe_done saved",
    "vector": """x_pad x_ready meansq h_ready hTb a_ms rows_ready cT_ready q_dve kv_dve qr_ready
        nm_ready pT_m_ready o_m_ready wuk_dve qlat_ready qb_ready kt1 mx_ready mrow_ready nms_ready
        lbc_ready pTb_s olat_ready oTs_ready wo_added lg_ready gsub_ready esub_ready sel_ready nb_ready
        list_ready lst_ready onehot_ready idx_ready hid_ready hidT_ready y1_ready y_added 
                 
          """,
    "scalar": """sumsq_ready root_ready hTa a_sq a_root cqT_ready q_act kv_act p_ready oT_act
        wuk_act kt0 kt2 p_s_ready pTa_s o_s_ready gexp_ready eexp_ready silu_ready y0_ready xeT_ready
              """,
    "tensor": """hT_mm a_mm rowsT_mm q_mm swap_mm kv_mm s_mm pT_mm o_mm oT_mm wuk_mm qlat_mm kt_mm0
        kt_mm1 kt_mm2 qk_mm new_mm mxT_mm mb_mm pT_s_mm pv_mm oc_mm oTs_mm wo_mm lg_mm rank_mm pre_mm
        listrow_mm idx_mm gu_mm ht_mm d_mm xt_mm       
        sample_s_mm sample_pT_mm sample_o_mm""",
}
LATER = {
    "v_ready": ("q_dve", PAIRS),
    "qkr_ready": ("kv_dve", PAIRS),
    "qTb_w": ("qr_ready", PAIRS),
    "s_w_ready": ("nm_ready", UNITS),
    "pT_w_ready": ("pT_m_ready", UNITS),
    "o_w_ready": ("o_m_ready", UNITS),
    "oTb_w": ("cT_ready", TILES),
    "sink_clear": ("wuk_dve", 2),
    "kb_dve": ("qb_ready", NB),
    "sample_s": ("mx_ready", NB),
    "sample_p": ("mrow_ready", NB),
    "sample_pT_dve": ("nms_ready", NB),
    "sample_o": ("lbc_ready", NB),
    "y_ready": ("pTb_s", NB),
    "v_w": ("q_act", PAIRS),
    "qTa_w": ("kv_act", PAIRS),
    "p_w": ("p_ready", UNITS),
    "oTa_w": ("oT_act", UNITS),
    "kb_act": ("wuk_act", 2),
    "sample_e": ("p_s_ready", NB),
    "sample_pT_act": ("pTa_s", NB),
    "qkv_mm": ("q_mm", PAIRS),
    "qT_mm": ("swap_mm", PAIRS),
    "s_w_mm": ("s_mm", UNITS),
    "pT_w_mm": ("pT_mm", UNITS),
    "o_w_mm": ("o_mm", UNITS),
    "oT_w_mm": ("oT_mm", UNITS),
    "kb_mm": ("wuk_mm", 4),
}
TRANSFERS = {
    "pool": """gain_in consts_in xn_out gathered0 gathered1 scattered0 scattered1
        mlaconst_in swaconst_in""",
    "sync": """x_in w_a_in wqp_in wkp_in pages0 pages1 wkvb_in wo_in rows_out g0_in g1_in u0_in u1_in
        d0_in d1_in wqkv_in wo_w_in y_out0 y_out1 state_out windows_out cacheb_in ptab_in rw_in ybuf0 ybuf1""",
}
POOLS = TRANSFERS["pool"].split()
MORE_EVENTS = """more_marks more_idx_mm more_idx_cv more_xt_mm more_xeT more_gu_mm more_silu more_hid more_ht_mm
    more_hidT more_d_mm more_y0 more_y1 more_done"""
MORE_TRANSFERS = "more_weights more_gather0 more_gather1 more_scatter0 more_scatter1"



def cols(start, size):
    return slice(start, start + size) if isinstance(start, int) else bass.ds(start, size)


def rows_of(T):
    return NS if isinstance(T, int) and T == PT else P


class Arena:

    def __init__(self, mem, start, end):
        self.mem, self.at, self.end = mem, start, end

    def take(self, *shape, dt=F32):
        n = 1
        for size in shape:
            n *= size
        v = self.mem[:, self.at:self.at + n]
        self.at += n
        assert self.at <= self.end, (self.at, self.end)
        if dt is not F32:
            v = v.bitcast(dt)
        if len(shape) == 2:
            v = v.rearrange("p (a b) -> p a b", a=shape[0])
        elif len(shape) == 3:
            v = v.rearrange("p (a b c) -> p a b c", a=shape[0], b=shape[1])
        elif len(shape) == 4:
            v = v.rearrange("p (a b c d) -> p a b c d", a=shape[0], b=shape[1], c=shape[2])
        return v


def build(nc, a, o):
    with ExitStack() as ctx:
        WORDS = 53120
        mem = ctx.enter_context(nc.sbuf_tensor("mem", [P, WORDS], F32))
        ps = ctx.enter_context(nc.psum_tensor("ps", [P, 8, 512], F32))
        sig = {}
        for names in (*EVENTS.values(), *TRANSFERS.values()):
            for name in names.split():
                sig[name] = ctx.enter_context(nc.semaphore(name))
        for name in (MORE_EVENTS + " " + MORE_TRANSFERS).split():
            sig[name] = ctx.enter_context(nc.semaphore(name))
        sig["passed"] = ctx.enter_context(nc.semaphore("passed"))
        for name, (base, _) in LATER.items():
            sig[name] = sig[base]

        def happened(name, k):
            return k + AHEAD + (LATER[name][1] if name in LATER else 0)

        def landed(name, k):
            return (k if name in POOLS else k + AHEAD) * DMA

        def turnstile(eng):
            eng.sem_inc(sig["passed"], 1)

        def start_more(eng, L, names):
            if L:
                for name in names.split():
                    eng.sem_clear(sig["more_" + name])

        def start_counts(eng, which):
            for name in EVENTS.get(which, "").split():
                eng.sem_inc(sig[name], AHEAD)
            for name in TRANSFERS["sync"].split() if which == "sync" else ():
                eng.sem_inc(sig[name], AHEAD * DMA)

        keep = Arena(mem, 0, WORDS)
        x = keep.take(TILES * D)
        ident = keep.take(P)
        before = keep.take(P)
        ones = keep.take(P)
        slots = keep.take(BLK)
        idx = keep.take(NE)
        idxm = keep.take(NE)
        blkat = keep.take(MORE)
        epart = keep.take(1)
        tokcode = keep.take(2, TILES)
        valid = keep.take(TILES)
        consts = mem[:, TILES * D:keep.at]
        cos_tok = keep.take(TILES * DR // 2)
        sin_tok = keep.take(TILES * DR // 2)
        gain = keep.take(D)
        sumsq = keep.take(8)
        rstd = keep.take(8)
        gate1 = keep.take(TILES)
        gate2 = keep.take(TILES)
        rest = keep.at
        slot_at = [rest, rest + 3 * KD * FF]
        wgt = [[mem[:, at + n * KD * FF:at + (n + 1) * KD * FF] for n in range(3)] for at in slot_at]
        work = rest + 6 * KD * FF
        wqkv = mem[:, WORDS - KD * QKV:WORDS].rearrange("p (k n) -> p k n", k=KD)
        moe_end = WORDS - KD * QKV

        m = Arena(mem, rest, WORDS)
        pages = [m.take(PAGES, ROW) for _ in range(2)]
        over = Arena(mem, rest, rest + PAGES * ROW)
        w_a = over.take(KD, QL + ROW)
        hT_m = over.take(KD, P)
        h_m = over.take(D)
        over = Arena(mem, rest, rest + PAGES * ROW)
        wo_m = over.take(KD, D)
        cqT = m.take(3, TOK)
        cT = m.take(2, TOK)
        krT = m.take(TOK)
        oT = m.take(H, TOK)
        rowbuf = m.take(ROW)
        cq = m.take(QL)
        qgain = m.take(QL)
        kvgain = m.take(CL)
        rt = m.take(4, DR // 2)
        cqjunk = m.take(QL)
        ams = m.take(4)
        qnS = m.take(H, NS)
        qrS = m.take(PAIRS, NS)
        causal = m.take(P)
        swap = m.take(P)
        ptab = m.take(NB * PAGES, dt=I32)
        cosT = m.take(TOK)
        sinT = m.take(TOK)
        pair_from = m.at
        wqp = m.take(3, 2 * (DN + DR))
        wkp = m.take(2, 4 * DN)
        qn = [m.take(SEQ) for _ in range(2)]
        qr = m.take(TOK)
        qraw = m.take(TOK)
        qsw = m.take(TOK)
        kn = [m.take(SEQ) for _ in range(2)]
        v_m = m.take(PT, 2 * DN)
        p_m = [m.take(SEQ) for _ in range(2)]
        pT_m = [m.take(PT, P) for _ in range(2)]
        o_m = [m.take(P) for _ in range(2)]
        soft = [m.take(4) for _ in range(2)]
        s = Arena(mem, pair_from, WORDS)
        wkvb = s.take(2, 2 * H * DN)
        wukT = s.take(H, 2, P)
        kT = [s.take(3, 4, P) for _ in range(2)]
        pT_s = s.take(8, P)
        p_s = s.take(8 * P)
        pn_s = s.take(NS)
        pTn_s = s.take(NS)
        o_s = s.take(CL)
        l_bc = s.take(P)
        mrow = s.take(NS + P)
        qlat = s.take(2, NB, NS)
        qrope = s.take(NB, NS)
        qb = [s.take(3, NS) for _ in range(2)]
        olatT = s.take(2, H, NS)
        smask = s.take(NB, NS)
        sel32 = s.take(NS)
        st = s.take(8)
        linv = s.take(NS)

        r = Arena(mem, work, moe_end)
        rankm = r.take(TILES, FETCHES)
        code = r.take(2, TILES, FETCHES)
        jstart = r.take(LIST)
        lst = r.take(2 * NE, dt=I32)
        shift = r.take(TILES)
        onehot = [r.take(TILES, BLK) for _ in range(2)]
        fetch_at = [r.take(1, dt=I32) for _ in range(2)]
        store_at = [r.take(1, dt=I32) for _ in range(2)]
        store_rows = r.take(FETCHES, dt=I32)
        sg = r.take(FF)
        hid = r.take(FF)
        hidT = r.take(KF, BLK)
        xeT = [r.take(KD, BLK) for _ in range(2)]
        moe_at = r.at
        xe = [r.take(D) for _ in range(2)]
        ye = [r.take(D) for _ in range(2)]
        router = Arena(mem, moe_at, moe_end)
        h_r = router.take(D)
        hT_r = router.take(KD, P)
        rw = router.take(KD, NG + NE)
        rbias = router.take(NG + NE)
        lg = router.take(TILES, NG + NE)
        t5 = [router.take(TILES) for _ in range(8)]
        tg = [router.take(TILES, NG) for _ in range(3)]
        te = [router.take(TILES, NE) for _ in range(5)]
        lt = router.take(96)
        jrep = router.take(P)
        pages_flat = [mem[:, rest + n * PAGES * ROW:rest + (n + 1) * PAGES * ROW] for n in range(2)]
        h_fin = xe
        ybuf = [mem[:, slot_at[0] + n * 2 * D:slot_at[0] + (n + 1) * 2 * D] for n in range(2)]

        w = Arena(mem, rest, moe_end)
        wo_w = w.take(KD, D)
        h_w = w.take(D)
        hT_w = w.take(KD, P)
        qkv = w.take(QKV)
        half = (SH + SKV) * SD // 2
        tw = [w.take(half) for _ in range(2)]
        qkr = w.take((SH + SKV) * SD)
        qT_w = w.take(SUNITS, P)
        kT_w = w.take(SKV, 2 * P)
        vb = w.take((TILES + 1) * SKV * SD)
        bqkv = w.take(QKV)
        bo = w.take(D)
        sinks = w.take(SH)
        masks = w.take(PT * 2 * P)
        sw = [w.take(2, 2 * P) for _ in range(2)]
        pT_w = [w.take(4, P) for _ in range(2)]
        den = w.take(SH)
        mw = [w.take(8) for _ in range(2)]
        o_w = w.take(D)
        oT_w = w.take(KD, P)
        z = Arena(mem, moe_end, WORDS)
        kbuf = z.take(NB, SKV * SD)
        vbuf = z.take(NB, SKV * SD)
        kbT = z.take(NB, 2, P)
        qS = z.take(2, NB, NS)
        s_z = z.take(NB, P + NS)
        mask_z = z.take(P + NB * NS)
        sink_z = z.take(1)
        m_z = z.take(NB)
        l_z = z.take(NB)
        pT_z = z.take(NB, P)
        pTn_z = z.take(NB, P)

        rows_in = nc.dram_tensor("moe_rows_in", (TOK, D), F32, kind="Internal").ap()
        rows_back = nc.dram_tensor("moe_rows_back", (2 * TOK, D), F32, kind="Internal").ap()

        block = ctx.enter_context(nc.Block())

        def xt(T, n=P, c0=0, c1=D):
            return x[0:n, cols(T * D + c0, c1 - c0)]

        def unit(q):
            return divmod(q, PT)

        @block.sync
        def _(sp):
            start_counts(sp, "sync")
            sp.dma_start(x[:, 0:PT * D].rearrange("p (t d) -> p t d", t=PT),
                         a["x_prompt"][0].rearrange("(t p) d -> p t d", p=P)).then_inc(sig["x_in"], DMA)
            sp.wait_ge(sig["x_pad"], happened("x_pad", 1))
            sp.dma_start(xt(PT, NS), a["x_sample"].rearrange("b t d -> (b t) d")).then_inc(sig["x_in"], DMA)
            sp.dma_start(w_a, a["mla_w_a"][0].rearrange("(p k) n -> p k n", k=KD)).then_inc(sig["w_a_in"], DMA)
            sp.dma_start(ptab[0:1, :], a["page_table"].rearrange("b n -> (b n)").unsqueeze(0)
                         ).then_inc(sig["ptab_in"], DMA)
            wq = a["mla_wq_b"][0].rearrange("(k p) n -> p k n", p=P)
            wkv = a["mla_wkv_b"][0].rearrange("(k p) n -> p k n", p=P)

            def rows_out(T):
                sp.wait_ge(sig["rows_ready"], happened("rows_ready", T + 1))
                n = rows_of(T)
                dst = (o["mla_rows_sample"][0].rearrange("b t c -> (b t) c") if n == NS
                       else o["mla_rows_prompt"][0, 0][cols(T * P, P), :])
                sp.dma_start(dst, rowbuf[0:n, :]).then_inc(sig["rows_out"], DMA)

            def load_pages(b, par):
                with sp.Fori(0, PAGES) as j:
                    page = sp.value_load(ptab[0:1, bass.ds(b * PAGES + j, 1)], min_val=0, max_val=PHYS - 1)
                    sp.dma_start(pages_flat[par][:, bass.ds(j * ROW, ROW)],
                                 a["cache_mla"][0][bass.ds(page, 1)].rearrange("a p c -> p (a c)")
                                 ).then_inc(sig[f"pages{par}"], DMA)

            def load_pair(j):
                sp.wait_ge(sig["q_mm"], happened("q_mm", j))
                for hh in range(2):
                    head = (2 * j + hh) * (DN + DR)
                    sp.dma_start(wqp[:, :, hh * DN:(hh + 1) * DN], wq[:, :, cols(head, DN)]).then_inc(sig["wqp_in"], DMA)
                    sp.dma_start(wqp[:, :, 2 * DN + hh * DR:2 * DN + (hh + 1) * DR], wq[:, :, cols(head + DN, DR)]
                                 ).then_inc(sig["wqp_in"], DMA)
                sp.wait_ge(sig["kv_mm"], happened("kv_mm", j))
                sp.dma_start(wkp, wkv[:, :, cols(j * 4 * DN, 4 * DN)]).then_inc(sig["wkp_in"], DMA)

            with sp.Fori(0, PT) as T:
                rows_out(T)
            rows_out(PT)
            load_pair(0)
            sp.wait_ge(sig["a_mm"], happened("a_mm", TILES))
            sp.wait_ge(sig["ptab_in"], landed("ptab_in", 1))
            load_pages(0, 0)
            load_pages(1, 1)
            with sp.Fori(1, PAIRS) as j:
                load_pair(j)
            sp.wait_ge(sig["oT_act"], happened("oT_act", 2 * PAIRS * PT))
            sp.dma_start(wkvb, wkv).then_inc(sig["wkvb_in"], DMA)
            with sp.Fori(1, NB // 2) as i:
                for par in range(2):
                    sp.wait_ge(sig["pv_mm"], happened("pv_mm", 2 * i + par - 1))
                    turnstile(sp)
                    load_pages(2 * i + par, par)
            sp.wait_ge(sig["pv_mm"], happened("pv_mm", NB - 1))
            sp.dma_start(wo_m, a["mla_wo"][0].rearrange("(k p) n -> p k n", p=P)).then_inc(sig["wo_in"], DMA)

            def experts(L):
                sp.wait_ge(sig["wo_mm"], happened("wo_mm", (L + 1) * TILES))
                sp.wait_ge(sig["x_ready"], happened("x_ready", 2 * L + 1))
                start_more(sp, L, "weights")
                sp.dma_start(rw[:, :, 0:NG], a["moe_w_group"][L].rearrange("(p k) n -> p k n", k=KD)
                             ).then_inc(sig["rw_in"], DMA)
                sp.dma_start(rw[:, :, NG:], a["moe_w_expert"][L].rearrange("(p k) n -> p k n", k=KD)
                             ).then_inc(sig["rw_in"], DMA)
                sp.wait_ge(sig["saved"], happened("saved", TILES * (L + 1)))
                with sp.Fori(0, NE // 2) as i:
                    for par in range(2):
                        e = 2 * i + par
                        sp.wait_ge(sig["gu_mm"], happened("gu_mm", NE * L + e - 1))
                        for n, kind in enumerate(("gate", "up")):
                            sp.dma_start(wgt[par][n], a[f"moe_w_{kind}"][L][bass.ds(e, 1)]
                                         .rearrange("a (p k) f -> p (a k f)", k=KD)
                                         ).then_inc(sig[f"{kind[0]}{par}_in"], DMA)
                        sp.wait_ge(sig["d_mm"], happened("d_mm", NE * L + e - 1))
                        sp.dma_start(wgt[par][2], a["moe_w_down"][L][bass.ds(e, 1)]
                                     .rearrange("a (p k) n -> p (a k n)", k=KF)
                                     ).then_inc(sig[f"d{par}_in"], DMA)
                if L == 0:
                    sp.dma_start(wqkv, a["swa_wqkv"][0].rearrange("(p k) n -> p k n", k=KD)
                                 ).then_inc(sig["wqkv_in"], DMA)
                sp.wait_ge(sig["d_mm"], happened("d_mm", NE * (L + 1)))
                n = sp.value_load(lst[0:1, 2 * NE - 1:2 * NE], min_val=0, max_val=LIST)
                with sp.If(n > 0):
                    with sp.Fori(0, n) as i:
                        sp.wait_ge(sig["more_d_mm"], i + 1)
                        e = sp.value_load(lst[0:1, bass.ds(i, 1)], min_val=0, max_val=NE - 1)
                        for n_, kind in enumerate(("gate", "up", "down")):
                            sp.dma_start(wgt[0][n_], a[f"moe_w_{kind}"][L][bass.ds(e, 1)]
                                         .rearrange("a (p k) f -> p (a k f)", k=KF if kind == "down" else KD)
                                         ).then_inc(sig["more_weights"], DMA)
                sp.wait_ge(sig["moe_done"], happened("moe_done", L + 1))
                for T in range(TILES):
                    if T >= 2:
                        sp.wait_ge(sig["y_added"], happened("y_added", TILES * L + T - 1))
                    n = rows_of(T)
                    sp.dma_start(ybuf[T % 2][0:n, :],
                                 rows_back[2 * T * P:2 * T * P + 2 * n, :].rearrange("(p c) d -> p (c d)", c=2)
                                 ).then_inc(sig[f"ybuf{T % 2}"], DMA)

            experts(0)
            sp.wait_ge(sig["x_ready"], happened("x_ready", 2))
            sp.dma_start(wo_w, a["swa_wo"][0].rearrange("(k p) n -> p k n", p=P)).then_inc(sig["wo_w_in"], DMA)
            sp.wait_ge(sig["qkr_ready"], happened("qkr_ready", PT))
            sp.dma_start(o["swa_kv_prompt"][0, 0, :, 0].rearrange("p h d -> p (h d)"), qkr[:, SH * SD:]
                         ).then_inc(sig["state_out"], DMA)
            sp.dma_start(o["swa_kv_prompt"][0, 0, :, 1].rearrange("p h d -> p (h d)"), qkv[:, (SH + SKV) * SD:]
                         ).then_inc(sig["state_out"], DMA)
            cache = a["cache_swa_kv"][0].rearrange("b w s h d -> b w (s h d)")
            out_s = o["swa_kv_sample"][0].rearrange("b w s h d -> b w (s h d)")
            sp.dma_start(out_s[:, 0:P - NT, :], cache[:, NT:P, :]).then_inc(sig["windows_out"], DMA)
            sp.wait_ge(sig["qkr_ready"], happened("qkr_ready", TILES))
            for b in range(NB):
                for part, src in ((0, qkr[:, SH * SD:]), (1, qkv[:, (SH + SKV) * SD:])):
                    sp.dma_start(out_s[b, P - NT:P, part * SKV * SD:(part + 1) * SKV * SD],
                                 src[b * NT:(b + 1) * NT, :]).then_inc(sig["windows_out"], DMA)
            sp.wait_ge(sig["qkv_mm"], happened("qkv_mm", 3 * TILES))
            kv = a["cache_swa_kv"][0].rearrange("b w s h d -> w s b (h d)")
            sp.dma_start(kbuf, kv[:, 0]).then_inc(sig["cacheb_in"], DMA)
            sp.dma_start(vbuf, kv[:, 1]).then_inc(sig["cacheb_in"], DMA)
            sp.dma_start(mask_z, a["c_mask_z"]).then_inc(sig["cacheb_in"], DMA)
            sp.wait_ge(sig["sink_clear"], happened("sink_clear", 1))
            for g in range(SKV):
                sp.dma_start(sink_z[32 * g:32 * g + SG * NT, :],
                             a["swa_sinks"][0][g * SG:(g + 1) * SG].unsqueeze(1).broadcast_to([SG, NT])
                             ).then_inc(sig["cacheb_in"], DMA)
            experts(1)
            for T in range(TILES):
                sp.wait_ge(sig["y_ready"], happened("y_ready", T + 1))
                n = rows_of(T)
                dst = o["y_prompt"][0][T * P:(T + 1) * P, :] if T < PT else o["y_sample"].rearrange("b t d -> (b t) d")
                sp.dma_start(dst, h_fin[T % 2][0:n, :]).then_inc(sig[f"y_out{T % 2}"], DMA)
            sp.wait_ge(sig["rows_out"], landed("rows_out", TILES))
            sp.wait_ge(sig["state_out"], landed("state_out", 2))
            sp.wait_ge(sig["windows_out"], landed("windows_out", 1 + 2 * NB))
            sp.wait_ge(sig["y_out0"], landed("y_out0", 3))
            sp.wait_ge(sig["y_out1"], landed("y_out1", 2))

        @block.gpsimd
        def _(g):
            start_counts(g, "pool")
            g.dma_start(consts, a["c_consts"]).then_inc(sig["consts_in"], DMA)
            g.dma_start(cos_tok, a["c_cos_tok"]).then_inc(sig["consts_in"], DMA)
            g.dma_start(sin_tok, a["c_sin_tok"]).then_inc(sig["consts_in"], DMA)

            def row(ap, n=P):
                return ap.unsqueeze(0).broadcast_to([n, ap.shape[0]])

            g.dma_start(gain, row(a["norm_mix"][0])).then_inc(sig["gain_in"], DMA)
            for dst, src in ((qgain, row(a["mla_q_norm"][0])), (kvgain, row(a["mla_kv_norm"][0])),
                             (causal, a["c_causal"]), (swap, a["c_swap"]), (cosT, a["c_cosT"]), (sinT, a["c_sinT"])):
                g.dma_start(dst, src).then_inc(sig["mlaconst_in"], DMA)
            g.wait_ge(sig["oT_act"], happened("oT_act", 2 * PAIRS * PT))
            g.dma_start(smask, a["c_smask"]).then_inc(sig["mlaconst_in"], DMA)
            g.dma_start(sel32, a["c_sel32"]).then_inc(sig["mlaconst_in"], DMA)

            def experts(L):
                start_more(g, L, "done")
                g.sem_inc(sig["more_done"], 1)
                g.wait_ge(sig["h_ready"], happened("h_ready", TILES * (2 * L + 1)))
                g.dma_start(gain, row(a["norm_ffn"][L])).then_inc(sig["gain_in"], DMA)
                g.wait_ge(sig["wo_mm"], happened("wo_mm", (L + 1) * TILES))
                g.wait_ge(sig["x_ready"], happened("x_ready", 2 * L + 1))
                g.dma_start(rbias[:, 0:NG], row(a["moe_b_group"][L])).then_inc(sig["scattered0"], DMA)
                g.dma_start(rbias[:, NG:], row(a["moe_b_expert"][L])).then_inc(sig["scattered1"], DMA)

                def save(T):
                    g.wait_ge(sig["h_ready"], happened("h_ready", TILES * (2 * L + 1) + T + 1))
                    n = rows_of(T)
                    g.dma_start(rows_in[cols(T * P, n), :], h_r[0:n, :]).then_inc(sig["xn_out"], DMA)
                    g.wait_ge(sig["xn_out"], landed("xn_out", TILES * L + T + 1))
                    g.sem_inc(sig["saved"], 1)

                with g.Fori(0, PT) as T:
                    save(T)
                save(PT)
                g.wait_ge(sig["h_ready"], happened("h_ready", TILES * (2 * L + 2)))
                g.dma_start(gain, row(a["norm_mix"][1] if L == 0 else a["norm_final"])).then_inc(sig["gain_in"], DMA)
                g.wait_ge(sig["lst_ready"], happened("lst_ready", L + 1))
                for b in range(2):
                    g.memset(xe[b], 0.0)
                g.drain()

                def fetch(q, b):
                    g.wait_ge(sig["idx_ready"], happened("idx_ready", FETCHES * L + q + 1))
                    turnstile(g)
                    g.wait_ge(sig["xt_mm"], happened("xt_mm", (NE + 1) * L + q - 1))
                    turnstile(g)
                    g.indirect_dma_start(out=xe[b][0:BLK, :], out_offset=None, in_=rows_in,
                                         in_offset=bass.IndirectOffsetOnAxis(ap=fetch_at[b][0:BLK, 0:1].bitcast(U32), axis=0),
                                         bounds_check=TOK - 1, oob_is_err=False).then_inc(sig[f"gathered{b}"], DMA)

                def store(e, b):
                    g.wait_ge(sig["y0_ready"], happened("y0_ready", NE * L + e + 1))
                    turnstile(g)
                    g.wait_ge(sig["y1_ready"], happened("y1_ready", NE * L + e + 1))
                    turnstile(g)
                    g.indirect_dma_start(out=rows_back, out_offset=bass.IndirectOffsetOnAxis(ap=store_at[b][0:BLK, 0:1].bitcast(U32), axis=0),
                                         in_=ye[b][0:BLK, :], in_offset=None,
                                         bounds_check=2 * TOK - 1, oob_is_err=False).then_inc(sig[f"scattered{b}"], DMA)

                for q in range(LOOK):
                    fetch(q, q % 2)
                with g.Fori(0, NE // 2) as i:
                    for b in range(2):
                        fetch(2 * i + b + LOOK, 1 - b)
                        store(2 * i + b, b)
                for b in range(2):
                    g.wait_ge(sig[f"gathered{b}"], landed(f"gathered{b}", INTO[b] * (L + 1)))
                    g.wait_ge(sig[f"scattered{b}"], landed(f"scattered{b}", STORES * (L + 1)))
                n = g.value_load(lst[0:1, 2 * NE - 1:2 * NE], min_val=0, max_val=LIST)
                with g.If(n > 0):
                    with g.Fori(0, n) as i:
                        g.wait_ge(sig["more_idx_cv"], i + 1)
                        turnstile(g)
                        g.indirect_dma_start(out=xe[0][0:BLK, :], out_offset=None, in_=rows_in,
                                             in_offset=bass.IndirectOffsetOnAxis(ap=fetch_at[0][0:BLK, 0:1].bitcast(U32), axis=0),
                                             bounds_check=TOK - 1, oob_is_err=False).then_inc(sig[f"more_gather{L}"], DMA)
                        g.wait_ge(sig["more_y0"], i + 1)
                        turnstile(g)
                        g.wait_ge(sig["more_y1"], i + 1)
                        turnstile(g)
                        g.indirect_dma_start(out=rows_back, out_offset=bass.IndirectOffsetOnAxis(ap=store_at[0][0:BLK, 0:1].bitcast(U32), axis=0),
                                             in_=ye[0][0:BLK, :], in_offset=None,
                                             bounds_check=2 * TOK - 1, oob_is_err=False).then_inc(sig[f"more_scatter{L}"], DMA)
                        g.wait_ge(sig[f"more_scatter{L}"], (i + 1) * DMA)
                        turnstile(g)
                        g.sem_inc(sig["more_done"], 1)
                g.sem_inc(sig["moe_done"], 1)

            experts(0)
            g.wait_ge(sig["x_ready"], happened("x_ready", 2))
            for dst, src in ((bqkv, row(a["swa_bqkv"][0])), (bo, row(a["swa_bo"][0])),
                             (sinks, row(a["swa_sinks"][0])), (masks, a["c_masks"])):
                g.dma_start(dst, src).then_inc(sig["swaconst_in"], DMA)
            experts(1)

        @block.scalar
        def _(act):
            start_counts(act, "scalar")

            def copy(out, in_):
                return act.activation(out, in_, ACT.Copy)

            def sums(f, junk):
                if f == 0:
                    act.wait_ge(sig["x_in"], landed("x_in", 2))
                else:
                    act.wait_ge(sig["x_ready"], happened("x_ready", f))
                for T in range(TILES):
                    act.drain()
                    last = act.activation(junk, xt(T), ACT.Square, accum_out=sumsq[:, T:T + 1])
                act.drain().then_inc(sig["sumsq_ready"], 1)
                act.wait_ge(sig["meansq"], happened("meansq", f + 1))
                act.activation(rstd[:, 0:TILES], sumsq[:, 0:TILES], ACT.Sqrt).then_inc(sig["root_ready"], 1)

            def half_T(f, T, hT):
                n = rows_of(T)
                act.wait_ge(sig["hT_mm"], happened("hT_mm", TILES * f + T + 1))
                copy(hT[:, 0:4, 0:n], ps[:, 0, :].rearrange("p (k t) -> p k t", k=4)[:, :, 0:n]
                     ).then_inc(sig["hTa"], 1)

            sums(0, hT_m.rearrange("p k t -> p (k t)"))

            def project(T):
                n = rows_of(T)
                half_T(0, T, hT_m)
                act.wait_ge(sig["a_mm"], happened("a_mm", T + 1))
                act.activation(cqjunk[0:n, :], ps[0:n, 2, 0:QL], ACT.Square, accum_out=ams[0:n, 0:1])
                act.drain()
                act.activation(cqjunk[0:n, 0:CL], ps[0:n, 3, 0:CL], ACT.Square, accum_out=ams[0:n, 1:2])
                act.drain().then_inc(sig["a_sq"], 1)
                act.wait_ge(sig["a_ms"], happened("a_ms", T + 1))
                act.activation(ams[0:n, 2:4], ams[0:n, 0:2], ACT.Sqrt).then_inc(sig["a_root"], 1)
                act.wait_ge(sig["rowsT_mm"], happened("rowsT_mm", T + 1))
                copy(cqT[:, :, cols(T * P, n)], ps[:, 4, 0:QL].rearrange("p (k t) -> p k t", k=3)[:, :, 0:n]
                     ).then_inc(sig["cqT_ready"], 1)

            with act.Fori(0, PT) as T:
                project(T)
            project(PT)

            with act.Fori(0, PAIRS) as j:
                act.wait_ge(sig["q_mm"], happened("q_mm", j + 1))
                copy(qn[0][:, 0:SEQ], ps[:, 0, :])
                copy(qraw[:, 0:SEQ], ps[:, 3, :])
                act.drain().then_inc(sig["q_act"], 1)
                act.wait_ge(sig["kv_mm"], happened("kv_mm", j + 1))
                copy(kn[0], ps[:, 5, :])
                copy(v_m[:, 0:2, :], ps[:, 7, :].rearrange("p (t n) -> p t n", t=2))
                act.drain().then_inc(sig["kv_act"], 1)

                def finish(q):
                    hh, qi = unit(q)
                    act.wait_ge(sig["oT_mm"], happened("oT_mm", 2 * PT * j + q + 1))
                    copy(oT[:, bass.ds(2 * j + hh, 1), qi * P:(qi + 1) * P], ps[:, 6 + q % 2, 0:P].unsqueeze(1)
                         ).then_inc(sig["oT_act"], 1)

                for q in range(2 * PT):
                    hh, qi = unit(q)
                    nk = (qi + 1) * P
                    act.wait_ge(sig["nm_ready"], happened("nm_ready", 2 * PT * j + q + 1))
                    act.wait_ge(sig["pT_mm"], happened("pT_mm", 2 * PT * j + q - 1))
                    act.activation(p_m[q % 2][:, 0:nk], ps[:, q % 2, 0:nk], ACT.Exp, bias=soft[q % 2][:, 1:2],
                                   scale=MLA_SCALE, accum_out=soft[q % 2][:, 2:3])
                    act.drain().then_inc(sig["p_ready"], 1)
                    if q:
                        finish(q - 1)
                finish(2 * PT - 1)

            for n in range(0, 4, 2):
                act.wait_ge(sig["wuk_mm"], happened("wuk_mm", n + 1))
                copy(wukT[:, 2 * n:2 * n + 2], ps[:, n, :].rearrange("p (h k c) -> p h k c", h=2, k=2)
                     ).then_inc(sig["wuk_act"], 1)

            def sequence(b, par):
                for t in range(8):
                    step = 8 * b + t
                    act.wait_ge(sig["qk_mm"], happened("qk_mm", step - 1))
                    act.wait_ge(sig["kt_mm0"], happened("kt_mm0", step + 1))
                    copy(kT[t % 2][:, 0], ps[:, 2, :].rearrange("p (g c) -> p g c", g=4)).then_inc(sig["kt0"], 1)
                    act.wait_ge(sig["kt_mm2"], happened("kt_mm2", step + 1))
                    copy(kT[t % 2][0:DR, 2], ps[0:DR, 4, :].rearrange("p (g c) -> p g c", g=4)).then_inc(sig["kt2"], 1)
                act.wait_ge(sig["nms_ready"], happened("nms_ready", b + 1))
                act.activation(p_s.rearrange("p (n c) -> p n c", n=2), ps[:, 0:2, :], ACT.Exp, bias=st[:, 2:3],
                               scale=MLA_SCALE, accum_out=st[:, 3:4])
                act.activation(pn_s[0:NS, :], ps[0:NS, 5, 0:NS], ACT.Exp, bias=st[0:NS, 2:3],
                               scale=MLA_SCALE, accum_out=st[0:NS, 4:5])
                act.drain().then_inc(sig["p_s_ready"], 1)
                act.wait_ge(sig["pT_s_mm"], happened("pT_s_mm", 2 * b + 1))
                copy(pT_s[:, 0:4], ps[:, 7, :].rearrange("p (n c) -> p n c", n=4)).then_inc(sig["pTa_s"], 1)
                act.wait_ge(sig["pv_mm"], happened("pv_mm", b + 1))
                copy(o_s, ps[:, 6, 0:CL]).then_inc(sig["o_s_ready"], 1)

            with act.Fori(0, NB // 2) as i:
                for par in range(2):
                    sequence(2 * i + par, par)

            def experts(L):
                f = 2 * L + 1
                start_more(act, L, "xeT silu y0")
                sums(f, hT_r.rearrange("p k t -> p (k t)"))
                with act.Fori(0, PT) as T:
                    half_T(f, T, hT_r)
                half_T(f, PT, hT_r)
                act.wait_ge(sig["gsub_ready"], happened("gsub_ready", L + 1))
                act.activation(tg[1], tg[0], ACT.Exp).then_inc(sig["gexp_ready"], 1)
                act.wait_ge(sig["esub_ready"], happened("esub_ready", L + 1))
                act.activation(t5[5], t5[4], ACT.Exp).then_inc(sig["eexp_ready"], 1)

                def rows_T(q, b):
                    act.wait_ge(sig["xt_mm"], happened("xt_mm", (NE + 1) * L + q + 1))
                    copy(xeT[b], ps[:, 5, :].rearrange("p (k t) -> p k t", k=KD)).then_inc(sig["xeT_ready"], 1)

                act.wait_ge(sig["lst_ready"], happened("lst_ready", L + 1))
                rows_T(0, 0)
                with act.Fori(0, NE // 2) as i:
                    for b in range(2):
                        e = 2 * i + b
                        act.wait_ge(sig["gu_mm"], happened("gu_mm", NE * L + e + 1))
                        act.wait_ge(sig["hid_ready"], happened("hid_ready", NE * L + e))
                        act.activation(sg[BLK:2 * BLK, :], ps[0:BLK, b, :], ACT.Silu).then_inc(sig["silu_ready"], 1)
                        rows_T(e + 1, 1 - b)
                        act.wait_ge(sig["d_mm"], happened("d_mm", NE * L + e + 1))
                        act.wait_ge(sig[f"scattered{b}"], landed(f"scattered{b}", STORES * L + i + 1))
                        copy(ye[b][0:BLK, 0:FF], ps[0:BLK, 2 + b, :]).then_inc(sig["y0_ready"], 1)
                n = act.value_load(lst[0:1, 2 * NE - 1:2 * NE], min_val=0, max_val=LIST)
                with act.If(n > 0):
                    with act.Fori(0, n) as i:
                        act.wait_ge(sig["more_xt_mm"], i + 1)
                        copy(xeT[0], ps[:, 5, :].rearrange("p (k t) -> p k t", k=KD)).then_inc(sig["more_xeT"], 1)
                        act.wait_ge(sig["more_gu_mm"], i + 1)
                        act.activation(sg[BLK:2 * BLK, :], ps[0:BLK, 0, :], ACT.Silu).then_inc(sig["more_silu"], 1)
                        act.wait_ge(sig["more_d_mm"], i + 2)
                        copy(ye[0][0:BLK, 0:FF], ps[0:BLK, 2, :]).then_inc(sig["more_y0"], 1)

            experts(0)

            sums(2, hT_w.rearrange("p k t -> p (k t)"))

            def window(T):
                n = rows_of(T)
                half_T(2, T, hT_w)
                act.wait_ge(sig["v_ready"], happened("v_ready", T + 1))
                copy(vb[0:n, cols((T + 1) * SKV * SD, SKV * SD)], qkv[0:n, (SH + SKV) * SD:]).then_inc(sig["v_w"], 1)
                act.wait_ge(sig["qT_mm"], happened("qT_mm", T + 1))
                if n == P:
                    copy(qT_w[:, 0:4, 0:n], ps[:, 5, :].rearrange("p (k t) -> p k t", k=4)[:, :, 0:n]
                         ).then_inc(sig["qTa_w"], 1)

            def attend(T):
                for u in range(SUNITS):
                    act.wait_ge(sig["s_w_ready"], happened("s_w_ready", SUNITS * T + u + 1))
                    for c in range(2):
                        act.activation(sw[u % 2][:, c], sw[u % 2][:, c], ACT.Exp, bias=mw[u % 2][:, 2 + c:3 + c],
                                       scale=SWA_SCALE, accum_out=mw[u % 2][:, 4 + c:5 + c])
                    act.activation(mw[u % 2][:, 6:8], mw[u % 2][:, 6:8], ACT.Exp)
                    act.drain().then_inc(sig["p_w"], 1)

            def out_T(T):
                n = rows_of(T)
                act.wait_ge(sig["oT_w_mm"], happened("oT_w_mm", T + 1))
                copy(oT_w[:, 0:4, 0:n], ps[:, 0, :].rearrange("p (k t) -> p k t", k=4)[:, :, 0:n]
                     ).then_inc(sig["oTa_w"], 1)

            with act.Fori(0, PT) as T:
                window(T)
                attend(T)
                out_T(T)
            window(PT)
            for n in range(2):
                act.wait_ge(sig["kb_mm"], happened("kb_mm", 2 * n + 1))
                copy(kbT[:, 4 * n:4 * n + 2], ps[:, 2 * n, :].rearrange("p (b g c) -> p b g c", b=2, g=2)
                     ).then_inc(sig["kb_act"], 1)
            act.wait_ge(sig["sample_s"], happened("sample_s", 1))
            act.activation(s_z, s_z, ACT.Exp)
            act.activation(m_z, m_z, ACT.Exp)
            act.drain().then_inc(sig["sample_e"], 1)
            act.wait_ge(sig["sample_pT_mm"], happened("sample_pT_mm", 1))
            copy(pT_z[:, 0:4], ps[:, 4, :].rearrange("p (b r) -> p b r", b=4)).then_inc(sig["sample_pT_act"], 1)
            copy(pTn_z[0:NS, 0:4], ps[0:NS, 6, :].rearrange("p (b r) -> p b r", b=4)).then_inc(sig["sample_pT_act"], 1)
            experts(1)
            sums(4, ye[0])

        @block.vector
        def _(v):
            start_counts(v, "vector")
            v.memset(xt(PT), 0.0)
            v.drain().then_inc(sig["x_pad"], 1)

            def roots(f):
                v.wait_ge(sig["sumsq_ready"], happened("sumsq_ready", f + 1))
                v.tensor_scalar(sumsq[:, 0:TILES], sumsq[:, 0:TILES], 1.0 / D, EPS, ALU.mult, ALU.add
                                ).then_inc(sig["meansq"], 1)
                v.wait_ge(sig["root_ready"], happened("root_ready", f + 1))
                v.reciprocal(rstd[:, 0:TILES], rstd[:, 0:TILES])
                v.drain()
                v.wait_ge(sig["gain_in"], landed("gain_in", f + 1))

            def norm_tile(f, T, h):
                n = rows_of(T)
                v.wait_ge(sig["hT_mm"], happened("hT_mm", TILES * f + T))
                v.scalar_tensor_tensor(out=h[0:n, :], in0=xt(T, n), scalar=rstd[0:n, cols(T, 1)], in1=gain[0:n, :],
                                       op0=ALU.mult, op1=ALU.mult).then_inc(sig["h_ready"], 1)

            def half_T(f, T, hT):
                n = rows_of(T)
                v.wait_ge(sig["hT_mm"], happened("hT_mm", TILES * f + T + 1))
                v.tensor_copy(hT[:, 4:8, 0:n], ps[:, 1, :].rearrange("p (k t) -> p k t", k=4)[:, :, 0:n]
                              ).then_inc(sig["hTb"], 1)

            v.wait_ge(sig["consts_in"], landed("consts_in", 3))
            v.wait_ge(sig["x_in"], landed("x_in", 2))
            roots(0)
            v.wait_ge(sig["mlaconst_in"], landed("mlaconst_in", 6))

            def project(T):
                n = rows_of(T)
                norm_tile(0, T, h_m)
                half_T(0, T, hT_m)
                v.wait_ge(sig["a_sq"], happened("a_sq", T + 1))
                v.tensor_scalar(ams[0:n, 0:1], ams[0:n, 0:1], 1.0 / QL, EPS, ALU.mult, ALU.add)
                v.tensor_scalar(ams[0:n, 1:2], ams[0:n, 1:2], 1.0 / CL, EPS, ALU.mult, ALU.add)
                v.drain().then_inc(sig["a_ms"], 1)
                v.wait_ge(sig["a_root"], happened("a_root", T + 1))
                v.reciprocal(ams[0:n, 2:4], ams[0:n, 2:4])
                v.drain()
                v.wait_ge(sig["rows_out"], landed("rows_out", T))
                v.scalar_tensor_tensor(out=cq[0:n, :], in0=ps[0:n, 2, 0:QL], scalar=ams[0:n, 2:3], in1=qgain[0:n, :],
                                       op0=ALU.mult, op1=ALU.mult)
                v.scalar_tensor_tensor(out=rowbuf[0:n, 0:CL], in0=ps[0:n, 3, 0:CL], scalar=ams[0:n, 3:4],
                                       in1=kvgain[0:n, :], op0=ALU.mult, op1=ALU.mult)
                c, s_ = (q[0:n, cols(T * DR // 2 if isinstance(T, int) else T * (DR // 2), DR // 2)] for q in (cos_tok, sin_tok))
                k1, k2 = ps[0:n, 3, CL:CL + DR // 2], ps[0:n, 3, CL + DR // 2:ROW]
                for dst, k, t in ((0, k1, c), (1, k2, s_), (2, k2, c), (3, k1, s_)):
                    v.tensor_tensor(rt[0:n, dst], k, t, ALU.mult)
                v.drain()
                v.tensor_tensor(rowbuf[0:n, CL:CL + DR // 2], rt[0:n, 0], rt[0:n, 1], ALU.subtract)
                v.tensor_tensor(rowbuf[0:n, CL + DR // 2:ROW], rt[0:n, 2], rt[0:n, 3], ALU.add)
                v.drain().then_inc(sig["rows_ready"], 1)
                v.wait_ge(sig["rowsT_mm"], happened("rowsT_mm", T + 1))
                v.tensor_copy(cT[:, :, cols(T * P, n)], ps[:, 5, 0:CL].rearrange("p (k t) -> p k t", k=2)[:, :, 0:n])
                for half_ in range(2):
                    v.tensor_copy(krT[half_ * DR:(half_ + 1) * DR, cols(T * P, n)], ps[0:DR, 5, CL:CL + n])
                v.drain().then_inc(sig["cT_ready"], 1)

            with v.Fori(0, PT) as T:
                project(T)
            project(PT)

            with v.Fori(0, PAIRS) as j:
                v.wait_ge(sig["q_mm"], happened("q_mm", j + 1))
                v.tensor_copy(qn[1], ps[:, 1, :])
                v.tensor_copy(qnS[:, bass.ds(2 * j, 2), :], ps[:, 2, 0:2 * NS].rearrange("p (h t) -> p h t", h=2))
                v.tensor_copy(qraw[:, SEQ:], ps[:, 2, 2 * NS:3 * NS])
                v.drain().then_inc(sig["q_dve"], 1)
                v.wait_ge(sig["swap_mm"], happened("swap_mm", j + 1))
                v.tensor_tensor(qsw[:, 0:SEQ], ps[:, 4, :], sinT[:, 0:SEQ], ALU.mult)
                v.tensor_tensor(qsw[:, SEQ:], ps[:, 2, P:P + NS], sinT[:, SEQ:], ALU.mult)
                v.tensor_tensor(qraw, qraw, cosT, ALU.mult)
                v.drain()
                v.tensor_tensor(qr, qraw, qsw, ALU.add)
                v.drain()
                v.tensor_copy(qrS[:, bass.ds(j, 1), :], qr[:, SEQ:].unsqueeze(1))
                v.drain().then_inc(sig["qr_ready"], 1)
                v.wait_ge(sig["kv_mm"], happened("kv_mm", j + 1))
                v.tensor_copy(kn[1], ps[:, 6, :])
                v.tensor_copy(v_m[:, 2:4, :], ps[:, 1, :].rearrange("p (t n) -> p t n", t=2))
                v.drain().then_inc(sig["kv_dve"], 1)

                def largest(q):
                    hh, qi = unit(q)
                    v.wait_ge(sig["s_mm"], happened("s_mm", 2 * PT * j + q + 1))
                    v.reduce_max(soft[q % 2][:, 0:1], ps[:, q % 2, 0:(qi + 1) * P], X)
                    v.drain()
                    v.tensor_scalar(soft[q % 2][:, 1:2], soft[q % 2][:, 0:1], -MLA_SCALE, None, ALU.mult
                                    ).then_inc(sig["nm_ready"], 1)

                largest(0)
                for q in range(2 * PT):
                    hh, qi = unit(q)
                    if q + 1 < 2 * PT:
                        largest(q + 1)
                    v.wait_ge(sig["pT_mm"], happened("pT_mm", 2 * PT * j + q + 1))
                    v.tensor_copy(pT_m[q % 2][:, 0:qi + 1, :],
                                  ps[:, 2 + q % 2, 0:(qi + 1) * P].rearrange("p (t n) -> p t n", t=qi + 1)
                                  ).then_inc(sig["pT_m_ready"], 1)
                    v.reciprocal(soft[q % 2][:, 3:4], soft[q % 2][:, 2:3])
                    v.drain()
                    v.wait_ge(sig["o_mm"], happened("o_mm", 2 * PT * j + q + 1))
                    v.wait_ge(sig["oT_mm"], happened("oT_mm", 2 * PT * j + q - 1))
                    v.tensor_scalar(o_m[q % 2], ps[:, 4 + q % 2, 0:P], soft[q % 2][:, 3:4], None, ALU.mult
                                    ).then_inc(sig["o_m_ready"], 1)

            for n in range(1, 4, 2):
                v.wait_ge(sig["wuk_mm"], happened("wuk_mm", n + 1))
                v.tensor_copy(wukT[:, 2 * n:2 * n + 2], ps[:, n, :].rearrange("p (h k c) -> p h k c", h=2, k=2)
                              ).then_inc(sig["wuk_dve"], 1)
            v.wait_ge(sig["qlat_mm"], happened("qlat_mm", 1))
            for k in range(2):
                v.tensor_copy(qlat[:, k].rearrange("p b (h t) -> p b h t", h=H),
                              ps[:, 4, k * H * NS:(k + 1) * H * NS].rearrange("p (h b t) -> p b h t", h=H, b=NB))
            for c in range(2):
                for b in range(NB):
                    v.tensor_copy(qrope[0:DR, b].rearrange("p (j c t) -> p j c t", c=2, t=NT)[:, :, c, :],
                                  qrS[c * DR:(c + 1) * DR, :, b * NT:(b + 1) * NT])
            v.drain().then_inc(sig["qlat_ready"], 1)

            def sequence(b, par):
                v.tensor_copy(qb[par][:, 0:2, :], qlat[:, :, bass.ds(b, 1), :].rearrange("p k a q -> p k (a q)"))
                v.tensor_copy(qb[par][0:DR, 2:3, :], qrope[0:DR, bass.ds(b, 1), :])
                v.drain().then_inc(sig["qb_ready"], 1)
                for t in range(8):
                    step = 8 * b + t
                    v.wait_ge(sig["qk_mm"], happened("qk_mm", step - 1))
                    v.wait_ge(sig["kt_mm1"], happened("kt_mm1", step + 1))
                    v.tensor_copy(kT[t % 2][:, 1], ps[:, 3, :].rearrange("p (g c) -> p g c", g=4)).then_inc(sig["kt1"], 1)
                v.wait_ge(sig["new_mm"], happened("new_mm", b + 1))
                v.reduce_max(st[:, 0:1], ps[:, 0:2, :].rearrange("p n c -> p (n c)"), X)
                v.reduce_max(st[0:NS, 1:2], ps[0:NS, 5, 0:NS], X)
                v.drain()
                v.tensor_tensor(st[0:NS, 0:1], st[0:NS, 0:1], st[0:NS, 1:2], ALU.max)
                v.drain().then_inc(sig["mx_ready"], 1)
                v.wait_ge(sig["mxT_mm"], happened("mxT_mm", b + 1))
                v.reduce_max(mrow[0:1, 0:NS], ps[0:1, 5, 64:64 + P].rearrange("p (g q) -> p q g", g=4), X)
                v.drain()
                v.tensor_copy(mrow[0:1, NS:NS + P].rearrange("p (g q) -> p g q", g=4),
                              mrow[0:1, 0:NS].unsqueeze(1).broadcast_to([1, 4, NS])).then_inc(sig["mrow_ready"], 1)
                v.wait_ge(sig["mb_mm"], happened("mb_mm", b + 1))
                v.tensor_scalar(st[:, 2:3], ps[:, 5, 200:201], -MLA_SCALE, None, ALU.mult).then_inc(sig["nms_ready"], 1)
                v.wait_ge(sig["p_s_ready"], happened("p_s_ready", b + 1))
                v.tensor_tensor(st[0:NS, 3:4], st[0:NS, 3:4], st[0:NS, 4:5], ALU.add)
                v.drain()
                v.tensor_scalar(l_bc, ones, st[:, 3:4], None, ALU.mult).then_inc(sig["lbc_ready"], 1)
                v.wait_ge(sig["pT_s_mm"], happened("pT_s_mm", 2 * b + 2))
                v.tensor_copy(pT_s[:, 4:8], ps[:, 4, :].rearrange("p (n c) -> p n c", n=4))
                v.tensor_copy(pTn_s[0:NS, :], ps[0:NS, 5, 224:224 + NS])
                v.drain().then_inc(sig["pTb_s"], 1)
                v.wait_ge(sig["oc_mm"], happened("oc_mm", b + 1))
                v.reciprocal(linv, ps[:, 5, 320:320 + NS])
                v.drain()
                for k in range(2):
                    v.tensor_tensor(olatT[:, k, :, bass.ds(b * NT, NT)],
                                    ps[:, 5, 256 + k * NS:256 + (k + 1) * NS].rearrange("p (h t) -> p h t", h=H),
                                    linv.rearrange("p (h t) -> p h t", h=H), ALU.mult)
                v.drain().then_inc(sig["olat_ready"], 1)

            with v.Fori(0, NB // 2) as i:
                for par in range(2):
                    sequence(2 * i + par, par)
            v.wait_ge(sig["oTs_mm"], happened("oTs_mm", 1))
            v.tensor_copy(oT[:, :, SEQ:], ps[:, 0, 0:H * NS].rearrange("p (h t) -> p h t", h=H)
                          ).then_inc(sig["oTs_ready"], 1)
            for T in range(TILES):
                n = rows_of(T)
                v.wait_ge(sig["wo_mm"], happened("wo_mm", T + 1))
                for c in range(2):
                    v.tensor_tensor(xt(T, n, c * FF, (c + 1) * FF), xt(T, n, c * FF, (c + 1) * FF),
                                    ps[0:n, 2 + 2 * (T % 2) + c, :], ALU.add)
                v.drain().then_inc(sig["wo_added"], 1)
            v.drain().then_inc(sig["x_ready"], 1)

            def over_tiles(ap, n):
                return ap[:, 0:n].unsqueeze(1).broadcast_to([P, TILES, n])

            def over_last(ap, n):
                return ap.unsqueeze(2).broadcast_to([P, TILES, n])

            def first_largest(vals, n, top, low, hit, out):
                v.tensor_reduce(top, vals, X, ALU.max)
                v.drain()
                v.tensor_tensor(hit, vals, over_last(top, n), ALU.is_equal)
                v.drain()
                v.tensor_tensor(hit, hit, over_tiles(idxm, n), ALU.mult)
                v.drain()
                v.tensor_reduce(low, hit, X, ALU.min)
                v.drain()
                v.tensor_tensor(out, over_tiles(idxm, n), over_last(low, n), ALU.is_equal)
                v.drain()

            def experts(L):
                f = 2 * L + 1
                start_more(v, L, "marks idx_cv hid hidT y1")
                roots(f)
                v.memset(lg, 0.0)
                for b in range(2):
                    v.wait_ge(sig[f"scattered{b}"], landed(f"scattered{b}", STORES * L + 1))
                v.drain()

                def logits(T):
                    n = rows_of(T)
                    v.wait_ge(sig["saved"], happened("saved", TILES * L + T))
                    norm_tile(f, T, h_r)
                    half_T(f, T, hT_r)
                    v.wait_ge(sig["lg_mm"], happened("lg_mm", TILES * L + T + 1))
                    v.tensor_tensor(lg[0:n, cols(T, 1), :], ps[0:n, 2, 0:NG + NE].unsqueeze(1), rbias[0:n].unsqueeze(1),
                                    ALU.add).then_inc(sig["lg_ready"], 1)

                with v.Fori(0, PT) as T:
                    logits(T)
                logits(PT)
                v.drain()
                gl = lg[:, :, 0:NG]
                first_largest(gl, NG, t5[0], t5[1], tg[1], tg[2])
                v.tensor_tensor(tg[0], gl, over_last(t5[0], NG), ALU.subtract).then_inc(sig["gsub_ready"], 1)
                v.tensor_scalar(tg[2], tg[2], 1e30, -1e30, ALU.mult, ALU.add)
                v.drain()
                for T in range(TILES):
                    v.tensor_tensor(te[0][:, T].rearrange("p (g e) -> p g e", g=NG),
                                    lg[:, T, NG:].rearrange("p (g e) -> p g e", g=NG),
                                    tg[2][:, T].unsqueeze(2).broadcast_to([P, NG, EG]), ALU.add)
                v.drain()
                first_largest(te[0], NE, t5[3], t5[1], te[3], te[1])
                v.scalar_tensor_tensor(out=te[0], in0=te[1], scalar=-3e30, in1=te[0], op0=ALU.mult, op1=ALU.add)
                v.drain()
                first_largest(te[0], NE, t5[6], t5[1], te[3], te[2])
                v.tensor_tensor(t5[4], t5[6], t5[3], ALU.subtract).then_inc(sig["esub_ready"], 1)
                v.tensor_tensor(te[3], te[1], te[2], ALU.add)
                v.memset(rankm, -1.0)
                v.memset(code, 0.0)
                v.drain()
                v.tensor_tensor(te[4], te[3], over_last(valid, NE), ALU.mult)
                v.tensor_copy(code[:, 0, :, 0:NE], over_last(tokcode[:, 0], NE))
                v.tensor_tensor(code[:, 1, :, 0:NE], te[2], over_last(tokcode[:, 1], NE), ALU.add)
                v.drain().then_inc(sig["sel_ready"], 1)
                v.wait_ge(sig["gexp_ready"], happened("gexp_ready", L + 1))
                v.tensor_reduce(t5[2], tg[1], X, ALU.add)
                v.wait_ge(sig["eexp_ready"], happened("eexp_ready", L + 1))
                v.tensor_scalar(t5[7], t5[5], 1.0, None, ALU.add)
                v.drain()
                v.tensor_tensor(t5[6], t5[2], t5[7], ALU.mult)
                v.drain()
                v.reciprocal(gate1, t5[6])
                v.drain()
                v.tensor_tensor(gate2, gate1, t5[5], ALU.mult)
                v.wait_ge(sig["rank_mm"], happened("rank_mm", L + 1))
                v.scalar_tensor_tensor(out=te[3], in0=ps[:, 3, 0:TILES * NE].rearrange("p (t e) -> p t e", t=TILES),
                                       scalar=1.0, in1=te[4], op0=ALU.add, op1=ALU.mult)
                v.tensor_copy(lt[0:NE, 0:1], ps[0:NE, 4, 0:1])
                v.drain()
                v.tensor_scalar(rankm[:, :, 0:NE], te[3], -1.0, None, ALU.add)
                v.tensor_scalar(lt[0:NE, 16:16 + MORE], blkat[0:NE, :], lt[0:NE, 0:1], None, ALU.is_lt)
                v.drain()
                v.reduce_sum(lt[0:NE, 1:2], lt[0:NE, 16:16 + MORE], X)
                v.drain().then_inc(sig["nb_ready"], 1)
                v.wait_ge(sig["pre_mm"], happened("pre_mm", L + 1))
                v.tensor_copy(lt[0:NE, 2:3], ps[0:NE, 4, 8:9])
                v.drain()
                v.tensor_scalar(lt[0:NE, 3:4], lt[0:NE, 2:3], -1.0, 1.0, ALU.mult, ALU.add)
                v.tensor_tensor(lt[0:NE, 4:5], lt[0:NE, 2:3], lt[0:NE, 1:2], ALU.add)
                v.tensor_scalar(lt[0:NE, 32:32 + LIST], idx[0:NE, 0:LIST], lt[0:NE, 2:3], None, ALU.is_ge)
                v.drain()
                v.tensor_scalar(lt[0:NE, 64:64 + LIST], idx[0:NE, 0:LIST], lt[0:NE, 4:5], None, ALU.is_lt)
                v.tensor_scalar(jrep[0:NE, :], ones[0:NE, :], lt[0:NE, 3:4], None, ALU.mult)
                v.drain()
                v.tensor_tensor(lt[0:NE, 32:32 + LIST], lt[0:NE, 32:32 + LIST], lt[0:NE, 64:64 + LIST], ALU.mult)
                v.drain().then_inc(sig["list_ready"], 1)
                v.wait_ge(sig["listrow_mm"], happened("listrow_mm", L + 1))
                v.tensor_copy(lst[0:1, 0:LIST], ps[0:1, 4, 16:16 + LIST])
                v.tensor_copy(lst[0:1, 2 * NE - 1:2 * NE], ps[0:1, 4, 40:41])
                v.tensor_tensor(jstart, ps[:, 4, 64:64 + LIST], idx[:, 0:LIST], ALU.add)
                v.drain()
                v.tensor_scalar(jstart, jstart, float(BLK), None, ALU.mult)
                v.drain().then_inc(sig["lst_ready"], 1)

                def mark(q, b):
                    v.tensor_tensor(onehot[b], rankm[:, :, cols(q, 1)].broadcast_to([P, TILES, BLK]),
                                    slots.unsqueeze(1).broadcast_to([P, TILES, BLK]), ALU.is_equal
                                    ).then_inc(sig["onehot_ready"], 1)

                def numbers(q, b):
                    v.wait_ge(sig["idx_mm"], happened("idx_mm", FETCHES * L + q + 1))
                    v.tensor_scalar(store_rows[0:BLK, cols(q, 1)], ps[0:BLK, 4, 2 * b + 1:2 * b + 2], FAR, None, ALU.add)
                    v.drain()
                    v.tensor_scalar(fetch_at[b][0:BLK, :], ps[0:BLK, 4, 2 * b:2 * b + 1], FAR, None, ALU.add
                                    ).then_inc(sig["idx_ready"], 1)

                for q in range(LOOK):
                    if q >= 2:
                        v.wait_ge(sig["idx_mm"], happened("idx_mm", FETCHES * L + q - 1))
                    mark(q, q % 2)
                    if q:
                        numbers(q - 1, (q - 1) % 2)
                numbers(LOOK - 1, (LOOK - 1) % 2)
                with v.Fori(0, NE // 2) as i:
                    for b in range(2):
                        e = 2 * i + b
                        v.wait_ge(sig["idx_mm"], happened("idx_mm", FETCHES * L + e + LOOK - 1))
                        mark(e + LOOK, 1 - b)
                        v.wait_ge(sig[f"scattered{b}"], landed(f"scattered{b}", STORES * L + i + 1))
                        v.tensor_copy(store_at[b][0:BLK, :], store_rows[0:BLK, cols(e, 1)])
                        v.drain()
                        v.wait_ge(sig["silu_ready"], happened("silu_ready", NE * L + e + 1))
                        v.wait_ge(sig["ht_mm"], happened("ht_mm", NE * L + e))
                        v.tensor_tensor(hid[0:BLK, :], sg[BLK:2 * BLK, :], ps[BLK:2 * BLK, b, :], ALU.mult
                                        ).then_inc(sig["hid_ready"], 1)
                        numbers(e + LOOK, 1 - b)
                        v.wait_ge(sig["ht_mm"], happened("ht_mm", NE * L + e + 1))
                        v.wait_ge(sig["d_mm"], happened("d_mm", NE * L + e))
                        v.tensor_copy(hidT, ps[:, 6, 0:KF * BLK].rearrange("p (k t) -> p k t", k=KF)
                                      ).then_inc(sig["hidT_ready"], 1)
                        v.wait_ge(sig["d_mm"], happened("d_mm", NE * L + e + 1))
                        v.tensor_copy(ye[b][0:BLK, FF:D], ps[BLK:2 * BLK, 2 + b, :]).then_inc(sig["y1_ready"], 1)
                for b in range(2):
                    v.wait_ge(sig[f"scattered{b}"], landed(f"scattered{b}", STORES * (L + 1)))
                    v.wait_ge(sig[f"gathered{b}"], landed(f"gathered{b}", INTO[b] * (L + 1)))
                n = v.value_load(lst[0:1, 2 * NE - 1:2 * NE], min_val=0, max_val=LIST)
                with v.If(n > 0):
                    with v.Fori(0, n) as i:
                        v.wait_ge(sig["more_done"], i + 1)
                        e = v.value_load(lst[0:1, bass.ds(i, 1)], min_val=0, max_val=NE - 1)
                        v.tensor_scalar(shift, rankm[:, :, bass.ds(e, 1)].rearrange("p t a -> p (t a)"),
                                        jstart[:, bass.ds(i, 1)], None, ALU.subtract)
                        v.drain()
                        v.tensor_tensor(onehot[0], shift.unsqueeze(2).broadcast_to([P, TILES, BLK]),
                                        slots.unsqueeze(1).broadcast_to([P, TILES, BLK]), ALU.is_equal
                                        ).then_inc(sig["more_marks"], 1)
                        v.wait_ge(sig["more_idx_mm"], i + 1)
                        v.tensor_scalar(store_at[0][0:BLK, :], ps[0:BLK, 4, 1:2], FAR, None, ALU.add)
                        v.drain()
                        v.tensor_scalar(fetch_at[0][0:BLK, :], ps[0:BLK, 4, 0:1], FAR, None, ALU.add
                                        ).then_inc(sig["more_idx_cv"], 1)
                        v.wait_ge(sig["more_silu"], i + 1)
                        v.tensor_tensor(hid[0:BLK, :], sg[BLK:2 * BLK, :], ps[BLK:2 * BLK, 0, :], ALU.mult
                                        ).then_inc(sig["more_hid"], 1)
                        v.wait_ge(sig["more_ht_mm"], i + 1)
                        v.tensor_copy(hidT, ps[:, 6, 0:KF * BLK].rearrange("p (k t) -> p k t", k=KF)
                                      ).then_inc(sig["more_hidT"], 1)
                        v.wait_ge(sig["more_d_mm"], i + 2)
                        v.tensor_copy(ye[0][0:BLK, FF:D], ps[BLK:2 * BLK, 2, :]).then_inc(sig["more_y1"], 1)
                for T in range(TILES):
                    n = rows_of(T)
                    v.wait_ge(sig[f"ybuf{T % 2}"], landed(f"ybuf{T % 2}", (TILES - T % 2 + 1) // 2 * L + T // 2 + 1))
                    for part, weight in enumerate((gate1, gate2)):
                        v.scalar_tensor_tensor(out=xt(T, n), in0=ybuf[T % 2][0:n, part * D:(part + 1) * D],
                                               scalar=weight[0:n, T:T + 1], in1=xt(T, n), op0=ALU.mult, op1=ALU.add)
                        v.drain()
                    v.drain().then_inc(sig["y_added"], 1)
                v.drain().then_inc(sig["x_ready"], 1)

            experts(0)

            roots(2)
            v.wait_ge(sig["swaconst_in"], landed("swaconst_in", 4))
            v.memset(vb[:, 0:SKV * SD], 0.0)
            v.memset(kT_w, 0.0)
            v.drain()

            def window(T):
                n = rows_of(T)
                norm_tile(2, T, h_w)
                half_T(2, T, hT_w)
                v.wait_ge(sig["v_w"], happened("v_w", T))
                if n != P:
                    v.wait_ge(sig["state_out"], landed("state_out", 2))
                for c in range(3):
                    v.wait_ge(sig["qkv_mm"], happened("qkv_mm", 3 * T + c + 1))
                    v.tensor_tensor(qkv[0:n, c * FF:(c + 1) * FF], ps[0:n, 2 + c, :], bqkv[0:n, c * FF:(c + 1) * FF], ALU.add)
                v.tensor_copy(kT_w[:, :, 0:P], kT_w[:, :, P:])
                v.drain().then_inc(sig["v_ready"], 1)
                heads = SH + SKV
                src = qkv[0:n, 0:heads * SD].rearrange("p (h c r) -> p h c r", h=heads, c=2)
                dst = qkr[0:n].rearrange("p (h c r) -> p h c r", h=heads, c=2)
                t0, t1 = (t[0:n].rearrange("p (h r) -> p h r", h=heads) for t in tw)
                c, s_ = (q[0:n, cols(T * (DR // 2), DR // 2)].unsqueeze(1).broadcast_to([n, heads, DR // 2])
                         for q in (cos_tok, sin_tok))
                for out, op, one, two in ((0, ALU.subtract, 0, 1), (1, ALU.add, 1, 0)):
                    v.tensor_tensor(t0, src[:, :, one], c, ALU.mult)
                    v.tensor_tensor(t1, src[:, :, two], s_, ALU.mult)
                    v.drain()
                    v.tensor_tensor(dst[:, :, out], t0, t1, op)
                    v.drain()
                v.drain().then_inc(sig["qkr_ready"], 1)
                v.wait_ge(sig["qT_mm"], happened("qT_mm", T + 1))
                for c in range(2):
                    for half_ in range(2):
                        v.tensor_copy(kT_w[half_ * SD:(half_ + 1) * SD, c:SKV:2, P:P + n],
                                      ps[c * SD:(c + 1) * SD, 7, 0:2 * P].rearrange("p (k t) -> p k t", k=2)[:, :, 0:n])
                if n == P:
                    v.tensor_copy(qT_w[:, 4:8, 0:n], ps[:, 6, :].rearrange("p (k t) -> p k t", k=4)[:, :, 0:n])
                else:
                    v.memset(qS, 0.0)
                    v.drain()
                    for h in range(SH):
                        g, a_ = divmod(h, SG)
                        tile_, c = divmod(h, 2)
                        v.tensor_copy(qS[g % 2 * SD:(g % 2 + 1) * SD, g // 2, :, a_ * NT:(a_ + 1) * NT],
                                      ps[c * SD:(c + 1) * SD, 5 + tile_ // 4, tile_ % 4 * P:tile_ % 4 * P + NS]
                                      .rearrange("p (b t) -> p b t", b=NB))
                v.drain().then_inc(sig["qTb_w"], 1)

            def attend(T):
                def scores(u):
                    r_ = mw[u % 2]
                    sk = sinks[:, 2 * u:2 * u + 2]
                    v.wait_ge(sig["s_w_mm"], happened("s_w_mm", SUNITS * T + u + 1))
                    v.tensor_tensor(sw[u % 2], ps[:, 2 * (u % 2):2 * (u % 2) + 2, 0:2 * P],
                                    masks[:, cols(T * 2 * P, 2 * P)].unsqueeze(1).broadcast_to([P, 2, 2 * P]), ALU.add)
                    v.drain()
                    v.tensor_reduce(r_[:, 0:2], sw[u % 2], X, ALU.max)
                    v.drain()
                    v.scalar_tensor_tensor(out=r_[:, 0:2], in0=r_[:, 0:2], scalar=SWA_SCALE, in1=sk, op0=ALU.mult, op1=ALU.max)
                    v.drain()
                    v.tensor_scalar(r_[:, 2:4], r_[:, 0:2], -1.0, None, ALU.mult)
                    v.tensor_tensor(r_[:, 6:8], sk, r_[:, 0:2], ALU.subtract)
                    v.drain().then_inc(sig["s_w_ready"], 1)

                scores(0)
                for u in range(SUNITS):
                    if u + 1 < SUNITS:
                        scores(u + 1)
                    v.wait_ge(sig["pT_w_mm"], happened("pT_w_mm", SUNITS * T + u + 1))
                    v.tensor_copy(pT_w[u % 2], ps[:, 4 + u % 2, :].rearrange("p (n t) -> p n t", n=4)
                                  ).then_inc(sig["pT_w_ready"], 1)
                    v.tensor_tensor(den[:, 2 * u:2 * u + 2], mw[u % 2][:, 4:6], mw[u % 2][:, 6:8], ALU.add)
                    v.drain()
                v.reciprocal(den, den)
                v.drain()
                v.wait_ge(sig["o_w_mm"], happened("o_w_mm", SUNITS * (T + 1)))
                v.tensor_tensor(o_w.rearrange("p (h d) -> p h d", h=SH), ps[:, 6:8, :].rearrange("p n (h d) -> p (n h) d", d=SD),
                                den.unsqueeze(2).broadcast_to([P, SH, SD]), ALU.mult).then_inc(sig["o_w_ready"], 1)
                v.wait_ge(sig["oT_w_mm"], happened("oT_w_mm", T + 1))
                v.tensor_copy(oT_w[:, 4:8, :], ps[:, 1, :].rearrange("p (k t) -> p k t", k=4)).then_inc(sig["oTb_w"], 1)

            def add_out(T):
                n = rows_of(T)
                v.wait_ge(sig["wo_mm"], happened("wo_mm", TILES + T + 1))
                v.tensor_tensor(xt(T, n), xt(T, n), bo[0:n, :], ALU.add)
                v.drain()
                v.tensor_tensor(xt(T, n), xt(T, n), ps[0:n, 2:4, :].rearrange("p n c -> p (n c)"), ALU.add)
                v.drain().then_inc(sig["wo_added"], 1)

            with v.Fori(0, PT) as T:
                window(T)
                attend(T)
                add_out(T)
            window(PT)
            v.wait_ge(sig["qkv_mm"], happened("qkv_mm", 3 * TILES))
            v.memset(sink_z, 0.0)
            v.drain().then_inc(sig["sink_clear"], 1)
            for n in range(2):
                v.wait_ge(sig["kb_mm"], happened("kb_mm", 2 * n + 2))
                v.tensor_copy(kbT[:, 4 * n + 2:4 * n + 4], ps[:, 2 * n + 1, :].rearrange("p (b g c) -> p b g c", b=2, g=2)
                              ).then_inc(sig["kb_dve"], 1)
            v.wait_ge(sig["cacheb_in"], landed("cacheb_in", 3 + SKV))
            v.wait_ge(sig["sample_s_mm"], happened("sample_s_mm", 1))
            for n in range(3):
                b0, nb = 3 * n, min(3, NB - 3 * n)
                src = ps[:, 4 + n, 0:nb * (P + NS)].rearrange("p (b k) -> p b k", b=nb)
                v.scalar_tensor_tensor(out=s_z[:, b0:b0 + nb, 0:P], in0=src[:, :, 0:P], scalar=SWA_SCALE,
                                       in1=mask_z[:, 0:P].unsqueeze(1).broadcast_to([P, nb, P]), op0=ALU.mult, op1=ALU.add)
                v.scalar_tensor_tensor(out=s_z[:, b0:b0 + nb, P:], in0=src[:, :, P:], scalar=SWA_SCALE,
                                       in1=mask_z[:, P + b0 * NS:P + (b0 + nb) * NS].rearrange("p (b k) -> p b k", b=nb),
                                       op0=ALU.mult, op1=ALU.add)
            v.drain()
            v.tensor_reduce(m_z, s_z, X, ALU.max)
            v.drain()
            v.tensor_scalar(m_z, m_z, sink_z[:, 0:1], None, ALU.max)
            v.drain()
            v.tensor_tensor(s_z, s_z, m_z.unsqueeze(2).broadcast_to([P, NB, P + NS]), ALU.subtract)
            v.drain()
            v.tensor_scalar(m_z, m_z, -1.0, sink_z[:, 0:1], ALU.mult, ALU.add)
            v.drain().then_inc(sig["sample_s"], 1)
            v.wait_ge(sig["sample_e"], happened("sample_e", 1))
            v.tensor_reduce(l_z, s_z, X, ALU.add)
            v.drain()
            v.tensor_tensor(l_z, l_z, m_z, ALU.add)
            v.drain()
            v.reciprocal(l_z, l_z)
            v.drain()
            v.tensor_tensor(s_z, s_z, l_z.unsqueeze(2).broadcast_to([P, NB, P + NS]), ALU.mult)
            v.drain().then_inc(sig["sample_p"], 1)
            v.wait_ge(sig["sample_pT_mm"], happened("sample_pT_mm", 1))
            v.tensor_copy(pT_z[:, 4:8], ps[:, 5, :].rearrange("p (b r) -> p b r", b=4))
            v.tensor_copy(pTn_z[0:NS, 4:8], ps[0:NS, 7, :].rearrange("p (b r) -> p b r", b=4))
            v.drain().then_inc(sig["sample_pT_dve"], 1)
            v.wait_ge(sig["sample_o_mm"], happened("sample_o_mm", 1))
            for g in range(SKV):
                src = ps[0:SD, 0, g * P:(g + 1) * P].rearrange("p (b a c t) -> p c a b t", b=NB, a=2, c=2)
                for c in range(2):
                    for a_ in range(2):
                        v.tensor_copy(oT_w[c * SD:(c + 1) * SD, 2 * g + a_, 0:NS].rearrange("p (b t) -> p b t", b=NB),
                                      src[:, c, a_])
            v.drain().then_inc(sig["sample_o"], 1)
            add_out(PT)
            v.drain().then_inc(sig["x_ready"], 1)
            experts(1)
            roots(4)
            for T in range(TILES):
                n = rows_of(T)
                v.wait_ge(sig[f"y_out{T % 2}"], landed(f"y_out{T % 2}", T // 2))
                v.scalar_tensor_tensor(out=h_fin[T % 2][0:n, :], in0=xt(T, n), scalar=rstd[0:n, T:T + 1], in1=gain[0:n, :],
                                       op0=ALU.mult, op1=ALU.mult).then_inc(sig["y_ready"], 1)

        @block.tensor
        def _(pe):
            start_counts(pe, "tensor")

            def mm(out, lhsT, rhs, start, stop):
                return pe.matmul(out, lhsT, rhs, start=start, stop=stop)

            def flip(out, in_):
                n, at = in_.shape[0], in_.start_partition()
                return pe.transpose(out, in_, ident[at:at + n, at:at + n])

            def rows_T(f, T, h):
                n = rows_of(T)
                pe.wait_ge(sig["h_ready"], happened("h_ready", TILES * f + T + 1))
                for k in range(KD):
                    last = flip(ps[:, k // 4, (k % 4) * P:(k % 4) * P + n], h[0:n, k:D:KD])
                last.then_inc(sig["hT_mm"], 1)
                pe.wait_ge(sig["hTa"], happened("hTa", TILES * f + T + 1))
                pe.wait_ge(sig["hTb"], happened("hTb", TILES * f + T + 1))

            pe.wait_ge(sig["consts_in"], landed("consts_in", 3))
            pe.wait_ge(sig["w_a_in"], landed("w_a_in", 1))

            def project(T):
                n = rows_of(T)
                rows_T(0, T, h_m)
                pe.wait_ge(sig["rows_ready"], happened("rows_ready", T))
                for bank, c0, c1 in ((2, 0, QL), (3, QL, QL + ROW)):
                    for k in range(KD):
                        last = mm(ps[0:n, bank, 0:c1 - c0], hT_m[:, k, 0:n], w_a[:, k, c0:c1], k == 0, k == KD - 1)
                last.then_inc(sig["a_mm"], 1)
                pe.wait_ge(sig["rows_ready"], happened("rows_ready", T + 1))
                pe.wait_ge(sig["cqT_ready"], happened("cqT_ready", T))
                pe.wait_ge(sig["cT_ready"], happened("cT_ready", T))
                for k in range(3):
                    flip(ps[:, 4, k * P:k * P + n], cq[0:n, k * P:(k + 1) * P])
                for k in range(2):
                    flip(ps[:, 5, k * P:k * P + n], rowbuf[0:n, k * P:(k + 1) * P])
                flip(ps[0:DR, 5, CL:CL + n], rowbuf[0:n, CL:ROW]).then_inc(sig["rowsT_mm"], 1)

            with pe.Fori(0, PT) as T:
                project(T)
            project(PT)
            pe.wait_ge(sig["cqT_ready"], happened("cqT_ready", TILES))
            pe.wait_ge(sig["cT_ready"], happened("cT_ready", TILES))
            pe.wait_ge(sig["mlaconst_in"], landed("mlaconst_in", 6))

            with pe.Fori(0, PAIRS) as j:
                pe.wait_ge(sig["wqp_in"], landed("wqp_in", 4 * (j + 1)))
                pe.wait_ge(sig["oT_act"], happened("oT_act", 2 * PT * j))
                for part, bank in enumerate((0, 1, 3)):
                    for k in range(3):
                        mm(ps[:, bank, :], wqp[:, k, part * DN:(part + 1) * DN], cqT[:, k, 0:SEQ], k == 0, k == 2)
                    for k in range(3):
                        last = mm(ps[:, 2, part * NS:(part + 1) * NS], wqp[:, k, part * DN:(part + 1) * DN],
                                  cqT[:, k, SEQ:], k == 0, k == 2)
                last.then_inc(sig["q_mm"], 1)
                pe.wait_ge(sig["wkp_in"], landed("wkp_in", j + 1))
                for hh in range(2):
                    for k in range(2):
                        mm(ps[:, 5 + hh, :], wkp[:, k, 2 * hh * DN:(2 * hh + 1) * DN], cT[:, k, 0:SEQ], k == 0, k == 1)
                pe.wait_ge(sig["q_act"], happened("q_act", j + 1))
                pe.wait_ge(sig["q_dve"], happened("q_dve", j + 1))
                mm(ps[:, 4, :], swap, qraw[:, 0:SEQ], True, True)
                mm(ps[:, 2, P:P + NS], swap, qraw[:, SEQ:], True, True).then_inc(sig["swap_mm"], 1)
                values = wkp.rearrange("p k (h c n) -> p k h c n", h=2, c=2)
                for t in range(PT):
                    for k in range(2):
                        last = mm(ps[:, 7 if t < 2 else 1, (t % 2) * CL:(t % 2 + 1) * CL].rearrange("p (h n) -> p h n", h=2),
                                  cT[:, k, t * P:(t + 1) * P], values[:, k, :, 1, :], k == 0, k == 1)
                last.then_inc(sig["kv_mm"], 1)
                pe.wait_ge(sig["qr_ready"], happened("qr_ready", j + 1))
                pe.wait_ge(sig["kv_act"], happened("kv_act", j + 1))
                pe.wait_ge(sig["kv_dve"], happened("kv_dve", j + 1))

                def scores(q):
                    hh, qi = unit(q)
                    nk = (qi + 1) * P
                    pe.wait_ge(sig["p_ready"], happened("p_ready", 2 * PT * j + q - 1))
                    mm(ps[:, q % 2, 0:nk], qn[hh][:, qi * P:nk], kn[hh][:, 0:nk], True, False)
                    mm(ps[:, q % 2, 0:nk], qr[hh * DR:(hh + 1) * DR, qi * P:nk], krT[hh * DR:(hh + 1) * DR, 0:nk], False, False)
                    mm(ps[:, q % 2, nk - P:nk], ident, causal, False, True).then_inc(sig["s_mm"], 1)

                def out_T(q):
                    pe.wait_ge(sig["o_m_ready"], happened("o_m_ready", 2 * PT * j + q + 1))
                    pe.wait_ge(sig["oT_act"], happened("oT_act", 2 * PT * j + q - 1))
                    flip(ps[:, 6 + q % 2, 0:P], o_m[q % 2]).then_inc(sig["oT_mm"], 1)

                scores(0)
                for q in range(2 * PT):
                    hh, qi = unit(q)
                    if q + 1 < 2 * PT:
                        scores(q + 1)
                    pe.wait_ge(sig["p_ready"], happened("p_ready", 2 * PT * j + q + 1))
                    pe.wait_ge(sig["pT_m_ready"], happened("pT_m_ready", 2 * PT * j + q - 1))
                    for t in range(qi + 1):
                        last = flip(ps[:, 2 + q % 2, t * P:(t + 1) * P], p_m[q % 2][:, t * P:(t + 1) * P])
                    last.then_inc(sig["pT_mm"], 1)
                    if q:
                        out_T(q - 1)
                    pe.wait_ge(sig["pT_m_ready"], happened("pT_m_ready", 2 * PT * j + q + 1))
                    for t in range(qi + 1):
                        last = mm(ps[:, 4 + q % 2, 0:P], pT_m[q % 2][:, t, :], v_m[:, t, hh * DN:(hh + 1) * DN], t == 0, t == qi)
                    last.then_inc(sig["o_mm"], 1)
                out_T(2 * PT - 1)

            pe.wait_ge(sig["oT_act"], happened("oT_act", 2 * PT * PAIRS))
            pe.wait_ge(sig["wkvb_in"], landed("wkvb_in", 1))
            for n in range(4):
                for i in range(4):
                    hh, k = 2 * n + i // 2, i % 2
                    last = flip(ps[:, n, i * P:(i + 1) * P], wkvb[:, k, 2 * hh * DN:(2 * hh + 1) * DN])
                last.then_inc(sig["wuk_mm"], 1)
            pe.wait_ge(sig["wuk_act"], happened("wuk_act", 2))
            pe.wait_ge(sig["wuk_dve"], happened("wuk_dve", 2))
            for k in range(2):
                for hh in range(H):
                    last = mm(ps[:, 4, (k * H + hh) * NS:(k * H + hh + 1) * NS], wukT[:, hh, k, :], qnS[:, hh, :], True, True)
            last.then_inc(sig["qlat_mm"], 1)
            pe.wait_ge(sig["qlat_ready"], happened("qlat_ready", 1))
            pe.wait_ge(sig["mlaconst_in"], landed("mlaconst_in", 8))

            def sequence(b, par, i):
                page = pages[par]

                def keys_T(t):
                    for k in range(3):
                        pe.wait_ge(sig[f"kt{k}"], happened(f"kt{k}", 8 * b + t))
                        turnstile(pe)
                        w_ = DR if k == 2 else P
                        for G in range(4):
                            last = flip(ps[0:w_, 2 + k, G * P:(G + 1) * P], page[:, 8 * G + t, k * P:k * P + w_])
                        last.then_inc(sig[f"kt_mm{k}"], 1)

                def scores(t):
                    for k in range(3):
                        w_ = DR if k == 2 else P
                        pe.wait_ge(sig[f"kt{k}"], happened(f"kt{k}", 8 * b + t + 1))
                        turnstile(pe)
                        for G in range(4):
                            last = mm(ps[G * NS:(G + 1) * NS, t // 4, (t % 4) * P:(t % 4 + 1) * P], qb[par][0:w_, k, :],
                                      kT[t % 2][0:w_, k, G, :], k == 0, k == 2)
                    last.then_inc(sig["qk_mm"], 1)

                pe.wait_ge(sig[f"pages{par}"], landed(f"pages{par}", PAGES * (i + 1)))
                pe.wait_ge(sig["pTb_s"], happened("pTb_s", b))
                keys_T(0)
                pe.wait_ge(sig["qb_ready"], happened("qb_ready", b + 1))
                pe.wait_ge(sig["p_s_ready"], happened("p_s_ready", b))
                for t in range(8):
                    if t < 7:
                        keys_T(t + 1)
                    scores(t)
                pe.wait_ge(sig["olat_ready"], happened("olat_ready", b))
                for k, rhs in enumerate((cT[:, 0, SEQ:], cT[:, 1, SEQ:], krT[0:DR, SEQ:])):
                    w_ = DR if k == 2 else P
                    mm(ps[0:NS, 5, 0:NS], qb[par][0:w_, k, :], rhs, k == 0, False)
                mm(ps[0:NS, 5, 0:NS], ident[:, 0:NS], smask[:, bass.ds(b, 1), :].rearrange("p a q -> p (a q)"), False, True
                   ).then_inc(sig["new_mm"], 1)
                pe.wait_ge(sig["mx_ready"], happened("mx_ready", b + 1))
                flip(ps[0:1, 5, 64:64 + P], st[:, 0:1]).then_inc(sig["mxT_mm"], 1)
                pe.wait_ge(sig["mrow_ready"], happened("mrow_ready", b + 1))
                mm(ps[:, 5, 200:201], mrow[0:1, NS:NS + P], ones[0:1, 0:1], True, True).then_inc(sig["mb_mm"], 1)
                pe.wait_ge(sig["p_s_ready"], happened("p_s_ready", b + 1))
                for t in range(4):
                    last = flip(ps[:, 7, t * P:(t + 1) * P], p_s[:, t * P:(t + 1) * P])
                last.then_inc(sig["pT_s_mm"], 1)
                for t in range(4):
                    flip(ps[:, 4, t * P:(t + 1) * P], p_s[:, (4 + t) * P:(5 + t) * P])
                flip(ps[0:NS, 5, 224:224 + NS], pn_s[0:NS, :]).then_inc(sig["pT_s_mm"], 1)
                pe.wait_ge(sig["o_s_ready"], happened("o_s_ready", b))
                pe.wait_ge(sig["pTa_s"], happened("pTa_s", b + 1))
                for t in range(8):
                    if t == 4:
                        pe.wait_ge(sig["pTb_s"], happened("pTb_s", b + 1))
                    for G in range(4):
                        last = mm(ps[G * NS:(G + 1) * NS, 6, 0:CL], pT_s[:, t, G * NS:(G + 1) * NS], page[:, 8 * G + t, 0:CL],
                                  t == 0, t == 7 and G > 0)
                last = mm(ps[0:NS, 6, 0:CL], pTn_s[0:NS, :], rowbuf[0:NS, 0:CL], False, True)
                last.then_inc(sig["pv_mm"], 1)
                pe.wait_ge(sig["o_s_ready"], happened("o_s_ready", b + 1))
                pe.wait_ge(sig["lbc_ready"], happened("lbc_ready", b + 1))
                for k in range(2):
                    mm(ps[:, 5, 256 + k * NS:256 + (k + 1) * NS], o_s[:, k * P:(k + 1) * P], sel32, True, True)
                mm(ps[:, 5, 320:320 + NS], l_bc, sel32, True, True).then_inc(sig["oc_mm"], 1)

            with pe.Fori(0, NB // 2) as i:
                for par in range(2):
                    sequence(2 * i + par, par, i)
            pe.wait_ge(sig["olat_ready"], happened("olat_ready", NB))
            for hh in range(H):
                for k in range(2):
                    last = mm(ps[:, 0, hh * NS:(hh + 1) * NS], wkvb[:, k, (2 * hh + 1) * DN:(2 * hh + 2) * DN], olatT[:, k, hh, :],
                              k == 0, k == 1)
            last.then_inc(sig["oTs_mm"], 1)
            pe.wait_ge(sig["wo_in"], landed("wo_in", 1))
            for T in range(TILES):
                n = rows_of(T)
                if T == PT:
                    pe.wait_ge(sig["oTs_ready"], happened("oTs_ready", 1))
                pe.wait_ge(sig["wo_added"], happened("wo_added", T - 1))
                for c in range(2):
                    for k in range(H):
                        last = mm(ps[0:n, 2 + 2 * (T % 2) + c, :], oT[:, k, T * P:T * P + n], wo_m[:, k, c * FF:(c + 1) * FF],
                                  k == 0, k == H - 1)
                last.then_inc(sig["wo_mm"], 1)

            def experts(L):
                f = 2 * L + 1
                start_more(pe, L, "idx_mm xt_mm gu_mm ht_mm d_mm")
                pe.sem_inc(sig["more_d_mm"], 1)
                pe.wait_ge(sig["rw_in"], landed("rw_in", 2 * (L + 1)))
                pe.wait_ge(sig["wo_added"], happened("wo_added", TILES * (L + 1)))

                def logits(T):
                    n = rows_of(T)
                    rows_T(f, T, h_r)
                    pe.wait_ge(sig["lg_ready"], happened("lg_ready", TILES * L + T))
                    for k in range(KD):
                        last = mm(ps[0:n, 2, 0:NG + NE], hT_r[:, k, 0:n], rw[:, k, :], k == 0, k == KD - 1)
                    last.then_inc(sig["lg_mm"], 1)

                with pe.Fori(0, PT) as T:
                    logits(T)
                logits(PT)
                pe.wait_ge(sig["sel_ready"], happened("sel_ready", L + 1))
                sel = te[4]
                for T in range(TILES):
                    for U in range(T + 1):
                        mm(ps[:, 3, T * NE:(T + 1) * NE], before if U == T else ones, sel[:, U, :], U == 0, U == T)
                for T in range(TILES):
                    last = mm(ps[0:NE, 4, 0:1], sel[:, T, :], ones[:, 0:1], T == 0, T == TILES - 1)
                last.then_inc(sig["rank_mm"], 1)
                pe.wait_ge(sig["nb_ready"], happened("nb_ready", L + 1))
                mm(ps[0:NE, 4, 8:9], before[0:NE, 0:NE], lt[0:NE, 1:2], True, True).then_inc(sig["pre_mm"], 1)
                pe.wait_ge(sig["list_ready"], happened("list_ready", L + 1))
                entry = lt[0:NE, 32:32 + LIST]
                mm(ps[0:1, 4, 16:16 + LIST], epart[0:NE, :], entry, True, True)
                mm(ps[0:1, 4, 40:41], lt[0:NE, 1:2], ones[0:NE, 0:1], True, True)
                mm(ps[:, 4, 64:64 + LIST], jrep[0:NE, :], entry, True, True).then_inc(sig["listrow_mm"], 1)
                pe.wait_ge(sig["lst_ready"], happened("lst_ready", L + 1))

                def numbers(q, b):
                    pe.wait_ge(sig["onehot_ready"], happened("onehot_ready", FETCHES * L + q + 1))
                    pe.wait_ge(sig["idx_ready"], happened("idx_ready", FETCHES * L + q))
                    turnstile(pe)
                    for T in range(TILES):
                        last = mm(ps[0:BLK, 4, 2 * b:2 * b + 2], onehot[b][:, T, :],
                                  code[:, :, T, cols(q, 1)].rearrange("p c a -> p (c a)"), T == 0, T == TILES - 1)
                    last.then_inc(sig["idx_mm"], 1)

                def fetched_T(q, b, fetched):
                    pe.wait_ge(sig[f"gathered{b}"], landed(f"gathered{b}", fetched))
                    turnstile(pe)
                    pe.wait_ge(sig["xeT_ready"], happened("xeT_ready", (NE + 1) * L + q))
                    turnstile(pe)
                    for k in range(KD):
                        last = flip(ps[:, 5, k * BLK:(k + 1) * BLK], xe[b][0:BLK, k:D:KD])
                    last.then_inc(sig["xt_mm"], 1)

                even, odd = INTO[0] * L, INTO[1] * L
                numbers(0, 0)
                numbers(1, 1)
                fetched_T(0, 0, even + 1)
                numbers(2, 0)
                with pe.Fori(0, NE // 2) as i:
                    for b in range(2):
                        e = 2 * i + b
                        pe.wait_ge(sig["xeT_ready"], happened("xeT_ready", (NE + 1) * L + e + 1))
                        pe.wait_ge(sig["hid_ready"], happened("hid_ready", NE * L + e - 1))
                        turnstile(pe)
                        pe.wait_ge(sig[f"g{b}_in"], landed(f"g{b}_in", NE // 2 * L + i + 1))
                        pe.wait_ge(sig[f"u{b}_in"], landed(f"u{b}_in", NE // 2 * L + i + 1))
                        for k in range(KD):
                            for part in range(2):
                                last = mm(ps[part * BLK:(part + 1) * BLK, b, :], xeT[b][:, k, :],
                                          wgt[b][part][:, k * FF:(k + 1) * FF], k == 0, k == KD - 1)
                        last.then_inc(sig["gu_mm"], 1)
                        fetched_T(e + 1, 1 - b, (odd if b == 0 else even + 1) + i + 1)
                        numbers(e + LOOK, 1 - b)
                        pe.wait_ge(sig["hid_ready"], happened("hid_ready", NE * L + e + 1))
                        turnstile(pe)
                        pe.wait_ge(sig["hidT_ready"], happened("hidT_ready", NE * L + e))
                        turnstile(pe)
                        for k in range(KF):
                            last = flip(ps[:, 6, k * BLK:(k + 1) * BLK], hid[0:BLK, k:FF:KF])
                        last.then_inc(sig["ht_mm"], 1)
                        pe.wait_ge(sig[f"d{b}_in"], landed(f"d{b}_in", NE // 2 * L + i + 1))
                        pe.wait_ge(sig["hidT_ready"], happened("hidT_ready", NE * L + e + 1))
                        turnstile(pe)
                        pe.wait_ge(sig["y0_ready"], happened("y0_ready", NE * L + e - 1))
                        turnstile(pe)
                        pe.wait_ge(sig["y1_ready"], happened("y1_ready", NE * L + e - 1))
                        for k in range(KF):
                            for part in range(2):
                                last = mm(ps[part * BLK:(part + 1) * BLK, 2 + b, :], hidT[:, k, :],
                                          wgt[b][2][:, k * D + part * FF:k * D + (part + 1) * FF], k == 0, k == KF - 1)
                        last.then_inc(sig["d_mm"], 1)
                pe.wait_ge(sig["xeT_ready"], happened("xeT_ready", (NE + 1) * (L + 1)))
                pe.wait_ge(sig["idx_ready"], happened("idx_ready", FETCHES * (L + 1)))
                pe.wait_ge(sig["y0_ready"], happened("y0_ready", NE * (L + 1)))
                pe.wait_ge(sig["y1_ready"], happened("y1_ready", NE * (L + 1)))
                n = pe.value_load(lst[0:1, 2 * NE - 1:2 * NE], min_val=0, max_val=LIST)
                with pe.If(n > 0):
                    with pe.Fori(0, n) as i:
                        e = pe.value_load(lst[0:1, bass.ds(i, 1)], min_val=0, max_val=NE - 1)
                        pe.wait_ge(sig["more_marks"], i + 1)
                        turnstile(pe)
                        for T in range(TILES):
                            last = mm(ps[0:BLK, 4, 0:2], onehot[0][:, T, :],
                                      code[:, :, T, bass.ds(e, 1)].rearrange("p c a -> p (c a)"), T == 0, T == TILES - 1)
                        last.then_inc(sig["more_idx_mm"], 1)
                        pe.wait_ge(sig[f"more_gather{L}"], (i + 1) * DMA)
                        turnstile(pe)
                        for k in range(KD):
                            last = flip(ps[:, 5, k * BLK:(k + 1) * BLK], xe[0][0:BLK, k:D:KD])
                        last.then_inc(sig["more_xt_mm"], 1)
                        pe.wait_ge(sig["more_xeT"], i + 1)
                        turnstile(pe)
                        pe.wait_ge(sig["more_weights"], (i + 1) * 3 * DMA)
                        turnstile(pe)
                        for k in range(KD):
                            for part in range(2):
                                last = mm(ps[part * BLK:(part + 1) * BLK, 0, :], xeT[0][:, k, :],
                                          wgt[0][part][:, k * FF:(k + 1) * FF], k == 0, k == KD - 1)
                        last.then_inc(sig["more_gu_mm"], 1)
                        pe.wait_ge(sig["more_hid"], i + 1)
                        turnstile(pe)
                        for k in range(KF):
                            last = flip(ps[:, 6, k * BLK:(k + 1) * BLK], hid[0:BLK, k:FF:KF])
                        last.then_inc(sig["more_ht_mm"], 1)
                        pe.wait_ge(sig["more_hidT"], i + 1)
                        turnstile(pe)
                        for k in range(KF):
                            for part in range(2):
                                last = mm(ps[part * BLK:(part + 1) * BLK, 2, :], hidT[:, k, :],
                                          wgt[0][2][:, k * D + part * FF:k * D + (part + 1) * FF], k == 0, k == KF - 1)
                        last.then_inc(sig["more_d_mm"], 1)

            experts(0)

            pe.wait_ge(sig["wqkv_in"], landed("wqkv_in", 1))

            def window(T):
                n = rows_of(T)
                rows_T(2, T, h_w)
                for c in range(3):
                    for k in range(KD):
                        last = mm(ps[0:n, 2 + c, :], hT_w[:, k, 0:n], wqkv[:, k, c * FF:(c + 1) * FF], k == 0, k == KD - 1)
                    last.then_inc(sig["qkv_mm"], 1)
                pe.wait_ge(sig["qkr_ready"], happened("qkr_ready", T + 1))
                for k in range(2):
                    flip(ps[:, 7, k * P:k * P + n], qkr[0:n, SH * SD + k * P:SH * SD + (k + 1) * P])
                for u in range(SUNITS):
                    last = flip(ps[:, 5 + u // 4, u % 4 * P:u % 4 * P + n], qkr[0:n, u * P:(u + 1) * P])
                last.then_inc(sig["qT_mm"], 1)
                if n == P:
                    pe.wait_ge(sig["qTa_w"], happened("qTa_w", T + 1))
                pe.wait_ge(sig["qTb_w"], happened("qTb_w", T + 1))

            def attend(T):
                pe.wait_ge(sig["v_w"], happened("v_w", T + 1))

                def scores(u):
                    if u >= 2:
                        pe.wait_ge(sig["s_w_ready"], happened("s_w_ready", SUNITS * T + u - 1))
                    for c in range(2):
                        last = mm(ps[:, 2 * (u % 2) + c, 0:2 * P], qT_w[c * SD:(c + 1) * SD, u, :],
                                  kT_w[c * SD:(c + 1) * SD, u // 2, :], True, True)
                    last.then_inc(sig["s_w_mm"], 1)

                scores(0)
                for u in range(SUNITS):
                    if u + 1 < SUNITS:
                        scores(u + 1)
                    pe.wait_ge(sig["p_w"], happened("p_w", SUNITS * T + u + 1))
                    pe.wait_ge(sig["pT_w_ready"], happened("pT_w_ready", SUNITS * T + u - 1))
                    for n in range(4):
                        last = flip(ps[:, 4 + u % 2, n * P:(n + 1) * P], sw[u % 2][:, n // 2, (n % 2) * P:(n % 2 + 1) * P])
                    last.then_inc(sig["pT_w_mm"], 1)
                    pe.wait_ge(sig["pT_w_ready"], happened("pT_w_ready", SUNITS * T + u + 1))
                    for c in range(2):
                        at = (u % 4 * 2 + c) * SD
                        for past in range(2):
                            last = mm(ps[:, 6 + u // 4, at:at + SD], pT_w[u % 2][:, 2 * c + past, :],
                                      vb[:, cols((T + past) * SKV * SD + u // 2 * SD, SD)], past == 0, past == 1)
                    last.then_inc(sig["o_w_mm"], 1)
                pe.wait_ge(sig["o_w_ready"], happened("o_w_ready", T + 1))
                for k in range(KD):
                    last = flip(ps[:, k // 4, (k % 4) * P:(k % 4 + 1) * P], o_w[:, k * P:(k + 1) * P])
                last.then_inc(sig["oT_w_mm"], 1)
                pe.wait_ge(sig["oTa_w"], happened("oTa_w", T + 1))
                pe.wait_ge(sig["oTb_w"], happened("oTb_w", T + 1))

            def project_out(T):
                n = rows_of(T)
                pe.wait_ge(sig["wo_w_in"], landed("wo_w_in", 1))
                for c in range(2):
                    for k in range(KD):
                        last = mm(ps[0:n, 2 + c, :], oT_w[:, k, 0:n], wo_w[:, k, c * FF:(c + 1) * FF], k == 0, k == KD - 1)
                last.then_inc(sig["wo_mm"], 1)
                pe.wait_ge(sig["wo_added"], happened("wo_added", TILES + T + 1))

            with pe.Fori(0, PT) as T:
                window(T)
                attend(T)
                project_out(T)
            window(PT)
            pe.wait_ge(sig["v_w"], happened("v_w", TILES))
            pe.wait_ge(sig["cacheb_in"], landed("cacheb_in", 3 + SKV))
            for n in range(4):
                for i in range(4):
                    last = flip(ps[:, n, i * P:(i + 1) * P], kbuf[:, 2 * n + i // 2, (i % 2) * P:(i % 2 + 1) * P])
                last.then_inc(sig["kb_mm"], 1)
            pe.wait_ge(sig["kb_act"], happened("kb_act", 2))
            pe.wait_ge(sig["kb_dve"], happened("kb_dve", 2))
            for b in range(NB):
                at = (b % 3) * (P + NS)
                for g in range(SKV):
                    G, c = divmod(g, 2)
                    rows = slice(c * SD, (c + 1) * SD)
                    mm(ps[g * NS:(g + 1) * NS, 4 + b // 3, at:at + P], qS[rows, G, b, :], kbT[rows, b, G, :], True, True)
                    last = mm(ps[g * NS:(g + 1) * NS, 4 + b // 3, at + P:at + P + NS], qS[rows, G, b, :],
                              kT_w[rows, g, P:P + NS], True, True)
            last.then_inc(sig["sample_s_mm"], 1)
            pe.wait_ge(sig["sample_p"], happened("sample_p", 1))
            for b in range(NB):
                flip(ps[:, 4 + b // 4, (b % 4) * P:(b % 4 + 1) * P], s_z[:, b, 0:P])
                last = flip(ps[0:NS, 6 + b // 4, (b % 4) * P:(b % 4 + 1) * P], s_z[:, b, P:])
            last.then_inc(sig["sample_pT_mm"], 1)
            pe.wait_ge(sig["sample_pT_act"], happened("sample_pT_act", 2))
            pe.wait_ge(sig["sample_pT_dve"], happened("sample_pT_dve", 1))
            for g in range(SKV):
                for b in range(NB):
                    at = (g * NB + b) * SG * NT
                    rows = slice(g * NS, g * NS + SG * NT)
                    mm(ps[0:SD, 0, at:at + SG * NT], vbuf[:, b, g * SD:(g + 1) * SD], pT_z[:, b, rows], True, False)
                    last = mm(ps[0:SD, 0, at:at + SG * NT], vb[0:NS, TILES * SKV * SD + g * SD:TILES * SKV * SD + (g + 1) * SD],
                              pTn_z[0:NS, b, rows], False, True)
            last.then_inc(sig["sample_o_mm"], 1)
            pe.wait_ge(sig["sample_o"], happened("sample_o", 1))
            project_out(PT)
            experts(1)


_INS = ["x_prompt", "x_sample", "cache_mla", "cache_swa_kv", "page_table", "norm_mix", "norm_ffn", "norm_final",
        "mla_w_a", "mla_q_norm", "mla_wq_b", "mla_kv_norm", "mla_wkv_b", "mla_wo", "swa_wqkv", "swa_bqkv",
        "swa_sinks", "swa_wo", "swa_bo", "moe_w_group", "moe_b_group", "moe_w_expert", "moe_b_expert",
        "moe_w_gate", "moe_w_up", "moe_w_down"]
_OUTS = [("y_prompt", (1, SEQ, D)), ("y_sample", (NB, NT, D)), ("mla_rows_prompt", (1, 1, SEQ, ROW)),
         ("mla_rows_sample", (1, NB, NT, ROW)), ("swa_kv_prompt", (1, 1, WIN, 2, SKV, SD)),
         ("swa_kv_sample", (1, NB, WIN, 2, SKV, SD))]


def shape_constants(np):
    f = np.float32
    r = np.arange(P)
    tok = np.arange(TILES)[None, :] * P + r[:, None]
    pos = np.where(tok < SEQ, tok, 4096 + (tok - SEQ) % NT)
    inv = (10000.0 ** (-np.arange(DR // 2) / (DR // 2))).astype(f)
    ang = pos[:, :, None].astype(f) * inv[None, None, :]
    cos, sin = np.cos(ang).astype(f), np.sin(ang).astype(f)
    col = lambda v: np.broadcast_to(np.asarray(v, f), (P, len(v)))
    packed = np.concatenate([
        np.eye(P, dtype=f), (r[:, None] < r[None, :]).astype(f), np.ones((P, P), f), col(np.arange(BLK)),
        col(np.arange(NE)), col(np.arange(NE) - 1024), col(BLK * np.arange(1, MORE + 1)), r[:, None].astype(f),
        (tok - FAR).astype(f), (2 * tok - FAR).astype(f), (tok < TOK).astype(f)], axis=1)
    at = np.arange(TOK)
    cosT = cos.transpose(2, 1, 0).reshape(DR // 2, -1)[:, at]
    sinT = sin.transpose(2, 1, 0).reshape(DR // 2, -1)[:, at]
    swap = np.zeros((P, P), f)
    for h0 in (0, DR):
        for i in range(DR // 2):
            swap[h0 + DR // 2 + i, h0 + i] = -1.0
            swap[h0 + i, h0 + DR // 2 + i] = 1.0
    allowed = lambda ok: np.where(ok, f(0.0), f(NEG)).astype(f)
    q, k = r[:, None], np.arange(2 * P)[None, :]
    dist = P + q - k
    masks = np.concatenate([allowed((dist >= 0) & (dist < WIN) & (T * P - P + k >= 0)) for T in range(PT)], axis=1)
    row_t = (np.arange(P) % NT)[:, None, None]
    b, key = np.arange(NB)[None, :, None], np.arange(NS)[None, None, :]
    new = allowed((key // NT == b) & (key % NT <= row_t))
    past = allowed(np.arange(P)[None, :] > (np.arange(P) % NT)[:, None])
    return {
        "c_consts": packed, "c_cos_tok": cos.reshape(P, -1), "c_sin_tok": sin.reshape(P, -1),
        "c_causal": allowed(r[None, :] <= r[:, None]), "c_swap": swap,
        "c_cosT": np.tile(cosT, (P // (DR // 2), 1)), "c_sinT": np.tile(sinT, (P // (DR // 2), 1)),
        "c_smask": new, "c_sel32": (r[:, None] % NS == np.arange(NS)[None, :]).astype(f),
        "c_masks": masks, "c_mask_z": np.concatenate([past, new.reshape(P, -1)], axis=1),
    }


def kernel(**inputs):
    import numpy as np
    import concourse.bacc as bacc
    from concourse.bass_utils import run_bass_kernel_spmd

    nc = bacc.Bacc("TRN2", target_bir_lowering=False, num_devices=1)
    arrays = {name: np.ascontiguousarray(inputs[name]) for name in _INS}
    arrays |= {name: np.ascontiguousarray(v) for name, v in shape_constants(np).items()}
    a = {name: nc.dram_tensor(f"in_{name}", v.shape, mybir.dt.from_np(v.dtype), kind="ExternalInput").ap()
         for name, v in arrays.items()}
    o = {name: nc.dram_tensor(f"out_{name}", shape, F32, kind="ExternalOutput").ap() for name, shape in _OUTS}
    build(nc, a, o)
    r = run_bass_kernel_spmd(nc, [{f"in_{name}": v for name, v in arrays.items()}], core_ids=[0])
    return tuple(r.results[0][f"out_{name}"] for name, _ in _OUTS)
```

```python
from contextlib import ExitStack

import concourse.bass as bass
from concourse import mybir

F32 = mybir.dt.float32
I32 = mybir.dt.int32
U32 = mybir.dt.uint32
ALU = mybir.AluOpType
ACT = mybir.ActivationFunctionType
X = mybir.AxisListType.X

P = 128
D = 1024
KD = D // P
SEQ, NB, NT = 512, 8, 4
NS = NB * NT
PT = SEQ // P
TILES = PT + 1
TOK = SEQ + NS
QL, CL, DR = 384, 256, 64
ROW = CL + DR
H, DN = 8, 128
PAIRS = H // 2
PAGES = 32
PHYS = 320
MLA_SCALE = 1.0 / (DN + DR) ** 0.5
UNITS = H * PT
SH, SKV, SD = 16, 4, 64
SG = SH // SKV
SUNITS = SH // 2
WIN = 128
SWA_SCALE = 1.0 / SD ** 0.5
QKV = (SH + 2 * SKV) * SD
NE, NG, EG = 32, 4, 8
FF = 512
KF = FF // P
BLK = 64
MORE = (TOK + BLK - 1) // BLK - 1
LIST = 2 * TOK // BLK + 1
FAR = 4096.0
EPS = 1e-6
NEG = -1e30
AHEAD = 2
LOOK = 3
FETCHES = NE + LOOK
INTO = ((FETCHES + 1) // 2, FETCHES // 2)
SAVES = ((TILES + 1) // 2, TILES // 2)
STORES = NE // 2 + 1
DMA = 16

EVENTS = {
    "pool": "moe_done",
    "vector": """x_pad x_ready meansq h_ready hTb a_ms rows_ready cT_ready q_dve kv_dve qr_ready
        nm_ready pT_m_ready o_m_ready wuk_dve qlat_ready qb_ready kt1 mx_ready mrow_ready nms_ready
        lbc_ready pTb_s olat_ready oTs_ready wo_added lg_ready gsub_ready esub_ready sel_ready nb_ready
        list_ready lst_ready onehot_ready idx_ready hid_ready hidT_ready y1_ready y_added""",
    "scalar": """sumsq_ready root_ready hTa a_sq a_root cqT_ready q_act kv_act p_ready oT_act
        wuk_act kt0 kt2 p_s_ready pTa_s o_s_ready gexp_ready eexp_ready silu_ready y0_ready xeT_ready""",
    "tensor": """hT_mm a_mm rowsT_mm q_mm swap_mm kv_mm s_mm pT_mm o_mm oT_mm wuk_mm qlat_mm kt_mm0
        kt_mm1 kt_mm2 qk_mm new_mm mxT_mm mb_mm pT_s_mm pv_mm oc_mm oTs_mm wo_mm lg_mm rank_mm pre_mm
        listrow_mm idx_mm gu_mm ht_mm d_mm xt_mm
        sample_s_mm sample_pT_mm sample_o_mm""",
}
LATER = {
    "v_ready": ("q_dve", PAIRS),
    "qkr_ready": ("kv_dve", PAIRS),
    "qTb_w": ("qr_ready", PAIRS),
    "s_w_ready": ("nm_ready", UNITS),
    "pT_w_ready": ("pT_m_ready", UNITS),
    "o_w_ready": ("o_m_ready", UNITS),
    "oTb_w": ("cT_ready", TILES),
    "sink_clear": ("wuk_dve", 2),
    "kb_dve": ("qb_ready", NB),
    "sample_s": ("mx_ready", NB),
    "sample_p": ("mrow_ready", NB),
    "sample_pT_dve": ("nms_ready", NB),
    "sample_o": ("lbc_ready", NB),
    "y_ready": ("pTb_s", NB),
    "v_w": ("q_act", PAIRS),
    "qTa_w": ("kv_act", PAIRS),
    "p_w": ("p_ready", UNITS),
    "oTa_w": ("oT_act", UNITS),
    "kb_act": ("wuk_act", 2),
    "sample_e": ("p_s_ready", NB),
    "sample_pT_act": ("pTa_s", NB),
    "qkv_mm": ("q_mm", PAIRS),
    "qT_mm": ("swap_mm", PAIRS),
    "s_w_mm": ("s_mm", UNITS),
    "pT_w_mm": ("pT_mm", UNITS),
    "o_w_mm": ("o_mm", UNITS),
    "oT_w_mm": ("oT_mm", UNITS),
    "kb_mm": ("wuk_mm", 4),
}
TRANSFERS = {
    "pool": """gain_in consts_in xn_out0 xn_out1 gathered0 gathered1 scattered0 scattered1 late_pages0 late_pages1
        mlaconst_in swaconst_in""",
    "sync": """x_first_in x_in w_a_in w_a_late_in wqp_in wkp_in pages0 pages1 wkvb_in wo_in rows_out g0_in g1_in u0_in u1_in
        d0_in d1_in wqkv_in wo_w_in y_out0 y_out1 state_out windows_out cacheb_in ptab_in rw_in ybuf0 ybuf1""",
}
POOLS = TRANSFERS["pool"].split()
MORE_EVENTS = """more_marks more_idx_mm more_idx_cv more_xt_mm more_xeT more_gu_mm more_silu more_hid more_ht_mm
    more_hidT more_d_mm more_y0 more_y1 more_done"""
MORE_TRANSFERS = "more_weights more_gather0 more_gather1 more_scatter0 more_scatter1"



def cols(start, size):
    return slice(start, start + size) if isinstance(start, int) else bass.ds(start, size)


def rows_of(T):
    return NS if isinstance(T, int) and T == PT else P


class Arena:

    def __init__(self, mem, start, end):
        self.mem, self.at, self.end = mem, start, end

    def take(self, *shape, dt=F32):
        n = 1
        for size in shape:
            n *= size
        v = self.mem[:, self.at:self.at + n]
        self.at += n
        assert self.at <= self.end, (self.at, self.end)
        if dt is not F32:
            v = v.bitcast(dt)
        if len(shape) == 2:
            v = v.rearrange("p (a b) -> p a b", a=shape[0])
        elif len(shape) == 3:
            v = v.rearrange("p (a b c) -> p a b c", a=shape[0], b=shape[1])
        elif len(shape) == 4:
            v = v.rearrange("p (a b c d) -> p a b c d", a=shape[0], b=shape[1], c=shape[2])
        return v


def build(nc, a, o):
    with ExitStack() as ctx:
        WORDS = 53120
        mem = ctx.enter_context(nc.sbuf_tensor("mem", [P, WORDS], F32))
        ps = ctx.enter_context(nc.psum_tensor("ps", [P, 8, 512], F32))
        sig = {}
        for names in (*EVENTS.values(), *TRANSFERS.values()):
            for name in names.split():
                sig[name] = ctx.enter_context(nc.semaphore(name))
        for name in (MORE_EVENTS + " " + MORE_TRANSFERS).split():
            sig[name] = ctx.enter_context(nc.semaphore(name))
        sig["passed"] = ctx.enter_context(nc.semaphore("passed"))
        for name, (base, _) in LATER.items():
            sig[name] = sig[base]

        def happened(name, k):
            return k + AHEAD + (LATER[name][1] if name in LATER else 0)

        def landed(name, k):
            return (k if name in POOLS else k + AHEAD) * DMA

        def turnstile(eng):
            eng.sem_inc(sig["passed"], 1)

        def start_more(eng, L, names):
            if L:
                for name in names.split():
                    eng.sem_clear(sig["more_" + name])

        def start_counts(eng, which):
            for name in EVENTS.get(which, "").split():
                eng.sem_inc(sig[name], AHEAD)
            for name in TRANSFERS["sync"].split() if which == "sync" else ():
                eng.sem_inc(sig[name], AHEAD * DMA)

        keep = Arena(mem, 0, WORDS)
        x = keep.take(TILES * D)
        ident = keep.take(P)
        before = keep.take(P)
        ones = keep.take(P)
        slots = keep.take(BLK)
        idx = keep.take(NE)
        idxm = keep.take(NE)
        blkat = keep.take(MORE)
        epart = keep.take(1)
        tokcode = keep.take(2, TILES)
        valid = keep.take(TILES)
        consts = mem[:, TILES * D:keep.at]
        cos_tok = keep.take(TILES * DR // 2)
        sin_tok = keep.take(TILES * DR // 2)
        gain = keep.take(D)
        sumsq = keep.take(8)
        rstd = keep.take(8)
        gate1 = keep.take(TILES)
        gate2 = keep.take(TILES)
        rest = keep.at
        slot_at = [rest, rest + 3 * KD * FF]
        wgt = [[mem[:, at + n * KD * FF:at + (n + 1) * KD * FF] for n in range(3)] for at in slot_at]
        work = rest + 6 * KD * FF
        wqkv = mem[:, WORDS - KD * QKV:WORDS].rearrange("p (k n) -> p k n", k=KD)
        moe_end = WORDS - KD * QKV

        m = Arena(mem, rest, WORDS)
        pages = [m.take(PAGES, ROW) for _ in range(2)]
        over = Arena(mem, rest, rest + PAGES * ROW)
        w_a = over.take(KD, QL + ROW)
        hT_m = over.take(KD, P)
        h_m = over.take(D)
        over = Arena(mem, rest, rest + PAGES * ROW)
        wo_m = over.take(KD, D)
        cqT = m.take(3, TOK)
        cT = m.take(2, TOK)
        krT = m.take(TOK)
        oT = m.take(H, TOK)
        rowbuf = m.take(ROW)
        cq = m.take(QL)
        qgain = m.take(QL)
        kvgain = m.take(CL)
        rt = m.take(4, DR // 2)
        cqjunk = m.take(QL)
        ams = m.take(4)
        qnS = m.take(H, NS)
        qrS = m.take(PAIRS, NS)
        causal = m.take(P)
        swap = m.take(P)
        ptab = m.take(NB * PAGES, dt=I32)
        cosT = m.take(TOK)
        sinT = m.take(TOK)
        pair_from = m.at
        wqp = m.take(3, 2 * (DN + DR))
        wkp = m.take(2, 4 * DN)
        qn = [m.take(SEQ) for _ in range(2)]
        qr = m.take(TOK)
        qraw = m.take(TOK)
        qsw = m.take(TOK)
        kn = [m.take(SEQ) for _ in range(2)]
        v_m = m.take(PT, 2 * DN)
        p_m = [m.take(SEQ) for _ in range(2)]
        pT_m = [m.take(PT, P) for _ in range(2)]
        o_m = [m.take(P) for _ in range(2)]
        soft = [m.take(4) for _ in range(2)]
        s = Arena(mem, pair_from, WORDS)
        wukT = s.take(H, 2, P)
        kT = [s.take(3, 4, P) for _ in range(2)]
        pT_s = s.take(8, P)
        p_s = s.take(8 * P)
        pn_s = s.take(NS)
        pTn_s = s.take(NS)
        o_s = s.take(CL)
        l_bc = s.take(P)
        mrow = s.take(NS + P)
        qlat = s.take(2, NB, NS)
        qrope = s.take(NB, NS)
        qb = [s.take(3, NS) for _ in range(2)]
        olatT = s.take(2, H, NS)
        smask = s.take(NB, NS)
        sel32 = s.take(NS)
        st = s.take(8)
        linv = s.take(NS)
        assert m.at <= s.at
        wkvb = s.take(2, 2 * H * DN)

        r = Arena(mem, work, moe_end)
        rankm = r.take(TILES, FETCHES)
        code = r.take(2, TILES, FETCHES)
        jstart = r.take(LIST)
        lst = r.take(2 * NE, dt=I32)
        shift = r.take(TILES)
        onehot = [r.take(TILES, BLK) for _ in range(2)]
        fetch_at = [r.take(1, dt=I32) for _ in range(2)]
        store_at = [r.take(1, dt=I32) for _ in range(2)]
        store_rows = r.take(FETCHES, dt=I32)
        sg = r.take(FF)
        hid = r.take(FF)
        hidT = r.take(KF, BLK)
        xeT_both = r.take(2 * KD * BLK)
        xeT = [xeT_both[:, n * KD * BLK:(n + 1) * KD * BLK].rearrange("p (k t) -> p k t", k=KD) for n in range(2)]
        moe_at = r.at
        xe = [r.take(D) for _ in range(2)]
        ye = [r.take(D) for _ in range(2)]
        lt = r.take(96)
        jrep = r.take(P)
        router = Arena(mem, moe_at, moe_end)
        h_r = [mem[:, moe_end + T * D:moe_end + (T + 1) * D] for T in range(TILES)]
        hT_r = [router.take(KD, P), xeT_both.rearrange("p (k t) -> p k t", k=KD)]
        rw = router.take(KD, NG + NE)
        rbias = router.take(NG + NE)
        lg = router.take(TILES, NG + NE)
        t5 = [router.take(TILES) for _ in range(8)]
        tg = [router.take(TILES, NG) for _ in range(3)]
        te = [router.take(TILES, NE) for _ in range(5)]
        pages_flat = [mem[:, rest + n * PAGES * ROW:rest + (n + 1) * PAGES * ROW] for n in range(2)]
        h_fin = xe
        ybuf = [mem[:, slot_at[0] + n * 2 * D:slot_at[0] + (n + 1) * 2 * D] for n in range(TILES)]

        w = Arena(mem, rest, moe_end)
        wo_w = w.take(KD, D)
        h_w = w.take(D)
        hT_w = w.take(KD, P)
        qkv = w.take(QKV)
        half = (SH + SKV) * SD // 2
        tw = [w.take(half) for _ in range(2)]
        qkr = w.take((SH + SKV) * SD)
        qT_w = w.take(SUNITS, P)
        kT_w = w.take(SKV, 2 * P)
        vb = w.take((TILES + 1) * SKV * SD)
        bqkv = w.take(QKV)
        bo = w.take(D)
        sinks = w.take(SH)
        masks = w.take(PT * 2 * P)
        sw = [w.take(2, 2 * P) for _ in range(2)]
        pT_w = [w.take(4, P) for _ in range(2)]
        den = w.take(SH)
        mw = [w.take(8) for _ in range(2)]
        o_w = w.take(D)
        oT_w = w.take(KD, P)
        z = Arena(mem, moe_end, WORDS)
        kbuf = z.take(NB, SKV * SD)
        vbuf = z.take(NB, SKV * SD)
        kbT = z.take(NB, 2, P)
        qS = z.take(2, NB, NS)
        s_z = z.take(NB, P + NS)
        mask_z = z.take(P + NB * NS)
        sink_z = z.take(1)
        m_z = z.take(NB)
        l_z = z.take(NB)
        pT_z = z.take(NB, P)
        pTn_z = z.take(NB, P)

        rows_in = nc.dram_tensor("moe_rows_in", (TOK, D), F32, kind="Internal").ap()
        rows_back = nc.dram_tensor("moe_rows_back", (2 * TOK, D), F32, kind="Internal").ap()

        block = ctx.enter_context(nc.Block())

        def xt(T, n=P, c0=0, c1=D):
            return x[0:n, cols(T * D + c0, c1 - c0)]

        def unit(q):
            return divmod(q, PT)

        @block.sync
        def _(sp):
            start_counts(sp, "sync")
            sp.dma_start(xt(0), a["x_prompt"][0, 0:P, :]).then_inc(sig["x_first_in"], DMA)
            w_a_src = a["mla_w_a"][0].rearrange("(p k) n -> p k n", k=KD)
            sp.dma_start(w_a[:, 0:KD // 2], w_a_src[:, 0:KD // 2]).then_inc(sig["w_a_in"], DMA)
            sp.dma_start(w_a[:, KD // 2:], w_a_src[:, KD // 2:]).then_inc(sig["w_a_late_in"], DMA)
            sp.dma_start(x[:, D:PT * D].rearrange("p (t d) -> p t d", t=PT - 1),
                         a["x_prompt"][0, P:].rearrange("(t p) d -> p t d", p=P)).then_inc(sig["x_in"], DMA)
            sp.wait_ge(sig["x_pad"], happened("x_pad", 1))
            sp.dma_start(xt(PT, NS), a["x_sample"].rearrange("b t d -> (b t) d")).then_inc(sig["x_in"], DMA)
            sp.dma_start(ptab[0:1, :], a["page_table"].rearrange("b n -> (b n)").unsqueeze(0)
                         ).then_inc(sig["ptab_in"], DMA)
            wq = a["mla_wq_b"][0].rearrange("(k p) n -> p k n", p=P)
            wkv = a["mla_wkv_b"][0].rearrange("(k p) n -> p k n", p=P)

            def rows_out(T):
                sp.wait_ge(sig["rows_ready"], happened("rows_ready", T + 1))
                n = rows_of(T)
                dst = (o["mla_rows_sample"][0].rearrange("b t c -> (b t) c") if n == NS
                       else o["mla_rows_prompt"][0, 0][cols(T * P, P), :])
                sp.dma_start(dst, rowbuf[0:n, :]).then_inc(sig["rows_out"], DMA)

            def load_pages(b, par):
                with sp.Fori(0, PAGES // 2) as j:
                    page = sp.value_load(ptab[0:1, bass.ds(b * PAGES + j, 1)], min_val=0, max_val=PHYS - 1)
                    sp.dma_start(pages_flat[par][:, bass.ds(j * ROW, ROW)],
                                 a["cache_mla"][0][bass.ds(page, 1)].rearrange("a p c -> p (a c)")
                                 ).then_inc(sig[f"pages{par}"], DMA)

            def load_pair(j):
                sp.wait_ge(sig["q_mm"], happened("q_mm", j))
                for hh in range(2):
                    head = (2 * j + hh) * (DN + DR)
                    sp.dma_start(wqp[:, :, hh * DN:(hh + 1) * DN], wq[:, :, cols(head, DN)]).then_inc(sig["wqp_in"], DMA)
                    sp.dma_start(wqp[:, :, 2 * DN + hh * DR:2 * DN + (hh + 1) * DR], wq[:, :, cols(head + DN, DR)]
                                 ).then_inc(sig["wqp_in"], DMA)
                sp.wait_ge(sig["kv_mm"], happened("kv_mm", j))
                sp.dma_start(wkp, wkv[:, :, cols(j * 4 * DN, 4 * DN)]).then_inc(sig["wkp_in"], DMA)

            with sp.Fori(0, PT) as T:
                rows_out(T)
            rows_out(PT)
            load_pair(0)
            with sp.Fori(1, PAIRS) as j:
                load_pair(j)
            sp.dma_start(wkvb, wkv).then_inc(sig["wkvb_in"], DMA)
            sp.wait_ge(sig["ptab_in"], landed("ptab_in", 1))
            with sp.Fori(1, NB // 2) as i:
                for par in range(2):
                    sp.wait_ge(sig["pv_mm"], happened("pv_mm", 2 * i + par - 1))
                    turnstile(sp)
                    load_pages(2 * i + par, par)
            sp.wait_ge(sig["pv_mm"], happened("pv_mm", NB - 1))
            sp.dma_start(wo_m, a["mla_wo"][0].rearrange("(k p) n -> p k n", p=P)).then_inc(sig["wo_in"], DMA)

            def experts(L):
                sp.wait_ge(sig["wo_mm"], happened("wo_mm", (L + 1) * TILES))
                sp.wait_ge(sig["sumsq_ready"], happened("sumsq_ready", 2 * L + 3))
                start_more(sp, L, "weights")
                sp.dma_start(rw[:, :, 0:NG], a["moe_w_group"][L].rearrange("(p k) n -> p k n", k=KD)
                             ).then_inc(sig["rw_in"], DMA)
                sp.dma_start(rw[:, :, NG:], a["moe_w_expert"][L].rearrange("(p k) n -> p k n", k=KD)
                             ).then_inc(sig["rw_in"], DMA)
                with sp.Fori(0, NE // 2) as i:
                    for par in range(2):
                        e = 2 * i + par
                        if par:
                            sp.wait_ge(sig["lg_mm"], happened("lg_mm", TILES * (L + 1)))
                        sp.wait_ge(sig["gu_mm"], happened("gu_mm", NE * L + e - 1))
                        for n, kind in enumerate(("gate", "up")):
                            sp.dma_start(wgt[par][n], a[f"moe_w_{kind}"][L][bass.ds(e, 1)]
                                         .rearrange("a (p k) f -> p (a k f)", k=KD)
                                         ).then_inc(sig[f"{kind[0]}{par}_in"], DMA)
                        sp.wait_ge(sig["d_mm"], happened("d_mm", NE * L + e - 1))
                        sp.dma_start(wgt[par][2], a["moe_w_down"][L][bass.ds(e, 1)]
                                     .rearrange("a (p k) n -> p (a k n)", k=KF)
                                     ).then_inc(sig[f"d{par}_in"], DMA)
                    if L == 0:
                        for b in range(2):
                            sp.wait_ge(sig[f"xn_out{b}"], landed(f"xn_out{b}", SAVES[b]))
                        piece = KD * QKV // NE
                        sp.dma_start(wqkv.rearrange("p k n -> p (k n)")[:, cols(i * piece, piece)],
                                     a["swa_wqkv"][0].rearrange("(p k) n -> p (k n)", k=KD)[:, cols(i * piece, piece)]
                                     ).then_inc(sig["wqkv_in"], DMA)
                if L == 0:
                    half_ = KD * QKV // 2
                    sp.dma_start(wqkv.rearrange("p k n -> p (k n)")[:, half_:],
                                 a["swa_wqkv"][0].rearrange("(p k) n -> p (k n)", k=KD)[:, half_:]
                                 ).then_inc(sig["wqkv_in"], DMA)
                sp.wait_ge(sig["d_mm"], happened("d_mm", NE * (L + 1)))
                n = sp.value_load(lst[0:1, 2 * NE - 1:2 * NE], min_val=0, max_val=LIST)
                with sp.If(n > 0):
                    with sp.Fori(0, n) as i:
                        sp.wait_ge(sig["more_d_mm"], i + 1)
                        e = sp.value_load(lst[0:1, bass.ds(i, 1)], min_val=0, max_val=NE - 1)
                        for n_, kind in enumerate(("gate", "up", "down")):
                            sp.dma_start(wgt[0][n_], a[f"moe_w_{kind}"][L][bass.ds(e, 1)]
                                         .rearrange("a (p k) f -> p (a k f)", k=KF if kind == "down" else KD)
                                         ).then_inc(sig["more_weights"], DMA)
                sp.wait_ge(sig["moe_done"], happened("moe_done", L + 1))
                for T in range(TILES):
                    if T >= 2:
                        sp.wait_ge(sig[f"ybuf{T % 2}"], landed(f"ybuf{T % 2}", SAVES[T % 2] * L + T // 2))
                    n = rows_of(T)
                    sp.dma_start(ybuf[T][0:n, :],
                                 rows_back[2 * T * P:2 * T * P + 2 * n, :].rearrange("(p c) d -> p (c d)", c=2)
                                 ).then_inc(sig[f"ybuf{T % 2}"], DMA)

            experts(0)
            sp.wait_ge(sig["h_ready"], happened("h_ready", TILES * 2 + 1))
            sp.dma_start(wo_w, a["swa_wo"][0].rearrange("(k p) n -> p k n", p=P)).then_inc(sig["wo_w_in"], DMA)
            sp.wait_ge(sig["qkr_ready"], happened("qkr_ready", PT))
            sp.dma_start(o["swa_kv_prompt"][0, 0, :, 0].rearrange("p h d -> p (h d)"), qkr[:, SH * SD:]
                         ).then_inc(sig["state_out"], DMA)
            sp.dma_start(o["swa_kv_prompt"][0, 0, :, 1].rearrange("p h d -> p (h d)"), qkv[:, (SH + SKV) * SD:]
                         ).then_inc(sig["state_out"], DMA)
            cache = a["cache_swa_kv"][0].rearrange("b w s h d -> b w (s h d)")
            out_s = o["swa_kv_sample"][0].rearrange("b w s h d -> b w (s h d)")
            sp.dma_start(out_s[:, 0:P - NT, :], cache[:, NT:P, :]).then_inc(sig["windows_out"], DMA)
            sp.wait_ge(sig["qkv_mm"], happened("qkv_mm", 3 * TILES))
            kv = a["cache_swa_kv"][0].rearrange("b w s h d -> w s b (h d)")
            sp.dma_start(kbuf, kv[:, 0]).then_inc(sig["cacheb_in"], DMA)
            sp.dma_start(vbuf, kv[:, 1]).then_inc(sig["cacheb_in"], DMA)
            sp.dma_start(mask_z, a["c_mask_z"]).then_inc(sig["cacheb_in"], DMA)
            sp.wait_ge(sig["sink_clear"], happened("sink_clear", 1))
            for g in range(SKV):
                sp.dma_start(sink_z[32 * g:32 * g + SG * NT, :],
                             a["swa_sinks"][0][g * SG:(g + 1) * SG].unsqueeze(1).broadcast_to([SG, NT])
                             ).then_inc(sig["cacheb_in"], DMA)
            sp.wait_ge(sig["qkr_ready"], happened("qkr_ready", TILES))
            for b in range(NB):
                for part, src in ((0, qkr[:, SH * SD:]), (1, qkv[:, (SH + SKV) * SD:])):
                    sp.dma_start(out_s[b, P - NT:P, part * SKV * SD:(part + 1) * SKV * SD],
                                 src[b * NT:(b + 1) * NT, :]).then_inc(sig["windows_out"], DMA)
            sp.wait_ge(sig["windows_out"], landed("windows_out", 1 + 2 * NB))
            experts(1)
            for T in range(TILES):
                sp.wait_ge(sig["y_ready"], happened("y_ready", T + 1))
                n = rows_of(T)
                dst = o["y_prompt"][0][T * P:(T + 1) * P, :] if T < PT else o["y_sample"].rearrange("b t d -> (b t) d")
                sp.dma_start(dst, h_fin[T % 2][0:n, :]).then_inc(sig[f"y_out{T % 2}"], DMA)
            sp.wait_ge(sig["rows_out"], landed("rows_out", TILES))
            sp.wait_ge(sig["state_out"], landed("state_out", 2))
            sp.wait_ge(sig["y_out0"], landed("y_out0", 3))
            sp.wait_ge(sig["y_out1"], landed("y_out1", 2))

        @block.gpsimd
        def _(g):
            start_counts(g, "pool")

            def row(ap, n=P):
                return ap.unsqueeze(0).broadcast_to([n, ap.shape[0]])

            g.dma_start(gain, row(a["norm_mix"][0])).then_inc(sig["gain_in"], DMA)
            g.dma_start(consts, a["c_consts"]).then_inc(sig["consts_in"], DMA)

            for dst, src in ((qgain, row(a["mla_q_norm"][0])), (kvgain, row(a["mla_kv_norm"][0])),
                             (cos_tok, a["c_cos_tok"]), (sin_tok, a["c_sin_tok"]), (causal, a["c_causal"]), (swap, a["c_swap"]), (cosT, a["c_cosT"]), (sinT, a["c_sinT"])):
                g.dma_start(dst, src).then_inc(sig["mlaconst_in"], DMA)

            def load_pages(b, par, first):
                with g.Fori(first, PAGES) as j:
                    page = g.value_load(ptab[0:1, bass.ds(b * PAGES + j, 1)], min_val=0, max_val=PHYS - 1)
                    g.dma_start(pages_flat[par][:, bass.ds(j * ROW, ROW)],
                                a["cache_mla"][0][bass.ds(page, 1)].rearrange("a p c -> p (a c)")
                                ).then_inc(sig[f"late_pages{par}"], DMA)

            g.wait_ge(sig["a_mm"], happened("a_mm", TILES))
            g.wait_ge(sig["ptab_in"], landed("ptab_in", 1))
            load_pages(0, 0, 0)
            load_pages(1, 1, 0)
            g.wait_ge(sig["oT_act"], happened("oT_act", 2 * PAIRS * PT))
            g.dma_start(smask, a["c_smask"]).then_inc(sig["mlaconst_in"], DMA)
            g.dma_start(sel32, a["c_sel32"]).then_inc(sig["mlaconst_in"], DMA)
            with g.Fori(1, NB // 2) as i:
                for par in range(2):
                    g.wait_ge(sig["pv_mm"], happened("pv_mm", 2 * i + par - 1))
                    turnstile(g)
                    load_pages(2 * i + par, par, PAGES // 2)

            def experts(L):
                start_more(g, L, "done")
                g.sem_inc(sig["more_done"], 1)
                g.wait_ge(sig["h_ready"], happened("h_ready", TILES * (2 * L + 1)))
                g.dma_start(gain, row(a["norm_ffn"][L])).then_inc(sig["gain_in"], DMA)
                g.wait_ge(sig["wo_mm"], happened("wo_mm", (L + 1) * TILES))
                g.wait_ge(sig["sumsq_ready"], happened("sumsq_ready", 2 * L + 3))
                g.dma_start(rbias[:, 0:NG], row(a["moe_b_group"][L])).then_inc(sig["scattered0"], DMA)
                g.dma_start(rbias[:, NG:], row(a["moe_b_expert"][L])).then_inc(sig["scattered1"], DMA)

                for T in range(TILES):
                    g.wait_ge(sig["h_ready"], happened("h_ready", TILES * (2 * L + 1) + T + 1))
                    n = rows_of(T)
                    g.dma_start(rows_in[T * P:T * P + n, :], h_r[T][0:n, :]).then_inc(sig[f"xn_out{T % 2}"], DMA)
                g.wait_ge(sig["h_ready"], happened("h_ready", TILES * (2 * L + 2)))
                g.dma_start(gain, row(a["norm_mix"][1] if L == 0 else a["norm_final"])).then_inc(sig["gain_in"], DMA)
                g.wait_ge(sig["onehot_ready"], happened("onehot_ready", FETCHES * L + 1))
                for b in range(2):
                    g.wait_ge(sig[f"xn_out{b}"], landed(f"xn_out{b}", SAVES[b] * (L + 1)))
                for b in range(2):
                    g.memset(xe[b], 0.0)
                g.drain()

                def fetch(q, b):
                    g.wait_ge(sig["idx_ready"], happened("idx_ready", FETCHES * L + q + 1))
                    turnstile(g)
                    g.wait_ge(sig["xt_mm"], happened("xt_mm", (NE + 1) * L + q - 1))
                    turnstile(g)
                    g.indirect_dma_start(out=xe[b][0:BLK, :], out_offset=None, in_=rows_in,
                                         in_offset=bass.IndirectOffsetOnAxis(ap=fetch_at[b][0:BLK, 0:1].bitcast(U32), axis=0),
                                         bounds_check=TOK - 1, oob_is_err=False).then_inc(sig[f"gathered{b}"], DMA)

                def store(e, b):
                    g.wait_ge(sig["y0_ready"], happened("y0_ready", NE * L + e + 1))
                    turnstile(g)
                    g.wait_ge(sig["y1_ready"], happened("y1_ready", NE * L + e + 1))
                    turnstile(g)
                    g.indirect_dma_start(out=rows_back, out_offset=bass.IndirectOffsetOnAxis(ap=store_at[b][0:BLK, 0:1].bitcast(U32), axis=0),
                                         in_=ye[b][0:BLK, :], in_offset=None,
                                         bounds_check=2 * TOK - 1, oob_is_err=False).then_inc(sig[f"scattered{b}"], DMA)

                for q in range(LOOK):
                    fetch(q, q % 2)
                with g.Fori(0, NE // 2) as i:
                    for b in range(2):
                        fetch(2 * i + b + LOOK, 1 - b)
                        store(2 * i + b, b)
                for b in range(2):
                    g.wait_ge(sig[f"gathered{b}"], landed(f"gathered{b}", INTO[b] * (L + 1)))
                    g.wait_ge(sig[f"scattered{b}"], landed(f"scattered{b}", STORES * (L + 1)))
                n = g.value_load(lst[0:1, 2 * NE - 1:2 * NE], min_val=0, max_val=LIST)
                with g.If(n > 0):
                    with g.Fori(0, n) as i:
                        g.wait_ge(sig["more_idx_cv"], i + 1)
                        turnstile(g)
                        g.indirect_dma_start(out=xe[0][0:BLK, :], out_offset=None, in_=rows_in,
                                             in_offset=bass.IndirectOffsetOnAxis(ap=fetch_at[0][0:BLK, 0:1].bitcast(U32), axis=0),
                                             bounds_check=TOK - 1, oob_is_err=False).then_inc(sig[f"more_gather{L}"], DMA)
                        g.wait_ge(sig["more_y0"], i + 1)
                        turnstile(g)
                        g.wait_ge(sig["more_y1"], i + 1)
                        turnstile(g)
                        g.indirect_dma_start(out=rows_back, out_offset=bass.IndirectOffsetOnAxis(ap=store_at[0][0:BLK, 0:1].bitcast(U32), axis=0),
                                             in_=ye[0][0:BLK, :], in_offset=None,
                                             bounds_check=2 * TOK - 1, oob_is_err=False).then_inc(sig[f"more_scatter{L}"], DMA)
                        g.wait_ge(sig[f"more_scatter{L}"], (i + 1) * DMA)
                        turnstile(g)
                        g.sem_inc(sig["more_done"], 1)
                g.sem_inc(sig["moe_done"], 1)

            experts(0)
            g.wait_ge(sig["x_ready"], happened("x_ready", 2))
            for dst, src in ((bqkv, row(a["swa_bqkv"][0])), (bo, row(a["swa_bo"][0])),
                             (sinks, row(a["swa_sinks"][0])), (masks, a["c_masks"])):
                g.dma_start(dst, src).then_inc(sig["swaconst_in"], DMA)
            experts(1)

        @block.scalar
        def _(act):
            start_counts(act, "scalar")

            def copy(out, in_):
                return act.activation(out, in_, ACT.Copy)

            def sums(f, junk, tiles):
                for T in tiles:
                    if f == 0 and T == 0:
                        act.wait_ge(sig["x_first_in"], landed("x_first_in", 1))
                    elif f == 0:
                        act.wait_ge(sig["x_in"], landed("x_in", 2))
                    elif f % 2:
                        act.wait_ge(sig["wo_added"], happened("wo_added", TILES * (f // 2) + T + 1))
                    else:
                        act.wait_ge(sig["y_added"], happened("y_added", TILES * (f // 2 - 1) + T + 1))
                    act.drain()
                    act.activation(junk, xt(T), ACT.Square, accum_out=sumsq[:, T:T + 1])

            def root(stage, T0, T1):
                act.drain().then_inc(sig["sumsq_ready"], 1)
                act.wait_ge(sig["meansq"], happened("meansq", stage + 1))
                act.activation(rstd[:, T0:T1], sumsq[:, T0:T1], ACT.Sqrt).then_inc(sig["root_ready"], 1)

            def half_T(f, T, hT, bank=0):
                n = rows_of(T)
                act.wait_ge(sig["hT_mm"], happened("hT_mm", TILES * f + T + 1))
                copy(hT[:, 0:4, 0:n], ps[:, bank, :].rearrange("p (k t) -> p k t", k=4)[:, :, 0:n]
                     ).then_inc(sig["hTa"], 1)

            def latent(T):
                n = rows_of(T)
                A = 2 + 4 * (T % 2)
                act.wait_ge(sig["a_mm"], happened("a_mm", T + 1))
                act.activation(cqjunk[0:n, :], ps[0:n, A, 0:QL], ACT.Square, accum_out=ams[0:n, 0:1])
                act.drain()
                act.activation(cqjunk[0:n, 0:CL], ps[0:n, A + 1, 0:CL], ACT.Square, accum_out=ams[0:n, 1:2])
                act.drain().then_inc(sig["a_sq"], 1)
                act.wait_ge(sig["a_ms"], happened("a_ms", T + 1))
                act.activation(ams[0:n, 2:4], ams[0:n, 0:2], ACT.Sqrt).then_inc(sig["a_root"], 1)

            def latent_T(T):
                n = rows_of(T)
                act.wait_ge(sig["rowsT_mm"], happened("rowsT_mm", T + 1))
                copy(cqT[:, :, cols(T * P, n)], ps[:, 4, 0:QL].rearrange("p (k t) -> p k t", k=3)[:, :, 0:n]
                     ).then_inc(sig["cqT_ready"], 1)

            junk = v_m.rearrange("p t n -> p (t n)")
            sums(0, junk, range(1))
            root(0, 0, 1)
            half_T(0, 0, hT_m)
            sums(0, junk, range(1, TILES))
            root(1, 1, TILES)
            for T in range(TILES):
                if T + 1 < TILES:
                    half_T(0, T + 1, hT_m)
                if T:
                    latent_T(T - 1)
                latent(T)
            latent_T(PT)

            with act.Fori(0, PAIRS) as j:
                act.wait_ge(sig["q_mm"], happened("q_mm", j + 1))
                copy(qn[0][:, 0:SEQ], ps[:, 0, :])
                copy(qraw[:, 0:SEQ], ps[:, 3, :])
                act.drain().then_inc(sig["q_act"], 1)
                act.wait_ge(sig["kv_mm"], happened("kv_mm", j + 1))
                copy(kn[0], ps[:, 5, :])
                copy(v_m[:, 0:2, :], ps[:, 7, :].rearrange("p (t n) -> p t n", t=2))
                act.drain().then_inc(sig["kv_act"], 1)

                def finish(q):
                    hh, qi = unit(q)
                    act.wait_ge(sig["oT_mm"], happened("oT_mm", 2 * PT * j + q + 1))
                    copy(oT[:, bass.ds(2 * j + hh, 1), qi * P:(qi + 1) * P], ps[:, 6 + q % 2, 0:P].unsqueeze(1)
                         ).then_inc(sig["oT_act"], 1)

                for q in range(2 * PT):
                    hh, qi = unit(q)
                    nk = (qi + 1) * P
                    act.wait_ge(sig["nm_ready"], happened("nm_ready", 2 * PT * j + q + 1))
                    act.wait_ge(sig["pT_mm"], happened("pT_mm", 2 * PT * j + q - 1))
                    act.activation(p_m[q % 2][:, 0:nk], ps[:, q % 2, 0:nk], ACT.Exp, bias=soft[q % 2][:, 1:2],
                                   scale=MLA_SCALE, accum_out=soft[q % 2][:, 2:3])
                    act.drain().then_inc(sig["p_ready"], 1)
                    if q >= 2:
                        finish(q - 2)
                finish(2 * PT - 2)
                finish(2 * PT - 1)

            for n in range(0, 4, 2):
                act.wait_ge(sig["wuk_mm"], happened("wuk_mm", n + 1))
                copy(wukT[:, 2 * n:2 * n + 2], ps[:, n, :].rearrange("p (h k c) -> p h k c", h=2, k=2)
                     ).then_inc(sig["wuk_act"], 1)

            def sequence(b, par):
                for t in range(8):
                    step = 8 * b + t
                    act.wait_ge(sig["qk_mm"], happened("qk_mm", step - 1))
                    act.wait_ge(sig["kt_mm0"], happened("kt_mm0", step + 1))
                    copy(kT[t % 2][:, 0], ps[:, 2, :].rearrange("p (g c) -> p g c", g=4)).then_inc(sig["kt0"], 1)
                    act.wait_ge(sig["kt_mm2"], happened("kt_mm2", step + 1))
                    copy(kT[t % 2][0:DR, 2], ps[0:DR, 4, :].rearrange("p (g c) -> p g c", g=4)).then_inc(sig["kt2"], 1)
                act.wait_ge(sig["nms_ready"], happened("nms_ready", b + 1))
                act.activation(p_s.rearrange("p (n c) -> p n c", n=2), ps[:, 0:2, :], ACT.Exp, bias=st[:, 2:3],
                               scale=MLA_SCALE, accum_out=st[:, 3:4])
                act.activation(pn_s[0:NS, :], ps[0:NS, 5, 0:NS], ACT.Exp, bias=st[0:NS, 2:3],
                               scale=MLA_SCALE, accum_out=st[0:NS, 4:5])
                act.drain().then_inc(sig["p_s_ready"], 1)
                act.wait_ge(sig["pT_s_mm"], happened("pT_s_mm", 2 * b + 1))
                copy(pT_s[:, 0:4], ps[:, 7, :].rearrange("p (n c) -> p n c", n=4)).then_inc(sig["pTa_s"], 1)
                act.wait_ge(sig["pv_mm"], happened("pv_mm", b + 1))
                copy(o_s, ps[:, 6, 0:CL]).then_inc(sig["o_s_ready"], 1)

            with act.Fori(0, NB // 2) as i:
                for par in range(2):
                    sequence(2 * i + par, par)

            def experts(L):
                f = 2 * L + 1
                start_more(act, L, "xeT silu y0")
                sums(f, o_w if L else p_s, range(PT, TILES) if L else range(TILES))
                root(f + 1, 0, TILES)
                for T in range(TILES):
                    half_T(f, T, hT_r[T % 2], 5 * (T % 2))
                act.wait_ge(sig["gsub_ready"], happened("gsub_ready", L + 1))
                act.activation(tg[1], tg[0], ACT.Exp).then_inc(sig["gexp_ready"], 1)
                act.wait_ge(sig["esub_ready"], happened("esub_ready", L + 1))
                act.activation(t5[5], t5[4], ACT.Exp).then_inc(sig["eexp_ready"], 1)

                def rows_T(q, b):
                    act.wait_ge(sig["xt_mm"], happened("xt_mm", (NE + 1) * L + q + 1))
                    copy(xeT[b], ps[:, 5, :].rearrange("p (k t) -> p k t", k=KD)).then_inc(sig["xeT_ready"], 1)

                rows_T(0, 0)
                with act.Fori(0, NE // 2) as i:
                    for b in range(2):
                        e = 2 * i + b
                        act.wait_ge(sig["gu_mm"], happened("gu_mm", NE * L + e + 1))
                        act.wait_ge(sig["hid_ready"], happened("hid_ready", NE * L + e))
                        act.activation(sg[BLK:2 * BLK, :], ps[0:BLK, b, :], ACT.Silu).then_inc(sig["silu_ready"], 1)
                        rows_T(e + 1, 1 - b)
                        act.wait_ge(sig["d_mm"], happened("d_mm", NE * L + e + 1))
                        act.wait_ge(sig[f"scattered{b}"], landed(f"scattered{b}", STORES * L + i + 1))
                        copy(ye[b][0:BLK, 0:FF], ps[0:BLK, 2 + b, :]).then_inc(sig["y0_ready"], 1)
                act.wait_ge(sig["lst_ready"], happened("lst_ready", L + 1))
                n = act.value_load(lst[0:1, 2 * NE - 1:2 * NE], min_val=0, max_val=LIST)
                with act.If(n > 0):
                    with act.Fori(0, n) as i:
                        act.wait_ge(sig["more_xt_mm"], i + 1)
                        copy(xeT[0], ps[:, 5, :].rearrange("p (k t) -> p k t", k=KD)).then_inc(sig["more_xeT"], 1)
                        act.wait_ge(sig["more_gu_mm"], i + 1)
                        act.activation(sg[BLK:2 * BLK, :], ps[0:BLK, 0, :], ACT.Silu).then_inc(sig["more_silu"], 1)
                        act.wait_ge(sig["more_d_mm"], i + 2)
                        copy(ye[0][0:BLK, 0:FF], ps[0:BLK, 2, :]).then_inc(sig["more_y0"], 1)

            experts(0)

            sums(2, ye[0], range(TILES))
            root(3, 0, TILES)

            def window(T):
                n = rows_of(T)
                half_T(2, T, hT_w)
                act.wait_ge(sig["v_ready"], happened("v_ready", T + 1))
                copy(vb[0:n, cols((T + 1) * SKV * SD, SKV * SD)], qkv[0:n, (SH + SKV) * SD:]).then_inc(sig["v_w"], 1)

            def queries_T(T):
                n = rows_of(T)
                act.wait_ge(sig["qT_mm"], happened("qT_mm", T + 1))
                if n == P:
                    copy(qT_w[:, 0:4, 0:n], ps[:, 5, :].rearrange("p (k t) -> p k t", k=4)[:, :, 0:n]
                         ).then_inc(sig["qTa_w"], 1)

            def attend(T):
                for u in range(SUNITS):
                    act.wait_ge(sig["s_w_ready"], happened("s_w_ready", SUNITS * T + u + 1))
                    for c in range(2):
                        act.activation(sw[u % 2][:, c], sw[u % 2][:, c], ACT.Exp, bias=mw[u % 2][:, 2 + c:3 + c],
                                       scale=SWA_SCALE, accum_out=mw[u % 2][:, 4 + c:5 + c])
                    act.activation(mw[u % 2][:, 6:8], mw[u % 2][:, 6:8], ACT.Exp)
                    act.drain().then_inc(sig["p_w"], 1)

            def out_T(T):
                n = rows_of(T)
                act.wait_ge(sig["oT_w_mm"], happened("oT_w_mm", T + 1))
                copy(oT_w[:, 0:4, 0:n], ps[:, 0, :].rearrange("p (k t) -> p k t", k=4)[:, :, 0:n]
                     ).then_inc(sig["oTa_w"], 1)

            def tile(T):
                queries_T(T)
                attend(T)
                out_T(T)
                window(T + 1)

            window(0)
            with act.Fori(0, PT - 1) as T:
                tile(T)
            tile(PT - 1)
            sums(3, o_w, range(PT))
            for n in range(2):
                act.wait_ge(sig["kb_mm"], happened("kb_mm", 2 * n + 1))
                copy(kbT[:, 4 * n:4 * n + 2], ps[:, 2 * n, :].rearrange("p (b g c) -> p b g c", b=2, g=2)
                     ).then_inc(sig["kb_act"], 1)
            act.wait_ge(sig["sample_s"], happened("sample_s", 1))
            act.activation(s_z, s_z, ACT.Exp)
            act.activation(m_z, m_z, ACT.Exp)
            act.drain().then_inc(sig["sample_e"], 1)
            act.wait_ge(sig["sample_pT_mm"], happened("sample_pT_mm", 1))
            copy(pT_z[:, 0:4], ps[:, 4, :].rearrange("p (b r) -> p b r", b=4)).then_inc(sig["sample_pT_act"], 1)
            copy(pTn_z[0:NS, 0:4], ps[0:NS, 6, :].rearrange("p (b r) -> p b r", b=4)).then_inc(sig["sample_pT_act"], 1)
            experts(1)
            sums(4, ye[0], range(TILES))
            root(5, 0, TILES)

        @block.vector
        def _(v):
            start_counts(v, "vector")
            v.memset(xt(PT), 0.0)
            v.drain().then_inc(sig["x_pad"], 1)

            def roots(stage, T0, T1):
                v.wait_ge(sig["sumsq_ready"], happened("sumsq_ready", stage + 1))
                v.tensor_scalar(sumsq[:, T0:T1], sumsq[:, T0:T1], 1.0 / D, EPS, ALU.mult, ALU.add
                                ).then_inc(sig["meansq"], 1)
                v.wait_ge(sig["root_ready"], happened("root_ready", stage + 1))
                v.reciprocal(rstd[:, T0:T1], rstd[:, T0:T1])
                v.drain()

            def norm_tile(f, T, h, buffers=1):
                n = rows_of(T)
                v.wait_ge(sig["hT_mm"], happened("hT_mm", TILES * f + T + 1 - buffers))
                v.scalar_tensor_tensor(out=h[0:n, :], in0=xt(T, n), scalar=rstd[0:n, cols(T, 1)], in1=gain[0:n, :],
                                       op0=ALU.mult, op1=ALU.mult).then_inc(sig["h_ready"], 1)

            def half_T(f, T, hT, bank=1):
                n = rows_of(T)
                v.wait_ge(sig["hT_mm"], happened("hT_mm", TILES * f + T + 1))
                v.tensor_copy(hT[:, 4:8, 0:n], ps[:, bank, :].rearrange("p (k t) -> p k t", k=4)[:, :, 0:n]
                              ).then_inc(sig["hTb"], 1)

            v.wait_ge(sig["gain_in"], landed("gain_in", 1))

            def latent(T):
                n = rows_of(T)
                A = 2 + 4 * (T % 2)
                v.wait_ge(sig["a_sq"], happened("a_sq", T + 1))
                v.tensor_scalar(ams[0:n, 0:1], ams[0:n, 0:1], 1.0 / QL, EPS, ALU.mult, ALU.add)
                v.tensor_scalar(ams[0:n, 1:2], ams[0:n, 1:2], 1.0 / CL, EPS, ALU.mult, ALU.add)
                v.drain().then_inc(sig["a_ms"], 1)
                v.wait_ge(sig["a_root"], happened("a_root", T + 1))
                v.reciprocal(ams[0:n, 2:4], ams[0:n, 2:4])
                v.drain()
                v.wait_ge(sig["rows_out"], landed("rows_out", T))
                v.scalar_tensor_tensor(out=cq[0:n, :], in0=ps[0:n, A, 0:QL], scalar=ams[0:n, 2:3], in1=qgain[0:n, :],
                                       op0=ALU.mult, op1=ALU.mult)
                v.scalar_tensor_tensor(out=rowbuf[0:n, 0:CL], in0=ps[0:n, A + 1, 0:CL], scalar=ams[0:n, 3:4],
                                       in1=kvgain[0:n, :], op0=ALU.mult, op1=ALU.mult)
                c, s_ = (q[0:n, cols(T * DR // 2 if isinstance(T, int) else T * (DR // 2), DR // 2)] for q in (cos_tok, sin_tok))
                k1, k2 = ps[0:n, A + 1, CL:CL + DR // 2], ps[0:n, A + 1, CL + DR // 2:ROW]
                for dst, k, t in ((0, k1, c), (1, k2, s_), (2, k2, c), (3, k1, s_)):
                    v.tensor_tensor(rt[0:n, dst], k, t, ALU.mult)
                v.drain()
                v.tensor_tensor(rowbuf[0:n, CL:CL + DR // 2], rt[0:n, 0], rt[0:n, 1], ALU.subtract)
                v.tensor_tensor(rowbuf[0:n, CL + DR // 2:ROW], rt[0:n, 2], rt[0:n, 3], ALU.add)
                v.drain().then_inc(sig["rows_ready"], 1)

            def latent_T(T):
                n = rows_of(T)
                v.wait_ge(sig["rowsT_mm"], happened("rowsT_mm", T + 1))
                v.tensor_copy(cT[:, :, cols(T * P, n)], ps[:, 5, 0:CL].rearrange("p (k t) -> p k t", k=2)[:, :, 0:n])
                for half_ in range(2):
                    v.tensor_copy(krT[half_ * DR:(half_ + 1) * DR, cols(T * P, n)], ps[0:DR, 5, CL:CL + n])
                v.drain().then_inc(sig["cT_ready"], 1)

            roots(0, 0, 1)
            norm_tile(0, 0, h_m)
            half_T(0, 0, hT_m)
            roots(1, 1, TILES)
            norm_tile(0, 1, h_m)
            v.wait_ge(sig["consts_in"], landed("consts_in", 1))
            v.wait_ge(sig["mlaconst_in"], landed("mlaconst_in", 8))
            for T in range(TILES):
                if T + 1 < TILES:
                    half_T(0, T + 1, hT_m)
                if T:
                    latent_T(T - 1)
                if T + 2 < TILES:
                    norm_tile(0, T + 2, h_m)
                latent(T)
            latent_T(PT)

            with v.Fori(0, PAIRS) as j:
                v.wait_ge(sig["q_mm"], happened("q_mm", j + 1))
                v.tensor_copy(qn[1], ps[:, 1, :])
                v.tensor_copy(qnS[:, bass.ds(2 * j, 2), :], ps[:, 2, 0:2 * NS].rearrange("p (h t) -> p h t", h=2))
                v.tensor_copy(qraw[:, SEQ:], ps[:, 2, 2 * NS:3 * NS])
                v.drain().then_inc(sig["q_dve"], 1)
                v.wait_ge(sig["swap_mm"], happened("swap_mm", j + 1))
                v.tensor_tensor(qsw[:, 0:SEQ], ps[:, 4, :], sinT[:, 0:SEQ], ALU.mult)
                v.tensor_tensor(qsw[:, SEQ:], ps[:, 2, P:P + NS], sinT[:, SEQ:], ALU.mult)
                v.tensor_tensor(qraw, qraw, cosT, ALU.mult)
                v.drain()
                v.tensor_tensor(qr, qraw, qsw, ALU.add)
                v.drain()
                v.tensor_copy(qrS[:, bass.ds(j, 1), :], qr[:, SEQ:].unsqueeze(1))
                v.drain().then_inc(sig["qr_ready"], 1)
                v.wait_ge(sig["kv_mm"], happened("kv_mm", j + 1))
                v.tensor_copy(kn[1], ps[:, 6, :])
                v.tensor_copy(v_m[:, 2:4, :], ps[:, 1, :].rearrange("p (t n) -> p t n", t=2))
                v.drain().then_inc(sig["kv_dve"], 1)

                def largest(q):
                    hh, qi = unit(q)
                    v.wait_ge(sig["s_mm"], happened("s_mm", 2 * PT * j + q + 1))
                    v.reduce_max(soft[q % 2][:, 0:1], ps[:, q % 2, 0:(qi + 1) * P], X)
                    v.drain()
                    v.tensor_scalar(soft[q % 2][:, 1:2], soft[q % 2][:, 0:1], -MLA_SCALE, None, ALU.mult
                                    ).then_inc(sig["nm_ready"], 1)

                def out(q):
                    v.wait_ge(sig["o_mm"], happened("o_mm", 2 * PT * j + q + 1))
                    v.wait_ge(sig["oT_mm"], happened("oT_mm", 2 * PT * j + q - 1))
                    v.tensor_scalar(o_m[q % 2], ps[:, 4 + q % 2, 0:P], soft[q % 2][:, 3:4], None, ALU.mult
                                    ).then_inc(sig["o_m_ready"], 1)

                largest(0)
                for q in range(2 * PT):
                    hh, qi = unit(q)
                    if q + 1 < 2 * PT:
                        largest(q + 1)
                    v.wait_ge(sig["pT_mm"], happened("pT_mm", 2 * PT * j + q + 1))
                    v.tensor_copy(pT_m[q % 2][:, 0:qi + 1, :],
                                  ps[:, 2 + q % 2, 0:(qi + 1) * P].rearrange("p (t n) -> p t n", t=qi + 1)
                                  ).then_inc(sig["pT_m_ready"], 1)
                    v.drain()
                    v.reciprocal(soft[q % 2][:, 3:4], soft[q % 2][:, 2:3])
                    v.drain()
                    if q:
                        out(q - 1)
                out(2 * PT - 1)

            for n in range(1, 4, 2):
                v.wait_ge(sig["wuk_mm"], happened("wuk_mm", n + 1))
                v.tensor_copy(wukT[:, 2 * n:2 * n + 2], ps[:, n, :].rearrange("p (h k c) -> p h k c", h=2, k=2)
                              ).then_inc(sig["wuk_dve"], 1)
            v.wait_ge(sig["qlat_mm"], happened("qlat_mm", 1))
            for k in range(2):
                v.tensor_copy(qlat[:, k].rearrange("p b (h t) -> p b h t", h=H),
                              ps[:, 4, k * H * NS:(k + 1) * H * NS].rearrange("p (h b t) -> p b h t", h=H, b=NB))
            for c in range(2):
                for b in range(NB):
                    v.tensor_copy(qrope[0:DR, b].rearrange("p (j c t) -> p j c t", c=2, t=NT)[:, :, c, :],
                                  qrS[c * DR:(c + 1) * DR, :, b * NT:(b + 1) * NT])
            v.drain().then_inc(sig["qlat_ready"], 1)

            def sequence(b, par):
                v.tensor_copy(qb[par][:, 0:2, :], qlat[:, :, bass.ds(b, 1), :].rearrange("p k a q -> p k (a q)"))
                v.tensor_copy(qb[par][0:DR, 2:3, :], qrope[0:DR, bass.ds(b, 1), :])
                v.drain().then_inc(sig["qb_ready"], 1)
                for t in range(8):
                    step = 8 * b + t
                    v.wait_ge(sig["qk_mm"], happened("qk_mm", step - 1))
                    v.wait_ge(sig["kt_mm1"], happened("kt_mm1", step + 1))
                    v.tensor_copy(kT[t % 2][:, 1], ps[:, 3, :].rearrange("p (g c) -> p g c", g=4)).then_inc(sig["kt1"], 1)
                v.wait_ge(sig["new_mm"], happened("new_mm", b + 1))
                v.reduce_max(st[:, 0:1], ps[:, 0:2, :].rearrange("p n c -> p (n c)"), X)
                v.reduce_max(st[0:NS, 1:2], ps[0:NS, 5, 0:NS], X)
                v.drain()
                v.tensor_tensor(st[0:NS, 0:1], st[0:NS, 0:1], st[0:NS, 1:2], ALU.max)
                v.drain().then_inc(sig["mx_ready"], 1)
                v.wait_ge(sig["mxT_mm"], happened("mxT_mm", b + 1))
                v.reduce_max(mrow[0:1, 0:NS], ps[0:1, 5, 64:64 + P].rearrange("p (g q) -> p q g", g=4), X)
                v.drain()
                v.tensor_copy(mrow[0:1, NS:NS + P].rearrange("p (g q) -> p g q", g=4),
                              mrow[0:1, 0:NS].unsqueeze(1).broadcast_to([1, 4, NS])).then_inc(sig["mrow_ready"], 1)
                v.wait_ge(sig["mb_mm"], happened("mb_mm", b + 1))
                v.tensor_scalar(st[:, 2:3], ps[:, 5, 200:201], -MLA_SCALE, None, ALU.mult).then_inc(sig["nms_ready"], 1)
                v.wait_ge(sig["p_s_ready"], happened("p_s_ready", b + 1))
                v.tensor_tensor(st[0:NS, 3:4], st[0:NS, 3:4], st[0:NS, 4:5], ALU.add)
                v.drain()
                v.tensor_scalar(l_bc, ones, st[:, 3:4], None, ALU.mult).then_inc(sig["lbc_ready"], 1)
                v.wait_ge(sig["pT_s_mm"], happened("pT_s_mm", 2 * b + 2))
                v.tensor_copy(pT_s[:, 4:8], ps[:, 4, :].rearrange("p (n c) -> p n c", n=4))
                v.tensor_copy(pTn_s[0:NS, :], ps[0:NS, 5, 224:224 + NS])
                v.drain().then_inc(sig["pTb_s"], 1)
                v.wait_ge(sig["oc_mm"], happened("oc_mm", b + 1))
                v.reciprocal(linv, ps[:, 5, 320:320 + NS])
                v.drain()
                for k in range(2):
                    v.tensor_tensor(olatT[:, k, :, bass.ds(b * NT, NT)],
                                    ps[:, 5, 256 + k * NS:256 + (k + 1) * NS].rearrange("p (h t) -> p h t", h=H),
                                    linv.rearrange("p (h t) -> p h t", h=H), ALU.mult)
                v.drain().then_inc(sig["olat_ready"], 1)

            with v.Fori(0, NB // 2) as i:
                for par in range(2):
                    sequence(2 * i + par, par)
            v.wait_ge(sig["oTs_mm"], happened("oTs_mm", 1))
            v.tensor_copy(oT[:, :, SEQ:], ps[:, 0, 0:H * NS].rearrange("p (h t) -> p h t", h=H)
                          ).then_inc(sig["oTs_ready"], 1)
            for T in range(TILES):
                n = rows_of(T)
                v.wait_ge(sig["wo_mm"], happened("wo_mm", T + 1))
                out = [ps[0:n, 2 + 2 * (T % 2) + c, :] for c in range(2)]
                if n == NS:
                    out[1] = pT_s.rearrange("p a b -> p (a b)")[0:n, 0:FF]
                    v.tensor_copy(out[1], ps[n:2 * n, 2 + 2 * (T % 2) + 1, :])
                    v.drain()
                for c in range(2):
                    v.tensor_tensor(xt(T, n, c * FF, (c + 1) * FF), xt(T, n, c * FF, (c + 1) * FF), out[c], ALU.add)
                v.drain().then_inc(sig["wo_added"], 1)
            v.drain().then_inc(sig["x_ready"], 1)

            def over_tiles(ap, n):
                return ap[:, 0:n].unsqueeze(1).broadcast_to([P, TILES, n])

            def over_last(ap, n):
                return ap.unsqueeze(2).broadcast_to([P, TILES, n])

            def first_largest(vals, n, top, low, hit, out):
                v.tensor_reduce(top, vals, X, ALU.max)
                v.drain()
                v.tensor_tensor(hit, vals, over_last(top, n), ALU.is_equal)
                v.drain()
                v.tensor_tensor(hit, hit, over_tiles(idxm, n), ALU.mult)
                v.drain()
                v.tensor_reduce(low, hit, X, ALU.min)
                v.drain()
                v.tensor_tensor(out, over_tiles(idxm, n), over_last(low, n), ALU.is_equal)
                v.drain()

            def experts(L):
                f = 2 * L + 1
                start_more(v, L, "marks idx_cv hid hidT y1")
                roots(f + 1, 0, TILES)
                v.wait_ge(sig["gain_in"], landed("gain_in", f + 1))
                v.memset(lg, 0.0)
                v.drain()

                def logits(T):
                    n = rows_of(T)
                    v.wait_ge(sig["lg_mm"], happened("lg_mm", TILES * L + T + 1))
                    v.tensor_tensor(lg[0:n, T:T + 1, :], ps[0:n, 2 + 5 * (T % 2), 0:NG + NE].unsqueeze(1),
                                    rbias[0:n].unsqueeze(1), ALU.add).then_inc(sig["lg_ready"], 1)

                norm_tile(f, 0, h_r[0], 2)
                for T in range(TILES):
                    if T + 1 < TILES:
                        norm_tile(f, T + 1, h_r[T + 1], 2)
                    half_T(f, T, hT_r[T % 2], 1 + 5 * (T % 2))
                    if T == 0:
                        for b in range(2):
                            v.wait_ge(sig[f"scattered{b}"], landed(f"scattered{b}", STORES * L + 1))
                    if T:
                        logits(T - 1)
                logits(PT)
                v.drain()
                gl = lg[:, :, 0:NG]
                first_largest(gl, NG, t5[0], t5[1], tg[1], tg[2])
                v.tensor_tensor(tg[0], gl, over_last(t5[0], NG), ALU.subtract).then_inc(sig["gsub_ready"], 1)
                v.tensor_scalar(tg[2], tg[2], 1e30, -1e30, ALU.mult, ALU.add)
                v.drain()
                for T in range(TILES):
                    v.tensor_tensor(te[0][:, T].rearrange("p (g e) -> p g e", g=NG),
                                    lg[:, T, NG:].rearrange("p (g e) -> p g e", g=NG),
                                    tg[2][:, T].unsqueeze(2).broadcast_to([P, NG, EG]), ALU.add)
                v.drain()
                first_largest(te[0], NE, t5[3], t5[1], te[3], te[1])
                v.scalar_tensor_tensor(out=te[0], in0=te[1], scalar=-3e30, in1=te[0], op0=ALU.mult, op1=ALU.add)
                v.drain()
                first_largest(te[0], NE, t5[6], t5[1], te[3], te[2])
                v.tensor_tensor(t5[4], t5[6], t5[3], ALU.subtract).then_inc(sig["esub_ready"], 1)
                v.tensor_tensor(te[3], te[1], te[2], ALU.add)
                v.memset(rankm, -1.0)
                v.memset(code, 0.0)
                v.drain()
                v.tensor_tensor(te[4], te[3], over_last(valid, NE), ALU.mult)
                v.tensor_copy(code[:, 0, :, 0:NE], over_last(tokcode[:, 0], NE))
                v.tensor_tensor(code[:, 1, :, 0:NE], te[2], over_last(tokcode[:, 1], NE), ALU.add)
                v.drain().then_inc(sig["sel_ready"], 1)
                v.wait_ge(sig["gexp_ready"], happened("gexp_ready", L + 1))
                v.tensor_reduce(t5[2], tg[1], X, ALU.add)
                v.wait_ge(sig["eexp_ready"], happened("eexp_ready", L + 1))
                v.tensor_scalar(t5[7], t5[5], 1.0, None, ALU.add)
                v.drain()
                v.tensor_tensor(t5[6], t5[2], t5[7], ALU.mult)
                v.drain()
                v.reciprocal(gate1, t5[6])
                v.drain()
                v.tensor_tensor(gate2, gate1, t5[5], ALU.mult)
                v.wait_ge(sig["rank_mm"], happened("rank_mm", L + 1))
                v.scalar_tensor_tensor(out=te[3], in0=ps[:, 3, 0:TILES * NE].rearrange("p (t e) -> p t e", t=TILES),
                                       scalar=1.0, in1=te[4], op0=ALU.add, op1=ALU.mult)
                v.tensor_copy(lt[0:NE, 0:1], ps[0:NE, 4, 0:1])
                v.drain()
                v.tensor_scalar(rankm[:, :, 0:NE], te[3], -1.0, None, ALU.add)
                v.drain()

                def mark(q, b):
                    v.tensor_tensor(onehot[b], rankm[:, :, cols(q, 1)].broadcast_to([P, TILES, BLK]),
                                    slots.unsqueeze(1).broadcast_to([P, TILES, BLK]), ALU.is_equal
                                    ).then_inc(sig["onehot_ready"], 1)

                def numbers(q, b):
                    v.wait_ge(sig["idx_mm"], happened("idx_mm", FETCHES * L + q + 1))
                    v.tensor_scalar(store_rows[0:BLK, cols(q, 1)], ps[0:BLK, 4, 2 * b + 1:2 * b + 2], FAR, None, ALU.add)
                    v.drain()
                    v.tensor_scalar(fetch_at[b][0:BLK, :], ps[0:BLK, 4, 2 * b:2 * b + 1], FAR, None, ALU.add
                                    ).then_inc(sig["idx_ready"], 1)

                for q in range(LOOK):
                    if q >= 2:
                        v.wait_ge(sig["idx_mm"], happened("idx_mm", FETCHES * L + q - 1))
                    mark(q, q % 2)
                    if q:
                        numbers(q - 1, (q - 1) % 2)
                v.tensor_scalar(lt[0:NE, 16:16 + MORE], blkat[0:NE, :], lt[0:NE, 0:1], None, ALU.is_lt)
                v.drain()
                v.reduce_sum(lt[0:NE, 1:2], lt[0:NE, 16:16 + MORE], X)
                v.drain().then_inc(sig["nb_ready"], 1)
                v.wait_ge(sig["pre_mm"], happened("pre_mm", L + 1))
                v.tensor_copy(lt[0:NE, 2:3], ps[0:NE, 4, 8:9])
                v.drain()
                v.tensor_scalar(lt[0:NE, 3:4], lt[0:NE, 2:3], -1.0, 1.0, ALU.mult, ALU.add)
                v.tensor_tensor(lt[0:NE, 4:5], lt[0:NE, 2:3], lt[0:NE, 1:2], ALU.add)
                v.tensor_scalar(lt[0:NE, 32:32 + LIST], idx[0:NE, 0:LIST], lt[0:NE, 2:3], None, ALU.is_ge)
                v.drain()
                v.tensor_scalar(lt[0:NE, 64:64 + LIST], idx[0:NE, 0:LIST], lt[0:NE, 4:5], None, ALU.is_lt)
                v.tensor_scalar(jrep[0:NE, :], ones[0:NE, :], lt[0:NE, 3:4], None, ALU.mult)
                v.drain()
                v.tensor_tensor(lt[0:NE, 32:32 + LIST], lt[0:NE, 32:32 + LIST], lt[0:NE, 64:64 + LIST], ALU.mult)
                v.drain().then_inc(sig["list_ready"], 1)
                v.wait_ge(sig["listrow_mm"], happened("listrow_mm", L + 1))
                v.tensor_copy(lst[0:1, 0:LIST], ps[0:1, 4, 16:16 + LIST])
                v.tensor_copy(lst[0:1, 2 * NE - 1:2 * NE], ps[0:1, 4, 40:41])
                v.tensor_tensor(jstart, ps[:, 4, 64:64 + LIST], idx[:, 0:LIST], ALU.add)
                v.drain()
                v.tensor_scalar(jstart, jstart, float(BLK), None, ALU.mult)
                v.drain().then_inc(sig["lst_ready"], 1)

                numbers(LOOK - 1, (LOOK - 1) % 2)
                with v.Fori(0, NE // 2) as i:
                    for b in range(2):
                        e = 2 * i + b
                        v.wait_ge(sig["idx_mm"], happened("idx_mm", FETCHES * L + e + LOOK - 1))
                        mark(e + LOOK, 1 - b)
                        v.wait_ge(sig["silu_ready"], happened("silu_ready", NE * L + e + 1))
                        v.wait_ge(sig["ht_mm"], happened("ht_mm", NE * L + e))
                        v.tensor_tensor(hid[0:BLK, :], sg[BLK:2 * BLK, :], ps[BLK:2 * BLK, b, :], ALU.mult
                                        ).then_inc(sig["hid_ready"], 1)
                        numbers(e + LOOK, 1 - b)
                        v.wait_ge(sig["ht_mm"], happened("ht_mm", NE * L + e + 1))
                        v.wait_ge(sig["d_mm"], happened("d_mm", NE * L + e))
                        v.tensor_copy(hidT, ps[:, 6, 0:KF * BLK].rearrange("p (k t) -> p k t", k=KF)
                                      ).then_inc(sig["hidT_ready"], 1)
                        v.wait_ge(sig[f"scattered{b}"], landed(f"scattered{b}", STORES * L + i + 1))
                        v.tensor_copy(store_at[b][0:BLK, :], store_rows[0:BLK, cols(e, 1)])
                        v.drain()
                        v.wait_ge(sig["d_mm"], happened("d_mm", NE * L + e + 1))
                        v.tensor_copy(ye[b][0:BLK, FF:D], ps[BLK:2 * BLK, 2 + b, :]).then_inc(sig["y1_ready"], 1)
                for b in range(2):
                    v.wait_ge(sig[f"scattered{b}"], landed(f"scattered{b}", STORES * (L + 1)))
                    v.wait_ge(sig[f"gathered{b}"], landed(f"gathered{b}", INTO[b] * (L + 1)))
                n = v.value_load(lst[0:1, 2 * NE - 1:2 * NE], min_val=0, max_val=LIST)
                with v.If(n > 0):
                    with v.Fori(0, n) as i:
                        v.wait_ge(sig["more_done"], i + 1)
                        e = v.value_load(lst[0:1, bass.ds(i, 1)], min_val=0, max_val=NE - 1)
                        v.tensor_scalar(shift, rankm[:, :, bass.ds(e, 1)].rearrange("p t a -> p (t a)"),
                                        jstart[:, bass.ds(i, 1)], None, ALU.subtract)
                        v.drain()
                        v.tensor_tensor(onehot[0], shift.unsqueeze(2).broadcast_to([P, TILES, BLK]),
                                        slots.unsqueeze(1).broadcast_to([P, TILES, BLK]), ALU.is_equal
                                        ).then_inc(sig["more_marks"], 1)
                        v.wait_ge(sig["more_idx_mm"], i + 1)
                        v.tensor_scalar(store_at[0][0:BLK, :], ps[0:BLK, 4, 1:2], FAR, None, ALU.add)
                        v.drain()
                        v.tensor_scalar(fetch_at[0][0:BLK, :], ps[0:BLK, 4, 0:1], FAR, None, ALU.add
                                        ).then_inc(sig["more_idx_cv"], 1)
                        v.wait_ge(sig["more_silu"], i + 1)
                        v.tensor_tensor(hid[0:BLK, :], sg[BLK:2 * BLK, :], ps[BLK:2 * BLK, 0, :], ALU.mult
                                        ).then_inc(sig["more_hid"], 1)
                        v.wait_ge(sig["more_ht_mm"], i + 1)
                        v.tensor_copy(hidT, ps[:, 6, 0:KF * BLK].rearrange("p (k t) -> p k t", k=KF)
                                      ).then_inc(sig["more_hidT"], 1)
                        v.wait_ge(sig["more_d_mm"], i + 2)
                        v.tensor_copy(ye[0][0:BLK, FF:D], ps[BLK:2 * BLK, 2, :]).then_inc(sig["more_y1"], 1)
                for T in range(TILES):
                    n = rows_of(T)
                    v.wait_ge(sig[f"ybuf{T % 2}"], landed(f"ybuf{T % 2}", SAVES[T % 2] * L + T // 2 + 1))
                    for part, weight in enumerate((gate1, gate2)):
                        v.scalar_tensor_tensor(out=xt(T, n), in0=ybuf[T][0:n, part * D:(part + 1) * D],
                                               scalar=weight[0:n, T:T + 1], in1=xt(T, n), op0=ALU.mult, op1=ALU.add)
                        v.drain()
                    v.drain().then_inc(sig["y_added"], 1)
                v.drain().then_inc(sig["x_ready"], 1)

            experts(0)

            v.memset(vb[:, 0:SKV * SD], 0.0)
            v.memset(kT_w, 0.0)
            roots(3, 0, TILES)
            v.wait_ge(sig["gain_in"], landed("gain_in", 3))

            def window(T):
                n = rows_of(T)
                half_T(2, T, hT_w)
                v.wait_ge(sig["swaconst_in"], landed("swaconst_in", 4))
                v.wait_ge(sig["v_w"], happened("v_w", T))
                if n != P:
                    v.wait_ge(sig["state_out"], landed("state_out", 2))
                for c in range(3):
                    v.wait_ge(sig["qkv_mm"], happened("qkv_mm", 3 * T + c + 1))
                    strip = slice(c * NS, (c + 1) * NS) if n == NS else slice(0, P)
                    v.tensor_tensor(qkv[0:n, c * FF:(c + 1) * FF], ps[strip, 2 + c, :], bqkv[strip, c * FF:(c + 1) * FF], ALU.add)
                v.tensor_copy(kT_w[:, :, 0:P], kT_w[:, :, P:])
                v.drain().then_inc(sig["v_ready"], 1)
                heads = SH + SKV
                src = qkv[0:n, 0:heads * SD].rearrange("p (h c r) -> p h c r", h=heads, c=2)
                dst = qkr[0:n].rearrange("p (h c r) -> p h c r", h=heads, c=2)
                t0, t1 = (t[0:n].rearrange("p (h r) -> p h r", h=heads) for t in tw)
                c, s_ = (q[0:n, cols(T * (DR // 2), DR // 2)].unsqueeze(1).broadcast_to([n, heads, DR // 2])
                         for q in (cos_tok, sin_tok))
                for out, op, one, two in ((0, ALU.subtract, 0, 1), (1, ALU.add, 1, 0)):
                    v.tensor_tensor(t0, src[:, :, one], c, ALU.mult)
                    v.tensor_tensor(t1, src[:, :, two], s_, ALU.mult)
                    v.drain()
                    v.tensor_tensor(dst[:, :, out], t0, t1, op)
                    v.drain()
                v.drain().then_inc(sig["qkr_ready"], 1)

            def queries_T(T):
                n = rows_of(T)
                v.wait_ge(sig["qT_mm"], happened("qT_mm", T + 1))
                for c in range(2):
                    for half_ in range(2):
                        v.tensor_copy(kT_w[half_ * SD:(half_ + 1) * SD, c:SKV:2, P:P + n],
                                      ps[c * SD:(c + 1) * SD, 7, 0:2 * P].rearrange("p (k t) -> p k t", k=2)[:, :, 0:n])
                if n == P:
                    v.tensor_copy(qT_w[:, 4:8, 0:n], ps[:, 6, :].rearrange("p (k t) -> p k t", k=4)[:, :, 0:n])
                else:
                    v.memset(qS, 0.0)
                    v.drain()
                    for h in range(SH):
                        g, a_ = divmod(h, SG)
                        tile_, c = divmod(h, 2)
                        v.tensor_copy(qS[g % 2 * SD:(g % 2 + 1) * SD, g // 2, :, a_ * NT:(a_ + 1) * NT],
                                      ps[c * SD:(c + 1) * SD, 5 + tile_ // 4, tile_ % 4 * P:tile_ % 4 * P + NS]
                                      .rearrange("p (b t) -> p b t", b=NB))
                v.drain().then_inc(sig["qTb_w"], 1)

            def attend(T):
                def scores(u):
                    r_ = mw[u % 2]
                    sk = sinks[:, 2 * u:2 * u + 2]
                    v.wait_ge(sig["s_w_mm"], happened("s_w_mm", SUNITS * T + u + 1))
                    v.tensor_tensor(sw[u % 2], ps[:, 2 - 2 * (u % 2):4 - 2 * (u % 2), 0:2 * P],
                                    masks[:, cols(T * 2 * P, 2 * P)].unsqueeze(1).broadcast_to([P, 2, 2 * P]), ALU.add)
                    v.drain()
                    v.tensor_reduce(r_[:, 0:2], sw[u % 2], X, ALU.max)
                    v.drain()
                    v.scalar_tensor_tensor(out=r_[:, 0:2], in0=r_[:, 0:2], scalar=SWA_SCALE, in1=sk, op0=ALU.mult, op1=ALU.max)
                    v.drain()
                    v.tensor_scalar(r_[:, 2:4], r_[:, 0:2], -1.0, None, ALU.mult)
                    v.tensor_tensor(r_[:, 6:8], sk, r_[:, 0:2], ALU.subtract)
                    v.drain().then_inc(sig["s_w_ready"], 1)

                scores(0)
                for u in range(SUNITS):
                    if u + 1 < SUNITS:
                        scores(u + 1)
                    v.wait_ge(sig["pT_w_mm"], happened("pT_w_mm", SUNITS * T + u + 1))
                    v.tensor_copy(pT_w[u % 2], ps[:, 4 + u % 2, :].rearrange("p (n t) -> p n t", n=4)
                                  ).then_inc(sig["pT_w_ready"], 1)
                    v.tensor_tensor(den[:, 2 * u:2 * u + 2], mw[u % 2][:, 4:6], mw[u % 2][:, 6:8], ALU.add)
                    v.drain()
                    if u == SUNITS // 2:
                        norm_tile(2, T + 1, h_w)
                v.reciprocal(den, den)
                v.drain()
                v.wait_ge(sig["o_w_mm"], happened("o_w_mm", SUNITS * (T + 1)))
                v.tensor_tensor(o_w.rearrange("p (h d) -> p h d", h=SH), ps[:, 6:8, :].rearrange("p n (h d) -> p (n h) d", d=SD),
                                den.unsqueeze(2).broadcast_to([P, SH, SD]), ALU.mult).then_inc(sig["o_w_ready"], 1)
                v.wait_ge(sig["oT_w_mm"], happened("oT_w_mm", T + 1))
                v.tensor_copy(oT_w[:, 4:8, :], ps[:, 1, :].rearrange("p (k t) -> p k t", k=4)).then_inc(sig["oTb_w"], 1)

            def add_out(T):
                n = rows_of(T)
                v.tensor_tensor(xt(T, n), xt(T, n), bo[0:n, :], ALU.add)
                v.drain()
                v.wait_ge(sig["wo_mm"], happened("wo_mm", TILES + T + 1))
                if n == NS:
                    v.tensor_copy(h_w[0:n, 0:FF], ps[n:2 * n, 1, :])
                    v.tensor_tensor(xt(T, n, 0, FF), xt(T, n, 0, FF), ps[0:n, 0, :], ALU.add)
                    v.drain()
                    v.tensor_tensor(xt(T, n, FF, D), xt(T, n, FF, D), h_w[0:n, 0:FF], ALU.add)
                    v.drain().then_inc(sig["wo_added"], 1)
                    return
                v.tensor_tensor(xt(T, n), xt(T, n), ps[0:n, 0:2, :].rearrange("p n c -> p (n c)"), ALU.add)
                v.drain().then_inc(sig["wo_added"], 1)

            def tile(T):
                queries_T(T)
                attend(T)
                window(T + 1)
                add_out(T)

            norm_tile(2, 0, h_w)
            window(0)
            with v.Fori(0, PT - 1) as T:
                tile(T)
            tile(PT - 1)
            queries_T(PT)
            v.wait_ge(sig["qkv_mm"], happened("qkv_mm", 3 * TILES))
            v.memset(sink_z, 0.0)
            v.drain().then_inc(sig["sink_clear"], 1)
            for n in range(2):
                v.wait_ge(sig["kb_mm"], happened("kb_mm", 2 * n + 2))
                v.tensor_copy(kbT[:, 4 * n + 2:4 * n + 4], ps[:, 2 * n + 1, :].rearrange("p (b g c) -> p b g c", b=2, g=2)
                              ).then_inc(sig["kb_dve"], 1)
            v.wait_ge(sig["cacheb_in"], landed("cacheb_in", 3 + SKV))
            v.wait_ge(sig["sample_s_mm"], happened("sample_s_mm", 1))
            for n in range(3):
                b0, nb = 3 * n, min(3, NB - 3 * n)
                src = ps[:, 4 + n, 0:nb * (P + NS)].rearrange("p (b k) -> p b k", b=nb)
                v.scalar_tensor_tensor(out=s_z[:, b0:b0 + nb, 0:P], in0=src[:, :, 0:P], scalar=SWA_SCALE,
                                       in1=mask_z[:, 0:P].unsqueeze(1).broadcast_to([P, nb, P]), op0=ALU.mult, op1=ALU.add)
                v.scalar_tensor_tensor(out=s_z[:, b0:b0 + nb, P:], in0=src[:, :, P:], scalar=SWA_SCALE,
                                       in1=mask_z[:, P + b0 * NS:P + (b0 + nb) * NS].rearrange("p (b k) -> p b k", b=nb),
                                       op0=ALU.mult, op1=ALU.add)
            v.drain()
            v.tensor_reduce(m_z, s_z, X, ALU.max)
            v.drain()
            v.tensor_scalar(m_z, m_z, sink_z[:, 0:1], None, ALU.max)
            v.drain()
            v.tensor_tensor(s_z, s_z, m_z.unsqueeze(2).broadcast_to([P, NB, P + NS]), ALU.subtract)
            v.drain()
            v.tensor_scalar(m_z, m_z, -1.0, sink_z[:, 0:1], ALU.mult, ALU.add)
            v.drain().then_inc(sig["sample_s"], 1)
            v.wait_ge(sig["sample_e"], happened("sample_e", 1))
            v.tensor_reduce(l_z, s_z, X, ALU.add)
            v.drain()
            v.tensor_tensor(l_z, l_z, m_z, ALU.add)
            v.drain()
            v.reciprocal(l_z, l_z)
            v.drain()
            v.tensor_tensor(s_z, s_z, l_z.unsqueeze(2).broadcast_to([P, NB, P + NS]), ALU.mult)
            v.drain().then_inc(sig["sample_p"], 1)
            v.wait_ge(sig["sample_pT_mm"], happened("sample_pT_mm", 1))
            v.tensor_copy(pT_z[:, 4:8], ps[:, 5, :].rearrange("p (b r) -> p b r", b=4))
            v.tensor_copy(pTn_z[0:NS, 4:8], ps[0:NS, 7, :].rearrange("p (b r) -> p b r", b=4))
            v.drain().then_inc(sig["sample_pT_dve"], 1)
            v.wait_ge(sig["sample_o_mm"], happened("sample_o_mm", 1))
            for g in range(SKV):
                src = ps[0:SD, 0, g * P:(g + 1) * P].rearrange("p (b a c t) -> p c a b t", b=NB, a=2, c=2)
                for c in range(2):
                    for a_ in range(2):
                        v.tensor_copy(oT_w[c * SD:(c + 1) * SD, 2 * g + a_, 0:NS].rearrange("p (b t) -> p b t", b=NB),
                                      src[:, c, a_])
            v.drain().then_inc(sig["sample_o"], 1)
            add_out(PT)
            v.drain().then_inc(sig["x_ready"], 1)
            experts(1)
            roots(5, 0, TILES)
            v.wait_ge(sig["gain_in"], landed("gain_in", 5))
            for T in range(TILES):
                n = rows_of(T)
                v.wait_ge(sig[f"y_out{T % 2}"], landed(f"y_out{T % 2}", T // 2))
                v.scalar_tensor_tensor(out=h_fin[T % 2][0:n, :], in0=xt(T, n), scalar=rstd[0:n, T:T + 1], in1=gain[0:n, :],
                                       op0=ALU.mult, op1=ALU.mult).then_inc(sig["y_ready"], 1)

        @block.tensor
        def _(pe):
            start_counts(pe, "tensor")

            def mm(out, lhsT, rhs, start, stop):
                return pe.matmul(out, lhsT, rhs, start=start, stop=stop)

            def flip(out, in_):
                n, at = in_.shape[0], in_.start_partition()
                return pe.transpose(out, in_, ident[at:at + n, at:at + n])

            def rows_T(f, T, h, bank=0, buffers=1):
                n = rows_of(T)
                pe.wait_ge(sig["hTa"], happened("hTa", TILES * f + T + 1 - buffers))
                pe.wait_ge(sig["hTb"], happened("hTb", TILES * f + T + 1 - buffers))
                pe.wait_ge(sig["h_ready"], happened("h_ready", TILES * f + T + 1))
                for k in range(KD):
                    last = flip(ps[:, bank + k // 4, (k % 4) * P:(k % 4) * P + n], h[0:n, k:D:KD])
                last.then_inc(sig["hT_mm"], 1)

            pe.wait_ge(sig["consts_in"], landed("consts_in", 1))

            def latent(T):
                n = rows_of(T)
                A = 2 + 4 * (T % 2)
                pe.wait_ge(sig["hTa"], happened("hTa", T + 1))
                pe.wait_ge(sig["hTb"], happened("hTb", T + 1))
                pe.wait_ge(sig["rows_ready"], happened("rows_ready", T - 1))
                for k in range(KD):
                    if T == 0 and k == 0:
                        pe.wait_ge(sig["w_a_in"], landed("w_a_in", 1))
                    if T == 0 and k == KD // 2:
                        pe.wait_ge(sig["w_a_late_in"], landed("w_a_late_in", 1))
                    for bank, c0, c1 in ((A, 0, QL), (A + 1, QL, QL + ROW)):
                        last = mm(ps[0:n, bank, 0:c1 - c0], hT_m[:, k, 0:n], w_a[:, k, c0:c1], k == 0, k == KD - 1)
                last.then_inc(sig["a_mm"], 1)

            def latent_T(T):
                n = rows_of(T)
                pe.wait_ge(sig["rows_ready"], happened("rows_ready", T + 1))
                pe.wait_ge(sig["cqT_ready"], happened("cqT_ready", T))
                pe.wait_ge(sig["cT_ready"], happened("cT_ready", T))
                for k in range(3):
                    flip(ps[:, 4, k * P:k * P + n], cq[0:n, k * P:(k + 1) * P])
                for k in range(2):
                    flip(ps[:, 5, k * P:k * P + n], rowbuf[0:n, k * P:(k + 1) * P])
                flip(ps[0:DR, 5, CL:CL + n], rowbuf[0:n, CL:ROW]).then_inc(sig["rowsT_mm"], 1)

            rows_T(0, 0, h_m)
            for T in range(TILES):
                latent(T)
                if T + 1 < TILES:
                    rows_T(0, T + 1, h_m)
                if T:
                    latent_T(T - 1)
            latent_T(PT)
            pe.wait_ge(sig["cqT_ready"], happened("cqT_ready", TILES))
            pe.wait_ge(sig["cT_ready"], happened("cT_ready", TILES))
            pe.wait_ge(sig["mlaconst_in"], landed("mlaconst_in", 8))

            with pe.Fori(0, PAIRS) as j:
                pe.wait_ge(sig["wqp_in"], landed("wqp_in", 4 * (j + 1)))
                pe.wait_ge(sig["pT_m_ready"], happened("pT_m_ready", 2 * PT * j))
                for part, bank in enumerate((0, 1, 3)):
                    for k in range(3):
                        mm(ps[:, bank, :], wqp[:, k, part * DN:(part + 1) * DN], cqT[:, k, 0:SEQ], k == 0, k == 2)
                    for k in range(3):
                        last = mm(ps[:, 2, part * NS:(part + 1) * NS], wqp[:, k, part * DN:(part + 1) * DN],
                                  cqT[:, k, SEQ:], k == 0, k == 2)
                last.then_inc(sig["q_mm"], 1)
                pe.wait_ge(sig["wkp_in"], landed("wkp_in", j + 1))
                pe.wait_ge(sig["oT_act"], happened("oT_act", 2 * PT * j))
                for hh in range(2):
                    for k in range(2):
                        mm(ps[:, 5 + hh, :], wkp[:, k, 2 * hh * DN:(2 * hh + 1) * DN], cT[:, k, 0:SEQ], k == 0, k == 1)
                pe.wait_ge(sig["q_act"], happened("q_act", j + 1))
                pe.wait_ge(sig["q_dve"], happened("q_dve", j + 1))
                mm(ps[:, 4, :], swap, qraw[:, 0:SEQ], True, True)
                mm(ps[:, 2, P:P + NS], swap, qraw[:, SEQ:], True, True).then_inc(sig["swap_mm"], 1)
                values = wkp.rearrange("p k (h c n) -> p k h c n", h=2, c=2)
                for t in range(PT):
                    for k in range(2):
                        last = mm(ps[:, 7 if t < 2 else 1, (t % 2) * CL:(t % 2 + 1) * CL].rearrange("p (h n) -> p h n", h=2),
                                  cT[:, k, t * P:(t + 1) * P], values[:, k, :, 1, :], k == 0, k == 1)
                last.then_inc(sig["kv_mm"], 1)
                pe.wait_ge(sig["qr_ready"], happened("qr_ready", j + 1))
                pe.wait_ge(sig["kv_act"], happened("kv_act", j + 1))
                pe.wait_ge(sig["kv_dve"], happened("kv_dve", j + 1))

                def scores(q):
                    hh, qi = unit(q)
                    nk = (qi + 1) * P
                    pe.wait_ge(sig["p_ready"], happened("p_ready", 2 * PT * j + q - 1))
                    mm(ps[:, q % 2, 0:nk], qn[hh][:, qi * P:nk], kn[hh][:, 0:nk], True, False)
                    mm(ps[:, q % 2, 0:nk], qr[hh * DR:(hh + 1) * DR, qi * P:nk], krT[hh * DR:(hh + 1) * DR, 0:nk], False, False)
                    mm(ps[:, q % 2, nk - P:nk], ident, causal, False, True).then_inc(sig["s_mm"], 1)

                def values_of(q):
                    hh, qi = unit(q)
                    pe.wait_ge(sig["pT_m_ready"], happened("pT_m_ready", 2 * PT * j + q + 1))
                    for t in range(qi + 1):
                        last = mm(ps[:, 4 + q % 2, 0:P], pT_m[q % 2][:, t, :], v_m[:, t, hh * DN:(hh + 1) * DN], t == 0, t == qi)
                    last.then_inc(sig["o_mm"], 1)

                def out_T(q):
                    pe.wait_ge(sig["o_m_ready"], happened("o_m_ready", 2 * PT * j + q + 1))
                    pe.wait_ge(sig["oT_act"], happened("oT_act", 2 * PT * j + q - 1))
                    flip(ps[:, 6 + q % 2, 0:P], o_m[q % 2]).then_inc(sig["oT_mm"], 1)

                scores(0)
                for q in range(2 * PT):
                    hh, qi = unit(q)
                    if q + 1 < 2 * PT:
                        scores(q + 1)
                    pe.wait_ge(sig["p_ready"], happened("p_ready", 2 * PT * j + q + 1))
                    pe.wait_ge(sig["pT_m_ready"], happened("pT_m_ready", 2 * PT * j + q - 1))
                    for t in range(qi + 1):
                        last = flip(ps[:, 2 + q % 2, t * P:(t + 1) * P], p_m[q % 2][:, t * P:(t + 1) * P])
                    last.then_inc(sig["pT_mm"], 1)
                    if q:
                        values_of(q - 1)
                    if q >= 2:
                        out_T(q - 2)
                values_of(2 * PT - 1)
                out_T(2 * PT - 2)
                out_T(2 * PT - 1)

            pe.wait_ge(sig["oT_act"], happened("oT_act", 2 * PT * PAIRS))
            pe.wait_ge(sig["wkvb_in"], landed("wkvb_in", 1))
            for n in range(4):
                for i in range(4):
                    hh, k = 2 * n + i // 2, i % 2
                    last = flip(ps[:, n, i * P:(i + 1) * P], wkvb[:, k, 2 * hh * DN:(2 * hh + 1) * DN])
                last.then_inc(sig["wuk_mm"], 1)
            pe.wait_ge(sig["wuk_act"], happened("wuk_act", 2))
            pe.wait_ge(sig["wuk_dve"], happened("wuk_dve", 2))
            for k in range(2):
                for hh in range(H):
                    last = mm(ps[:, 4, (k * H + hh) * NS:(k * H + hh + 1) * NS], wukT[:, hh, k, :], qnS[:, hh, :], True, True)
            last.then_inc(sig["qlat_mm"], 1)
            pe.wait_ge(sig["qlat_ready"], happened("qlat_ready", 1))
            pe.wait_ge(sig["mlaconst_in"], landed("mlaconst_in", 10))

            def sequence(b, par, i):
                page = pages[par]

                def keys_T(t):
                    for k in range(3):
                        pe.wait_ge(sig[f"kt{k}"], happened(f"kt{k}", 8 * b + t))
                        turnstile(pe)
                        w_ = DR if k == 2 else P
                        for G in range(4):
                            last = flip(ps[0:w_, 2 + k, G * P:(G + 1) * P], page[:, 8 * G + t, k * P:k * P + w_])
                        last.then_inc(sig[f"kt_mm{k}"], 1)

                def scores(t):
                    for k in range(3):
                        w_ = DR if k == 2 else P
                        pe.wait_ge(sig[f"kt{k}"], happened(f"kt{k}", 8 * b + t + 1))
                        turnstile(pe)
                        for G in range(4):
                            last = mm(ps[G * NS:(G + 1) * NS, t // 4, (t % 4) * P:(t % 4 + 1) * P], qb[par][0:w_, k, :],
                                      kT[t % 2][0:w_, k, G, :], k == 0, k == 2)
                    last.then_inc(sig["qk_mm"], 1)

                pe.wait_ge(sig[f"pages{par}"], landed(f"pages{par}", PAGES // 2 * i))
                pe.wait_ge(sig[f"late_pages{par}"], landed(f"late_pages{par}", PAGES // 2 * i + PAGES))
                turnstile(pe)
                pe.wait_ge(sig["pTb_s"], happened("pTb_s", b))
                keys_T(0)
                pe.wait_ge(sig["qb_ready"], happened("qb_ready", b + 1))
                pe.wait_ge(sig["p_s_ready"], happened("p_s_ready", b))
                for t in range(8):
                    if t < 7:
                        keys_T(t + 1)
                    scores(t)
                pe.wait_ge(sig["olat_ready"], happened("olat_ready", b))
                for k, rhs in enumerate((cT[:, 0, SEQ:], cT[:, 1, SEQ:], krT[0:DR, SEQ:])):
                    w_ = DR if k == 2 else P
                    mm(ps[0:NS, 5, 0:NS], qb[par][0:w_, k, :], rhs, k == 0, False)
                mm(ps[0:NS, 5, 0:NS], ident[:, 0:NS], smask[:, bass.ds(b, 1), :].rearrange("p a q -> p (a q)"), False, True
                   ).then_inc(sig["new_mm"], 1)
                pe.wait_ge(sig["mx_ready"], happened("mx_ready", b + 1))
                flip(ps[0:1, 5, 64:64 + P], st[:, 0:1]).then_inc(sig["mxT_mm"], 1)
                pe.wait_ge(sig["mrow_ready"], happened("mrow_ready", b + 1))
                mm(ps[:, 5, 200:201], mrow[0:1, NS:NS + P], ones[0:1, 0:1], True, True).then_inc(sig["mb_mm"], 1)
                pe.wait_ge(sig["p_s_ready"], happened("p_s_ready", b + 1))
                for t in range(4):
                    last = flip(ps[:, 7, t * P:(t + 1) * P], p_s[:, t * P:(t + 1) * P])
                last.then_inc(sig["pT_s_mm"], 1)
                for t in range(4):
                    flip(ps[:, 4, t * P:(t + 1) * P], p_s[:, (4 + t) * P:(5 + t) * P])
                flip(ps[0:NS, 5, 224:224 + NS], pn_s[0:NS, :]).then_inc(sig["pT_s_mm"], 1)
                pe.wait_ge(sig["o_s_ready"], happened("o_s_ready", b))
                pe.wait_ge(sig["pTa_s"], happened("pTa_s", b + 1))
                for t in range(8):
                    if t == 4:
                        pe.wait_ge(sig["pTb_s"], happened("pTb_s", b + 1))
                    for G in range(4):
                        last = mm(ps[G * NS:(G + 1) * NS, 6, 0:CL], pT_s[:, t, G * NS:(G + 1) * NS], page[:, 8 * G + t, 0:CL],
                                  t == 0, t == 7 and G > 0)
                last = mm(ps[0:NS, 6, 0:CL], pTn_s[0:NS, :], rowbuf[0:NS, 0:CL], False, True)
                last.then_inc(sig["pv_mm"], 1)
                pe.wait_ge(sig["o_s_ready"], happened("o_s_ready", b + 1))
                pe.wait_ge(sig["lbc_ready"], happened("lbc_ready", b + 1))
                for k in range(2):
                    mm(ps[:, 5, 256 + k * NS:256 + (k + 1) * NS], o_s[:, k * P:(k + 1) * P], sel32, True, True)
                mm(ps[:, 5, 320:320 + NS], l_bc, sel32, True, True).then_inc(sig["oc_mm"], 1)

            with pe.Fori(0, NB // 2) as i:
                for par in range(2):
                    sequence(2 * i + par, par, i)
            pe.wait_ge(sig["olat_ready"], happened("olat_ready", NB))
            for hh in range(H):
                for k in range(2):
                    last = mm(ps[:, 0, hh * NS:(hh + 1) * NS], wkvb[:, k, (2 * hh + 1) * DN:(2 * hh + 2) * DN], olatT[:, k, hh, :],
                              k == 0, k == 1)
            last.then_inc(sig["oTs_mm"], 1)
            pe.wait_ge(sig["wo_in"], landed("wo_in", 1))
            for T in range(TILES):
                n = rows_of(T)
                if T == PT:
                    pe.wait_ge(sig["oTs_ready"], happened("oTs_ready", 1))
                pe.wait_ge(sig["wo_added"], happened("wo_added", T - 1))
                for c, k in ([(c, k) for k in range(H) for c in range(2)] if n == NS else
                             [(c, k) for c in range(2) for k in range(H)]):
                    at = c * NS if n == NS else 0
                    last = mm(ps[at:at + n, 2 + 2 * (T % 2) + c, :], oT[:, k, T * P:T * P + n], wo_m[:, k, c * FF:(c + 1) * FF],
                              k == 0, k == H - 1)
                last.then_inc(sig["wo_mm"], 1)

            def experts(L):
                f = 2 * L + 1
                start_more(pe, L, "idx_mm xt_mm gu_mm ht_mm d_mm")
                pe.sem_inc(sig["more_d_mm"], 1)
                pe.wait_ge(sig["rw_in"], landed("rw_in", 2 * (L + 1)))
                pe.wait_ge(sig["wo_added"], happened("wo_added", TILES * (L + 1)))

                def logits(T):
                    n = rows_of(T)
                    pe.wait_ge(sig["hTa"], happened("hTa", TILES * f + T + 1))
                    pe.wait_ge(sig["hTb"], happened("hTb", TILES * f + T + 1))
                    pe.wait_ge(sig["lg_ready"], happened("lg_ready", TILES * L + T - 1))
                    for k in range(KD):
                        last = mm(ps[0:n, 2 + 5 * (T % 2), 0:NG + NE], hT_r[T % 2][:, k, 0:n], rw[:, k, :], k == 0, k == KD - 1)
                    last.then_inc(sig["lg_mm"], 1)

                rows_T(f, 0, h_r[0], 0, 2)
                for T in range(TILES):
                    if T + 1 < TILES:
                        rows_T(f, T + 1, h_r[T + 1], 5 * ((T + 1) % 2), 2)
                    logits(T)
                pe.wait_ge(sig["sel_ready"], happened("sel_ready", L + 1))
                sel = te[4]
                mm(ps[:, 3, 0:TILES * NE], before, sel, True, False)
                for U in range(PT):
                    mm(ps[:, 3, (U + 1) * NE:TILES * NE], ones,
                       sel[:, U, :].unsqueeze(1).broadcast_to([P, PT - U, NE]), False, U == PT - 1)
                for T in range(TILES):
                    last = mm(ps[0:NE, 4, 0:1], sel[:, T, :], ones[:, 0:1], T == 0, T == TILES - 1)
                last.then_inc(sig["rank_mm"], 1)
                def numbers(q, b):
                    pe.wait_ge(sig["onehot_ready"], happened("onehot_ready", FETCHES * L + q + 1))
                    pe.wait_ge(sig["idx_ready"], happened("idx_ready", FETCHES * L + q))
                    turnstile(pe)
                    for T in range(TILES):
                        last = mm(ps[0:BLK, 4, 2 * b:2 * b + 2], onehot[b][:, T, :],
                                  code[:, :, T, cols(q, 1)].rearrange("p c a -> p (c a)"), T == 0, T == TILES - 1)
                    last.then_inc(sig["idx_mm"], 1)

                def fetched_T(q, b, fetched):
                    pe.wait_ge(sig[f"gathered{b}"], landed(f"gathered{b}", fetched))
                    turnstile(pe)
                    pe.wait_ge(sig["xeT_ready"], happened("xeT_ready", (NE + 1) * L + q))
                    turnstile(pe)
                    for k in range(KD):
                        last = flip(ps[:, 5, k * BLK:(k + 1) * BLK], xe[b][0:BLK, k:D:KD])
                    last.then_inc(sig["xt_mm"], 1)

                even, odd = INTO[0] * L, INTO[1] * L
                numbers(0, 0)
                numbers(1, 1)
                pe.wait_ge(sig["nb_ready"], happened("nb_ready", L + 1))
                mm(ps[0:NE, 4, 8:9], before[0:NE, 0:NE], lt[0:NE, 1:2], True, True).then_inc(sig["pre_mm"], 1)
                pe.wait_ge(sig["list_ready"], happened("list_ready", L + 1))
                entry = lt[0:NE, 32:32 + LIST]
                mm(ps[0:1, 4, 16:16 + LIST], epart[0:NE, :], entry, True, True)
                mm(ps[0:1, 4, 40:41], lt[0:NE, 1:2], ones[0:NE, 0:1], True, True)
                mm(ps[:, 4, 64:64 + LIST], jrep[0:NE, :], entry, True, True).then_inc(sig["listrow_mm"], 1)
                pe.wait_ge(sig["lst_ready"], happened("lst_ready", L + 1))
                fetched_T(0, 0, even + 1)
                numbers(2, 0)
                with pe.Fori(0, NE // 2) as i:
                    for b in range(2):
                        e = 2 * i + b
                        pe.wait_ge(sig["xeT_ready"], happened("xeT_ready", (NE + 1) * L + e + 1))
                        pe.wait_ge(sig["hid_ready"], happened("hid_ready", NE * L + e - 1))
                        turnstile(pe)
                        pe.wait_ge(sig[f"g{b}_in"], landed(f"g{b}_in", NE // 2 * L + i + 1))
                        pe.wait_ge(sig[f"u{b}_in"], landed(f"u{b}_in", NE // 2 * L + i + 1))
                        for k in range(KD):
                            for part in range(2):
                                last = mm(ps[part * BLK:(part + 1) * BLK, b, :], xeT[b][:, k, :],
                                          wgt[b][part][:, k * FF:(k + 1) * FF], k == 0, k == KD - 1)
                        last.then_inc(sig["gu_mm"], 1)
                        fetched_T(e + 1, 1 - b, (odd if b == 0 else even + 1) + i + 1)
                        numbers(e + LOOK, 1 - b)
                        pe.wait_ge(sig["hid_ready"], happened("hid_ready", NE * L + e + 1))
                        turnstile(pe)
                        pe.wait_ge(sig["hidT_ready"], happened("hidT_ready", NE * L + e))
                        turnstile(pe)
                        for k in range(KF):
                            last = flip(ps[:, 6, k * BLK:(k + 1) * BLK], hid[0:BLK, k:FF:KF])
                        last.then_inc(sig["ht_mm"], 1)
                        pe.wait_ge(sig[f"d{b}_in"], landed(f"d{b}_in", NE // 2 * L + i + 1))
                        pe.wait_ge(sig["hidT_ready"], happened("hidT_ready", NE * L + e + 1))
                        turnstile(pe)
                        pe.wait_ge(sig["y0_ready"], happened("y0_ready", NE * L + e - 1))
                        turnstile(pe)
                        pe.wait_ge(sig["y1_ready"], happened("y1_ready", NE * L + e - 1))
                        for k in range(KF):
                            for part in range(2):
                                last = mm(ps[part * BLK:(part + 1) * BLK, 2 + b, :], hidT[:, k, :],
                                          wgt[b][2][:, k * D + part * FF:k * D + (part + 1) * FF], k == 0, k == KF - 1)
                        last.then_inc(sig["d_mm"], 1)
                pe.wait_ge(sig["xeT_ready"], happened("xeT_ready", (NE + 1) * (L + 1)))
                pe.wait_ge(sig["idx_ready"], happened("idx_ready", FETCHES * (L + 1)))
                pe.wait_ge(sig["y0_ready"], happened("y0_ready", NE * (L + 1)))
                pe.wait_ge(sig["y1_ready"], happened("y1_ready", NE * (L + 1)))
                n = pe.value_load(lst[0:1, 2 * NE - 1:2 * NE], min_val=0, max_val=LIST)
                with pe.If(n > 0):
                    with pe.Fori(0, n) as i:
                        e = pe.value_load(lst[0:1, bass.ds(i, 1)], min_val=0, max_val=NE - 1)
                        pe.wait_ge(sig["more_marks"], i + 1)
                        turnstile(pe)
                        for T in range(TILES):
                            last = mm(ps[0:BLK, 4, 0:2], onehot[0][:, T, :],
                                      code[:, :, T, bass.ds(e, 1)].rearrange("p c a -> p (c a)"), T == 0, T == TILES - 1)
                        last.then_inc(sig["more_idx_mm"], 1)
                        pe.wait_ge(sig[f"more_gather{L}"], (i + 1) * DMA)
                        turnstile(pe)
                        for k in range(KD):
                            last = flip(ps[:, 5, k * BLK:(k + 1) * BLK], xe[0][0:BLK, k:D:KD])
                        last.then_inc(sig["more_xt_mm"], 1)
                        pe.wait_ge(sig["more_xeT"], i + 1)
                        turnstile(pe)
                        pe.wait_ge(sig["more_weights"], (i + 1) * 3 * DMA)
                        turnstile(pe)
                        for k in range(KD):
                            for part in range(2):
                                last = mm(ps[part * BLK:(part + 1) * BLK, 0, :], xeT[0][:, k, :],
                                          wgt[0][part][:, k * FF:(k + 1) * FF], k == 0, k == KD - 1)
                        last.then_inc(sig["more_gu_mm"], 1)
                        pe.wait_ge(sig["more_hid"], i + 1)
                        turnstile(pe)
                        for k in range(KF):
                            last = flip(ps[:, 6, k * BLK:(k + 1) * BLK], hid[0:BLK, k:FF:KF])
                        last.then_inc(sig["more_ht_mm"], 1)
                        pe.wait_ge(sig["more_hidT"], i + 1)
                        turnstile(pe)
                        for k in range(KF):
                            for part in range(2):
                                last = mm(ps[part * BLK:(part + 1) * BLK, 2, :], hidT[:, k, :],
                                          wgt[0][2][:, k * D + part * FF:k * D + (part + 1) * FF], k == 0, k == KF - 1)
                        last.then_inc(sig["more_d_mm"], 1)

            experts(0)

            pe.wait_ge(sig["wqkv_in"], landed("wqkv_in", NE // 2 + 1))

            def window(T):
                n = rows_of(T)
                rows_T(2, T, h_w)
                pe.wait_ge(sig["hTa"], happened("hTa", TILES * 2 + T + 1))
                pe.wait_ge(sig["hTb"], happened("hTb", TILES * 2 + T + 1))
                if n == NS:
                    for k in range(KD):
                        for c in range(3):
                            last = mm(ps[c * NS:(c + 1) * NS, 2 + c, :], hT_w[:, k, 0:n], wqkv[:, k, c * FF:(c + 1) * FF],
                                      k == 0, k == KD - 1)
                    last.then_inc(sig["qkv_mm"], 3)
                    return
                for c in range(3):
                    for k in range(KD):
                        last = mm(ps[0:n, 2 + c, :], hT_w[:, k, 0:n], wqkv[:, k, c * FF:(c + 1) * FF], k == 0, k == KD - 1)
                    last.then_inc(sig["qkv_mm"], 1)

            def queries_T(T):
                n = rows_of(T)
                pe.wait_ge(sig["qkr_ready"], happened("qkr_ready", T + 1))
                for k in range(2):
                    flip(ps[:, 7, k * P:k * P + n], qkr[0:n, SH * SD + k * P:SH * SD + (k + 1) * P])
                for u in range(SUNITS):
                    last = flip(ps[:, 5 + u // 4, u % 4 * P:u % 4 * P + n], qkr[0:n, u * P:(u + 1) * P])
                last.then_inc(sig["qT_mm"], 1)
                if n == P:
                    pe.wait_ge(sig["qTa_w"], happened("qTa_w", T + 1))
                pe.wait_ge(sig["qTb_w"], happened("qTb_w", T + 1))

            def attend(T):
                pe.wait_ge(sig["v_w"], happened("v_w", T + 1))

                def scores(u):
                    if u >= 2:
                        pe.wait_ge(sig["s_w_ready"], happened("s_w_ready", SUNITS * T + u - 1))
                    if u == 1:
                        pe.wait_ge(sig["wo_added"], happened("wo_added", TILES + T))
                    for c in range(2):
                        last = mm(ps[:, 2 - 2 * (u % 2) + c, 0:2 * P], qT_w[c * SD:(c + 1) * SD, u, :],
                                  kT_w[c * SD:(c + 1) * SD, u // 2, :], True, True)
                    last.then_inc(sig["s_w_mm"], 1)

                def values(u):
                    pe.wait_ge(sig["pT_w_ready"], happened("pT_w_ready", SUNITS * T + u + 1))
                    for c in range(2):
                        at = (u % 4 * 2 + c) * SD
                        for past in range(2):
                            last = mm(ps[:, 6 + u // 4, at:at + SD], pT_w[u % 2][:, 2 * c + past, :],
                                      vb[:, cols((T + past) * SKV * SD + u // 2 * SD, SD)], past == 0, past == 1)
                    last.then_inc(sig["o_w_mm"], 1)

                scores(0)
                for u in range(SUNITS):
                    if u + 1 < SUNITS:
                        scores(u + 1)
                    pe.wait_ge(sig["p_w"], happened("p_w", SUNITS * T + u + 1))
                    pe.wait_ge(sig["pT_w_ready"], happened("pT_w_ready", SUNITS * T + u - 1))
                    for n in range(4):
                        last = flip(ps[:, 4 + u % 2, n * P:(n + 1) * P], sw[u % 2][:, n // 2, (n % 2) * P:(n % 2 + 1) * P])
                    last.then_inc(sig["pT_w_mm"], 1)
                    if u:
                        values(u - 1)
                values(SUNITS - 1)
                pe.wait_ge(sig["o_w_ready"], happened("o_w_ready", T + 1))
                for k in range(KD):
                    last = flip(ps[:, k // 4, (k % 4) * P:(k % 4 + 1) * P], o_w[:, k * P:(k + 1) * P])
                last.then_inc(sig["oT_w_mm"], 1)
                pe.wait_ge(sig["oTa_w"], happened("oTa_w", T + 1))
                pe.wait_ge(sig["oTb_w"], happened("oTb_w", T + 1))

            def project_out(T):
                n = rows_of(T)
                pe.wait_ge(sig["wo_w_in"], landed("wo_w_in", 1))
                for c, k in ([(c, k) for k in range(KD) for c in range(2)] if n == NS else
                             [(c, k) for c in range(2) for k in range(KD)]):
                    at = c * NS if n == NS else 0
                    last = mm(ps[at:at + n, c, :], oT_w[:, k, 0:n], wo_w[:, k, c * FF:(c + 1) * FF], k == 0, k == KD - 1)
                last.then_inc(sig["wo_mm"], 1)

            def tile(T):
                queries_T(T)
                attend(T)
                window(T + 1)
                project_out(T)

            window(0)
            with pe.Fori(0, PT - 1) as T:
                tile(T)
            tile(PT - 1)
            queries_T(PT)
            pe.wait_ge(sig["wo_added"], happened("wo_added", TILES + PT))
            pe.wait_ge(sig["v_w"], happened("v_w", TILES))
            pe.wait_ge(sig["cacheb_in"], landed("cacheb_in", 3 + SKV))
            for n in range(4):
                for i in range(4):
                    last = flip(ps[:, n, i * P:(i + 1) * P], kbuf[:, 2 * n + i // 2, (i % 2) * P:(i % 2 + 1) * P])
                last.then_inc(sig["kb_mm"], 1)
            pe.wait_ge(sig["kb_act"], happened("kb_act", 2))
            pe.wait_ge(sig["kb_dve"], happened("kb_dve", 2))
            for b in range(NB):
                at = (b % 3) * (P + NS)
                for g in range(SKV):
                    G, c = divmod(g, 2)
                    rows = slice(c * SD, (c + 1) * SD)
                    mm(ps[g * NS:(g + 1) * NS, 4 + b // 3, at:at + P], qS[rows, G, b, :], kbT[rows, b, G, :], True, True)
                    last = mm(ps[g * NS:(g + 1) * NS, 4 + b // 3, at + P:at + P + NS], qS[rows, G, b, :],
                              kT_w[rows, g, P:P + NS], True, True)
            last.then_inc(sig["sample_s_mm"], 1)
            pe.wait_ge(sig["sample_p"], happened("sample_p", 1))
            for b in range(NB):
                flip(ps[:, 4 + b // 4, (b % 4) * P:(b % 4 + 1) * P], s_z[:, b, 0:P])
                last = flip(ps[0:NS, 6 + b // 4, (b % 4) * P:(b % 4 + 1) * P], s_z[:, b, P:])
            last.then_inc(sig["sample_pT_mm"], 1)
            pe.wait_ge(sig["sample_pT_act"], happened("sample_pT_act", 2))
            pe.wait_ge(sig["sample_pT_dve"], happened("sample_pT_dve", 1))
            for g in range(SKV):
                for b in range(NB):
                    at = (g * NB + b) * SG * NT
                    rows = slice(g * NS, g * NS + SG * NT)
                    mm(ps[0:SD, 0, at:at + SG * NT], vbuf[:, b, g * SD:(g + 1) * SD], pT_z[:, b, rows], True, False)
                    last = mm(ps[0:SD, 0, at:at + SG * NT], vb[0:NS, TILES * SKV * SD + g * SD:TILES * SKV * SD + (g + 1) * SD],
                              pTn_z[0:NS, b, rows], False, True)
            last.then_inc(sig["sample_o_mm"], 1)
            pe.wait_ge(sig["sample_o"], happened("sample_o", 1))
            project_out(PT)
            experts(1)


_INS = ["x_prompt", "x_sample", "cache_mla", "cache_swa_kv", "page_table", "norm_mix", "norm_ffn", "norm_final",
        "mla_w_a", "mla_q_norm", "mla_wq_b", "mla_kv_norm", "mla_wkv_b", "mla_wo", "swa_wqkv", "swa_bqkv",
        "swa_sinks", "swa_wo", "swa_bo", "moe_w_group", "moe_b_group", "moe_w_expert", "moe_b_expert",
        "moe_w_gate", "moe_w_up", "moe_w_down"]
_OUTS = [("y_prompt", (1, SEQ, D)), ("y_sample", (NB, NT, D)), ("mla_rows_prompt", (1, 1, SEQ, ROW)),
         ("mla_rows_sample", (1, NB, NT, ROW)), ("swa_kv_prompt", (1, 1, WIN, 2, SKV, SD)),
         ("swa_kv_sample", (1, NB, WIN, 2, SKV, SD))]


def shape_constants(np):
    f = np.float32
    r = np.arange(P)
    tok = np.arange(TILES)[None, :] * P + r[:, None]
    pos = np.where(tok < SEQ, tok, 4096 + (tok - SEQ) % NT)
    inv = (10000.0 ** (-np.arange(DR // 2) / (DR // 2))).astype(f)
    ang = pos[:, :, None].astype(f) * inv[None, None, :]
    cos, sin = np.cos(ang).astype(f), np.sin(ang).astype(f)
    col = lambda v: np.broadcast_to(np.asarray(v, f), (P, len(v)))
    packed = np.concatenate([
        np.eye(P, dtype=f), (r[:, None] < r[None, :]).astype(f), np.ones((P, P), f), col(np.arange(BLK)),
        col(np.arange(NE)), col(np.arange(NE) - 1024), col(BLK * np.arange(1, MORE + 1)), r[:, None].astype(f),
        (tok - FAR).astype(f), (2 * tok - FAR).astype(f), (tok < TOK).astype(f)], axis=1)
    at = np.arange(TOK)
    cosT = cos.transpose(2, 1, 0).reshape(DR // 2, -1)[:, at]
    sinT = sin.transpose(2, 1, 0).reshape(DR // 2, -1)[:, at]
    swap = np.zeros((P, P), f)
    for h0 in (0, DR):
        for i in range(DR // 2):
            swap[h0 + DR // 2 + i, h0 + i] = -1.0
            swap[h0 + i, h0 + DR // 2 + i] = 1.0
    allowed = lambda ok: np.where(ok, f(0.0), f(NEG)).astype(f)
    q, k = r[:, None], np.arange(2 * P)[None, :]
    dist = P + q - k
    masks = np.concatenate([allowed((dist >= 0) & (dist < WIN) & (T * P - P + k >= 0)) for T in range(PT)], axis=1)
    row_t = (np.arange(P) % NT)[:, None, None]
    b, key = np.arange(NB)[None, :, None], np.arange(NS)[None, None, :]
    new = allowed((key // NT == b) & (key % NT <= row_t))
    past = allowed(np.arange(P)[None, :] > (np.arange(P) % NT)[:, None])
    return {
        "c_consts": packed, "c_cos_tok": cos.reshape(P, -1), "c_sin_tok": sin.reshape(P, -1),
        "c_causal": allowed(r[None, :] <= r[:, None]), "c_swap": swap,
        "c_cosT": np.tile(cosT, (P // (DR // 2), 1)), "c_sinT": np.tile(sinT, (P // (DR // 2), 1)),
        "c_smask": new, "c_sel32": (r[:, None] % NS == np.arange(NS)[None, :]).astype(f),
        "c_masks": masks, "c_mask_z": np.concatenate([past, new.reshape(P, -1)], axis=1),
    }


def kernel(**inputs):
    import numpy as np
    import concourse.bacc as bacc
    from concourse.bass_utils import run_bass_kernel_spmd

    nc = bacc.Bacc("TRN2", target_bir_lowering=False, num_devices=1)
    arrays = {name: np.ascontiguousarray(inputs[name]) for name in _INS}
    arrays |= {name: np.ascontiguousarray(v) for name, v in shape_constants(np).items()}
    a = {name: nc.dram_tensor(f"in_{name}", v.shape, mybir.dt.from_np(v.dtype), kind="ExternalInput").ap()
         for name, v in arrays.items()}
    o = {name: nc.dram_tensor(f"out_{name}", shape, F32, kind="ExternalOutput").ap() for name, shape in _OUTS}
    build(nc, a, o)
    r = run_bass_kernel_spmd(nc, [{f"in_{name}": v for name, v in arrays.items()}], core_ids=[0])
    return tuple(r.results[0][f"out_{name}"] for name, _ in _OUTS)
```
